# Optimizing a Trainium2 kernel written in Bass

```python
import math
import jax, jax.numpy as jnp
from jax import lax
import numpy as np
import jax
import jax.numpy as jnp

D_MODEL = 1024
BATCH = 1
SEQ = 256
DEPTH = 2

CHUNK = 64
N_MIXERS = 3
ALPHA = (2.0 * DEPTH) ** 0.25
BETA = (8.0 * DEPTH) ** -0.25
LN_EPS = 1e-5
RMS_EPS = 1e-6
SC_WIDTH = 3
MLA_HEADS = 8
QK_NOPE = 128
QK_ROPE = 64
V_HEAD = 128
Q_LORA = 3 * D_MODEL // 8
KV_LORA = D_MODEL // 4
ROPE_THETA = 10000.0
Q_BLOCK = 128
CONF_WIDTH = 31
D_FF = 4 * D_MODEL
N_A = len(range(0, DEPTH, N_MIXERS))
N_B = len(range(1, DEPTH, N_MIXERS))
N_C = len(range(2, DEPTH, N_MIXERS))


def _layer_norm(x, g, b):
    xf = x.astype(jnp.float32)
    mu = jnp.mean(xf, axis=-1, keepdims=True)
    var = jnp.mean(jnp.square(xf - mu), axis=-1, keepdims=True)
    y = (xf - mu) * lax.rsqrt(var + LN_EPS) * g.astype(jnp.float32) + b.astype(jnp.float32)
    return y.astype(x.dtype)

def _rms_norm(x, g):
    xf = x.astype(jnp.float32)
    y = xf * lax.rsqrt(jnp.mean(jnp.square(xf), axis=-1, keepdims=True) + RMS_EPS) * g.astype(jnp.float32)
    return y.astype(x.dtype)

def _causal_dwconv(x, w):
    k_width, c = w.shape
    return lax.conv_general_dilated(
        x, w[:, None, :].astype(x.dtype), window_strides=(1,), padding=[(k_width - 1, 0)],
        dimension_numbers=("NWC", "WIO", "NWC"), feature_group_count=c)

def _rope(x, cos, sin):
    x1, x2 = jnp.split(x, 2, axis=-1)
    c = cos[None, :, None, :].astype(x.dtype)
    s = sin[None, :, None, :].astype(x.dtype)
    return jnp.concatenate([x1 * c - x2 * s, x1 * s + x2 * c], axis=-1)

def _short_conv_mixer(x, w_in, conv_w, w_out):
    b_gate, c_gate, h = jnp.split(x @ w_in, 3, axis=-1)
    return (b_gate * _causal_dwconv(c_gate * h, conv_w)) @ w_out

def _mla_mixer(x, w_dq, g_q, w_uq, w_dkv, g_kv, w_uk, w_uv, w_o):
    bsz, seq, _ = x.shape
    pos = jnp.arange(seq, dtype=jnp.float32)
    inv_freq = ROPE_THETA ** (-jnp.arange(0, QK_ROPE, 2, dtype=jnp.float32) / QK_ROPE)
    ang = pos[:, None] * inv_freq[None, :]
    cos, sin = jnp.cos(ang), jnp.sin(ang)
    cq = _rms_norm(x @ w_dq, g_q)
    q = (cq @ w_uq).reshape(bsz, seq, MLA_HEADS, QK_NOPE + QK_ROPE)
    q_nope, q_pe = q[..., :QK_NOPE], _rope(q[..., QK_NOPE:], cos, sin)
    ckv_full = x @ w_dkv
    ckv = _rms_norm(ckv_full[..., :KV_LORA], g_kv)
    k_pe = _rope(ckv_full[..., None, KV_LORA:], cos, sin)[:, :, 0, :]
    k_nope = jnp.einsum("bsc,chd->bshd", ckv, w_uk)
    v = jnp.einsum("bsc,chd->bshd", ckv, w_uv)
    scale = (QK_NOPE + QK_ROPE) ** -0.5
    n_blk = seq // Q_BLOCK
    qn_b = q_nope.reshape(bsz, n_blk, Q_BLOCK, MLA_HEADS, QK_NOPE).transpose(1, 0, 2, 3, 4)
    qp_b = q_pe.reshape(bsz, n_blk, Q_BLOCK, MLA_HEADS, QK_ROPE).transpose(1, 0, 2, 3, 4)
    k_chunk = jnp.arange(seq) // CHUNK

    def block(args):
        qn, qp, blk = args
        s = (jnp.einsum("bqhd,bkhd->bhqk", qn, k_nope)
             + jnp.einsum("bqhd,bkd->bhqk", qp, k_pe)).astype(jnp.float32) * scale
        q_chunk = (blk * Q_BLOCK + jnp.arange(Q_BLOCK)) // CHUNK
        allowed = k_chunk[None, :] <= q_chunk[:, None]
        p = jax.nn.softmax(jnp.where(allowed[None, None], s, -jnp.inf), axis=-1).astype(v.dtype)
        return jnp.einsum("bhqk,bkhd->bqhd", p, v)

    o = lax.map(block, (qn_b, qp_b, jnp.arange(n_blk)))
    o = o.transpose(1, 0, 2, 3, 4).reshape(bsz, seq, MLA_HEADS * V_HEAD)
    return o @ w_o

def _conformer_conv_mixer(x, w_pw1, b_pw1, dw_w, dw_b, norm_g, norm_b, w_pw2, b_pw2):
    a, gate = jnp.split(x @ w_pw1 + b_pw1, 2, axis=-1)
    h = a * jax.nn.sigmoid(gate)
    h = _causal_dwconv(h, dw_w) + dw_b
    h = jax.nn.silu(_layer_norm(h, norm_g, norm_b))
    return h @ w_pw2 + b_pw2

def _sq_relu_mlp(x, w1, w2):
    return jnp.square(jax.nn.relu(x @ w1)) @ w2

def _normal(k, shape, fan_in, scale=1.0):
    return jax.random.normal(k, shape, jnp.float32) * (scale * fan_in ** -0.5)

def first_inputs(seed: int = 0) -> dict:
    key = jax.random.key(seed)
    ks = iter(jax.random.split(key, 40))
    D = D_MODEL
    gain = lambda shape: 1.0 + 0.02 * jax.random.normal(next(ks), shape, jnp.float32)
    bias = lambda shape: 0.02 * jax.random.normal(next(ks), shape, jnp.float32)
    return {
        "x": jax.random.normal(next(ks), (BATCH, SEQ, D), jnp.float32),
        "sc_w_in": _normal(next(ks), (N_A, D, 3 * D), D),
        "sc_conv_w": _normal(next(ks), (N_A, SC_WIDTH, D), SC_WIDTH),
        "sc_w_out": _normal(next(ks), (N_A, D, D), D, BETA),
        "mla_w_dq": _normal(next(ks), (N_B, D, Q_LORA), D),
        "mla_g_q": gain((N_B, Q_LORA)),
        "mla_w_uq": _normal(next(ks), (N_B, Q_LORA, MLA_HEADS * (QK_NOPE + QK_ROPE)), Q_LORA),
        "mla_w_dkv": _normal(next(ks), (N_B, D, KV_LORA + QK_ROPE), D),
        "mla_g_kv": gain((N_B, KV_LORA)),
        "mla_w_uk": _normal(next(ks), (N_B, KV_LORA, MLA_HEADS, QK_NOPE), KV_LORA),
        "mla_w_uv": _normal(next(ks), (N_B, KV_LORA, MLA_HEADS, V_HEAD), KV_LORA, BETA),
        "mla_w_o": _normal(next(ks), (N_B, MLA_HEADS * V_HEAD, D), MLA_HEADS * V_HEAD, BETA),
        "cf_w_pw1": _normal(next(ks), (N_C, D, 2 * D), D),
        "cf_b_pw1": bias((N_C, 2 * D)),
        "cf_dw_w": _normal(next(ks), (N_C, CONF_WIDTH, D), CONF_WIDTH),
        "cf_dw_b": bias((N_C, D)),
        "cf_norm_g": gain((N_C, D)),
        "cf_norm_b": bias((N_C, D)),
        "cf_w_pw2": _normal(next(ks), (N_C, D, D), D, BETA),
        "cf_b_pw2": bias((N_C, D)),
        "ff_w1": _normal(next(ks), (DEPTH, D, D_FF), D, BETA),
        "ff_w2": _normal(next(ks), (DEPTH, D_FF, D), D_FF, BETA),
        "ln_mix_g": gain((DEPTH, D)),
        "ln_mix_b": bias((DEPTH, D)),
        "ln_ff_g": gain((DEPTH, D)),
        "ln_ff_b": bias((DEPTH, D)),
    }

def first_block(x, sc_w_in, sc_conv_w, sc_w_out,
              mla_w_dq, mla_g_q, mla_w_uq, mla_w_dkv, mla_g_kv, mla_w_uk, mla_w_uv, mla_w_o,
              cf_w_pw1, cf_b_pw1, cf_dw_w, cf_dw_b, cf_norm_g, cf_norm_b, cf_w_pw2, cf_b_pw2,
              ff_w1, ff_w2, ln_mix_g, ln_mix_b, ln_ff_g, ln_ff_b):
    for i in range(DEPTH):
        m, j = i % N_MIXERS, i // N_MIXERS
        if m == 0:
            y = _short_conv_mixer(x, sc_w_in[j], sc_conv_w[j], sc_w_out[j])
        elif m == 1:
            y = _mla_mixer(x, mla_w_dq[j], mla_g_q[j], mla_w_uq[j], mla_w_dkv[j], mla_g_kv[j],
                           mla_w_uk[j], mla_w_uv[j], mla_w_o[j])
        else:
            y = _conformer_conv_mixer(x, cf_w_pw1[j], cf_b_pw1[j], cf_dw_w[j], cf_dw_b[j],
                                      cf_norm_g[j], cf_norm_b[j], cf_w_pw2[j], cf_b_pw2[j])
        x = _layer_norm(ALPHA * x + y, ln_mix_g[i], ln_mix_b[i])
        x = _layer_norm(ALPHA * x + _sq_relu_mlp(x, ff_w1[i], ff_w2[i]), ln_ff_g[i], ln_ff_b[i])
    return x


N_A_LAYERS = DEPTH // 2
N_B_LAYERS = DEPTH - N_A_LAYERS
EPS = 1e-6
D_RNN = D_MODEL
RG_HEADS = 4
RG_BLOCK = D_RNN // RG_HEADS
CONV_W = 4
RG_C = 8.0
HEAD_DIM = 128
N_HEADS = D_MODEL // HEAD_DIM
D_ATT = N_HEADS * HEAD_DIM
MOBA_BLOCK = 256
MOBA_TOPK = 3
Q_CHUNK = 16
NEG_INF = -1e30


def _rmsnorm(x, g):
    xf = x.astype(jnp.float32)
    y = xf * lax.rsqrt(jnp.mean(xf * xf, axis=-1, keepdims=True) + EPS)
    return (y * g.astype(jnp.float32)).astype(x.dtype)

def _modulate(h, shift, scale):
    return h * (1.0 + scale[:, None, :]) + shift[:, None, :]

def _lin_combine(left, right):
    a_l, b_l = left
    a_r, b_r = right
    return a_l * a_r, a_r * b_l + b_r

def _block_diag(u, w):
    b, s, _ = u.shape
    ub = u.reshape(b, s, RG_HEADS, RG_BLOCK)
    return jnp.einsum('bshi,hij->bshj', ub, w).reshape(b, s, D_RNN)

def _rglru_mixer(h, w_in, conv_w, conv_b, w_a, b_a, w_x, b_x, lam, w_out):
    u, g = jnp.split(h @ w_in, 2, axis=-1)
    u = lax.conv_general_dilated(
        u, conv_w[:, None, :], window_strides=(1,), padding=[(CONV_W - 1, 0)],
        dimension_numbers=('NWC', 'WIO', 'NWC'), feature_group_count=D_RNN) + conv_b
    r = jax.nn.sigmoid((_block_diag(u, w_a) + b_a).astype(jnp.float32))
    gi = jax.nn.sigmoid((_block_diag(u, w_x) + b_x).astype(jnp.float32))
    log_a = -RG_C * r * jax.nn.softplus(-lam.astype(jnp.float32))
    a = jnp.exp(log_a)
    b_in = jnp.sqrt(-jnp.expm1(2.0 * log_a)) * (gi * u.astype(jnp.float32))
    _, hs = lax.associative_scan(_lin_combine, (a, b_in), axis=1)
    y = hs.astype(h.dtype) * jax.nn.silu(g)
    return y @ w_out

def _shared_kv(x, cs, kv_norm_g, kv_mod_w, kv_mod_b, w_kv):
    b, s, _ = x.shape
    shift, scale = jnp.split(cs @ kv_mod_w + kv_mod_b, 2, axis=-1)
    h = _modulate(_rmsnorm(x, kv_norm_g), shift, scale)
    k, v = jnp.split(h @ w_kv, 2, axis=-1)
    k = k.reshape(b, s, N_HEADS, HEAD_DIM).transpose(0, 2, 1, 3)
    v = v.reshape(b, s, N_HEADS, HEAD_DIM).transpose(0, 2, 1, 3)
    s_pad = -(-s // MOBA_BLOCK) * MOBA_BLOCK
    pad = ((0, 0), (0, 0), (0, s_pad - s), (0, 0))
    k = jnp.pad(k, pad)
    v = jnp.pad(v, pad)
    n_blk = s_pad // MOBA_BLOCK
    k_mean = k.astype(jnp.float32).reshape(b, N_HEADS, n_blk, MOBA_BLOCK, HEAD_DIM).mean(axis=3)
    return k, v, k_mean.astype(k.dtype)

def _moba_attention(q, k, v, k_mean):
    b, nh, s, dh = q.shape
    n = b * nh
    s_pad = k.shape[2]
    n_blk = s_pad // MOBA_BLOCK
    k_sel = min(MOBA_TOPK, n_blk)
    qf = q.reshape(n, s, dh)
    kf = k.reshape(n, s_pad, dh)
    vf = v.reshape(n, s_pad, dh)
    kb = k.reshape(n * n_blk, MOBA_BLOCK, dh)
    vb = v.reshape(n * n_blk, MOBA_BLOCK, dh)
    km = k_mean.reshape(n, n_blk, dh)
    base = (jnp.arange(n, dtype=jnp.int32) * n_blk)[:, None, None]
    blk_ids = jnp.arange(n_blk, dtype=jnp.int32)
    sm_scale = dh ** -0.5

    def one_chunk(ci):
        q0 = ci * Q_CHUNK
        blk = q0 // MOBA_BLOCK
        qc = lax.dynamic_slice_in_dim(qf, q0, Q_CHUNK, axis=1)
        gate = jnp.einsum('nqd,nbd->nqb', qc, km).astype(jnp.float32)
        gate = jnp.where(blk_ids < blk, gate, NEG_INF)
        _, idx = lax.top_k(gate, k_sel)
        valid = idx < blk
        kg = kb[base + idx]
        vg = vb[base + idx]
        s_sel = jnp.einsum('nqd,nqkld->nqkl', qc, kg).astype(jnp.float32) * sm_scale
        s_sel = jnp.where(valid[..., None], s_sel, NEG_INF).reshape(n, Q_CHUNK, k_sel * MOBA_BLOCK)
        k_own = lax.dynamic_slice_in_dim(kf, blk * MOBA_BLOCK, MOBA_BLOCK, axis=1)
        v_own = lax.dynamic_slice_in_dim(vf, blk * MOBA_BLOCK, MOBA_BLOCK, axis=1)
        s_own = jnp.einsum('nqd,nld->nql', qc, k_own).astype(jnp.float32) * sm_scale
        q_pos = q0 + jnp.arange(Q_CHUNK, dtype=jnp.int32)
        k_pos = blk * MOBA_BLOCK + jnp.arange(MOBA_BLOCK, dtype=jnp.int32)
        s_own = jnp.where(k_pos[None, None, :] <= q_pos[None, :, None], s_own, NEG_INF)
        p = jax.nn.softmax(jnp.concatenate([s_sel, s_own], axis=-1), axis=-1).astype(v.dtype)
        p_sel = p[..., :k_sel * MOBA_BLOCK].reshape(n, Q_CHUNK, k_sel, MOBA_BLOCK)
        p_own = p[..., k_sel * MOBA_BLOCK:]
        return (jnp.einsum('nqkl,nqkld->nqd', p_sel, vg)
                + jnp.einsum('nql,nld->nqd', p_own, v_own))

    out = lax.map(one_chunk, jnp.arange(s // Q_CHUNK, dtype=jnp.int32))
    return out.transpose(1, 0, 2, 3).reshape(b, nh, s, dh)

def _moba_mixer(h, k, v, k_mean, w_in, w_out):
    b, s, _ = h.shape
    q, g = jnp.split(h @ w_in, 2, axis=-1)
    q = q.reshape(b, s, N_HEADS, HEAD_DIM).transpose(0, 2, 1, 3)
    o = _moba_attention(q, k, v, k_mean).transpose(0, 2, 1, 3).reshape(b, s, D_ATT)
    return (o * jax.nn.silu(g)) @ w_out

def second_inputs(seed: int = 0) -> dict:
    key = jax.random.key(seed)
    ks = jax.random.split(key, 24)
    f32 = jnp.float32

    def nrm(k, shape, scale):
        return scale * jax.random.normal(k, shape, f32)

    a0 = jax.random.uniform(ks[12], (N_A_LAYERS, D_RNN), f32, 0.9, 0.999)
    s0 = a0 ** (1.0 / RG_C)
    return {
        'x': nrm(ks[0], (BATCH, SEQ, D_MODEL), 1.0),
        'c': nrm(ks[1], (BATCH, D_MODEL), 1.0),
        'mod_w': nrm(ks[2], (DEPTH, D_MODEL, 3 * D_MODEL), 0.5 * D_MODEL ** -0.5),
        'mod_b': nrm(ks[3], (DEPTH, 3 * D_MODEL), 0.02),
        'norm_g': 1.0 + nrm(ks[4], (DEPTH, D_MODEL), 0.02),
        'rg_w_in': nrm(ks[5], (N_A_LAYERS, D_MODEL, 2 * D_RNN), D_MODEL ** -0.5),
        'rg_conv_w': nrm(ks[6], (N_A_LAYERS, CONV_W, D_RNN), CONV_W ** -0.5),
        'rg_conv_b': nrm(ks[7], (N_A_LAYERS, D_RNN), 0.01),
        'rg_w_a': nrm(ks[8], (N_A_LAYERS, RG_HEADS, RG_BLOCK, RG_BLOCK), RG_BLOCK ** -0.5),
        'rg_b_a': nrm(ks[9], (N_A_LAYERS, D_RNN), 0.01),
        'rg_w_x': nrm(ks[10], (N_A_LAYERS, RG_HEADS, RG_BLOCK, RG_BLOCK), RG_BLOCK ** -0.5),
        'rg_b_x': nrm(ks[11], (N_A_LAYERS, D_RNN), 0.01),
        'rg_lambda': jnp.log(s0) - jnp.log1p(-s0),
        'rg_w_out': nrm(ks[13], (N_A_LAYERS, D_RNN, D_MODEL), D_RNN ** -0.5),
        'kv_norm_g': 1.0 + nrm(ks[14], (D_MODEL,), 0.02),
        'kv_mod_w': nrm(ks[15], (D_MODEL, 2 * D_MODEL), 0.5 * D_MODEL ** -0.5),
        'kv_mod_b': nrm(ks[16], (2 * D_MODEL,), 0.02),
        'w_kv': nrm(ks[17], (D_MODEL, 2 * D_ATT), D_MODEL ** -0.5),
        'att_w_in': nrm(ks[18], (N_B_LAYERS, D_MODEL, 2 * D_ATT), D_MODEL ** -0.5),
        'att_w_out': nrm(ks[19], (N_B_LAYERS, D_ATT, D_MODEL), D_ATT ** -0.5),
        'final_norm_g': 1.0 + nrm(ks[20], (D_MODEL,), 0.02),
    }

def second_block(x, c, mod_w, mod_b, norm_g, rg_w_in, rg_conv_w, rg_conv_b, rg_w_a, rg_b_a,
              rg_w_x, rg_b_x, rg_lambda, rg_w_out, kv_norm_g, kv_mod_w, kv_mod_b, w_kv,
              att_w_in, att_w_out, final_norm_g):
    cs = jax.nn.silu(c)
    k_sh = v_sh = km_sh = None
    for layer in range(DEPTH):
        shift, scale, gate = jnp.split(cs @ mod_w[layer] + mod_b[layer], 3, axis=-1)
        h = _modulate(_rmsnorm(x, norm_g[layer]), shift, scale)
        if layer < N_A_LAYERS:
            i = layer
            y = _rglru_mixer(h, rg_w_in[i], rg_conv_w[i], rg_conv_b[i], rg_w_a[i], rg_b_a[i],
                             rg_w_x[i], rg_b_x[i], rg_lambda[i], rg_w_out[i])
        else:
            if layer == N_A_LAYERS:
                k_sh, v_sh, km_sh = _shared_kv(x, cs, kv_norm_g, kv_mod_w, kv_mod_b, w_kv)
            i = layer - N_A_LAYERS
            y = _moba_mixer(h, k_sh, v_sh, km_sh, att_w_in[i], att_w_out[i])
        x = x + gate[:, None, :] * y
    return _rmsnorm(x, final_norm_g)


def setup_inputs(seed=0):
    out = dict(first_inputs(seed))
    for name, value in second_inputs(seed + 1).items():
        if name != "x":
            out[name + "_2"] = value
    return out


def reference(
    x, sc_w_in, sc_conv_w, sc_w_out, mla_w_dq, mla_g_q, mla_w_uq, mla_w_dkv, mla_g_kv, mla_w_uk,
    mla_w_uv, mla_w_o, cf_w_pw1, cf_b_pw1, cf_dw_w, cf_dw_b, cf_norm_g, cf_norm_b, cf_w_pw2,
    cf_b_pw2, ff_w1, ff_w2, ln_mix_g, ln_mix_b, ln_ff_g, ln_ff_b, c_2, mod_w_2, mod_b_2,
    norm_g_2, rg_w_in_2, rg_conv_w_2, rg_conv_b_2, rg_w_a_2, rg_b_a_2, rg_w_x_2, rg_b_x_2,
    rg_lambda_2, rg_w_out_2, kv_norm_g_2, kv_mod_w_2, kv_mod_b_2, w_kv_2, att_w_in_2,
    att_w_out_2, final_norm_g_2,
):
    x = first_block(
        x, sc_w_in, sc_conv_w, sc_w_out, mla_w_dq, mla_g_q, mla_w_uq, mla_w_dkv, mla_g_kv,
        mla_w_uk, mla_w_uv, mla_w_o, cf_w_pw1, cf_b_pw1, cf_dw_w, cf_dw_b, cf_norm_g, cf_norm_b,
        cf_w_pw2, cf_b_pw2, ff_w1, ff_w2, ln_mix_g, ln_mix_b, ln_ff_g, ln_ff_b,
    )
    return second_block(
        x, c_2, mod_w_2, mod_b_2, norm_g_2, rg_w_in_2, rg_conv_w_2, rg_conv_b_2, rg_w_a_2,
        rg_b_a_2, rg_w_x_2, rg_b_x_2, rg_lambda_2, rg_w_out_2, kv_norm_g_2, kv_mod_w_2,
        kv_mod_b_2, w_kv_2, att_w_in_2, att_w_out_2, final_norm_g_2,
    )


_drawn_inputs = setup_inputs


def setup_inputs(seed=0):
    import zlib

    import numpy as np

    out = dict(_drawn_inputs(seed))
    spreads = {}
    factors = {'mla_g_q': 8.0,
     'mla_g_kv': 8.0,
     'mla_w_uk': 2.856,
     'norm_g_2': 8.0,
     'rg_conv_b_2': 7.553,
     'rg_b_a_2': 8.0,
     'rg_b_x_2': 8.0,
     'kv_norm_g_2': 8.0,
     'kv_mod_b_2': 8.0,
     'final_norm_g_2': 2.82}
    for name, (base, spread) in spreads.items():
        noise = np.random.default_rng([zlib.crc32(name.encode()), seed]).standard_normal(out[name].shape)
        drawn = base * np.exp(spread * noise) if base else spread * noise
        out[name] = jnp.asarray(drawn.astype(out[name].dtype))
    for name, factor in factors.items():
        out[name] = (out[name] * factor).astype(out[name].dtype)
    return out
```

```python
from contextlib import ExitStack

import concourse.bass as bass
import numpy as np
from concourse import mybir

F32 = mybir.dt.float32
F32R = mybir.dt.float32r
ALU = mybir.AluOpType
ACT = mybir.ActivationFunctionType
AXX = mybir.AxisListType.X

P = 128
SEQ, D, D_FF = 256, 1024, 4096
TB = SEQ // P
KT = D // P
HEADS = 8
NOPE, ROPE = 128, 64
Q_LORA, KV_LORA = 384, 256
QT, CT = Q_LORA // P, KV_LORA // P
RG_C = 8.0
ALPHA = 4.0 ** 0.25
LN_EPS, RMS_EPS = 1e-5, 1e-6
NEG_INF = -1e30
GT = 2
FFG = D_FF // (GT * P)
MXG = D // (GT * P)
NMOD = 2 * FFG

PIECE = 2048
RAW = 3
RING = 6
AHEAD = 4
PBANKS = 3
HRING = 3


def piece_table():
    t = []

    def add(phase, kind, n, cols=PIECE):
        t.append(((phase, kind, n), cols))

    for g in range(MXG):
        for kind in "ChB":
            add("sc", kind, g)
        if g:
            add("sc", "down", g - 1)
    add("sc", "down", MXG - 1)

    def ff(phase):
        for g in range(FFG):
            add(phase, "up", g)
            if g:
                add(phase, "down", g - 1)
        add(phase, "down", FFG - 1)

    ff("ff0")
    add("mla", "dq", 0)
    add("mla", "dq", 1, KT * P)
    add("mla", "dkv", 0)
    add("mla", "kpe", 0)
    add("mla", "uk", 0)
    add("mla", "uv", 0)
    for n in range(2):
        add("mla", "qn", n, 4 * QT * P)
    for n in range(2):
        add("mla", "qp", n, 4 * QT * P)
    for g in range(MXG):
        add("mla", "down", g)
    ff("ff1")
    for g in range(MXG + 2):
        if g < MXG:
            add("rg", "u", g)
            add("rg", "g", g)
        if 0 <= g - 1 < MXG:
            add("rg", "ax", g - 1, 2 * GT * 2 * P)
        if g >= 2:
            add("rg", "down", g - 2)
    for kind in "qgkv":
        for g in range(MXG):
            add("mo", kind, g)
    for g in range(MXG):
        add("mo", "down", g)
    return t


PIECES = piece_table()
COLS = [c for _, c in PIECES]
PI = {key: n for n, (key, _) in enumerate(PIECES)}


def stream_table():
    t, m = [], 0
    for n, ((phase, kind, g), _) in enumerate(PIECES):
        t.append(("w", n))
        if kind == "up":
            t.append(("mod", m))
            m += 1
    return t


STREAM = stream_table()
AT = {item: n for n, item in enumerate(STREAM)}
WIDTH = [COLS[n] if kind == "w" else PIECE for kind, n in STREAM]


def unit_table():
    t = []

    def norm(name):
        t.extend((name, b, q) for b in range(TB) for q in range(2))

    def attention(phase):
        for h in range(HEADS + 1):
            if h < HEADS:
                t.extend((phase, "S", h, b) for b in range(TB))
            if h:
                t.extend([(phase, "PT", h - 1), (phase, "O", h - 1)])

    norm("init")
    for g in range(MXG):
        t.extend(("sc", kind, g) for kind in "ChB")
    norm("ln0")
    t.extend(("ff0", g) for g in range(FFG))
    norm("ln1")
    t.extend([("mla", "cq", 0), ("mla", "cq", 1), ("mla", "ckv"), ("mla", "kpe")])
    t.extend([("mla", "tq", 0), ("mla", "tq", 1), ("mla", "tkv")])
    t.extend(("mla", "k", n) for n in range(4))
    t.extend(("mla", "v", b, n) for b in range(TB) for n in range(2))
    t.extend(("mla", "qn", n) for n in range(4))
    t.extend(("mla", "qp", n) for n in range(4))
    attention("mla")
    norm("ln2")
    t.extend(("ff1", g) for g in range(FFG))
    norm("rs1")
    t.extend([("gate", 0, 0), ("gate", 0, 1)])
    for g in range(MXG + 1):
        if g < MXG:
            t.extend([("rg", "u", g), ("rg", "g", g)])
        if g:
            t.extend([("rg", "a", g - 1), ("rg", "x", g - 1)])
    norm("rs2")
    t.extend(("mo", "q", g) for g in range(MXG))
    t.extend(("mo", "g", g) for g in range(MXG))
    norm("rs2kv")
    t.extend(("mo", "k", g) for g in range(MXG))
    t.extend(("mo", "v", g) for g in range(MXG))
    attention("mo")
    t.extend([("gate", 1, 0), ("gate", 1, 1)])
    return t


UNITS = unit_table()
UN = {key: n for n, key in enumerate(UNITS)}

def down_table():
    t = []
    for phase, groups in (("sc", MXG), ("ff0", FFG), ("mla", MXG), ("ff1", FFG), ("rg", MXG), ("mo", MXG)):
        t.extend((phase, g, b) for g in range(groups - 2) for b in range(TB))
        t.extend((phase, g, b) for b in range(TB) for g in (groups - 2, groups - 1))
    return t


DN = {key: n for n, key in enumerate(down_table())}
GROUPS = {"sc": MXG, "ff0": FFG, "mla": MXG, "ff1": FFG, "rg": MXG, "mo": MXG}


def last_unit(phase, kind, n):
    if kind == "up":
        return (phase, n)
    return {"dq": ("mla", "cq", n), "dkv": ("mla", "ckv"), "kpe": ("mla", "kpe"), "uk": ("mla", "k", 3),
            "uv": ("mla", "v", 1, 1), "qn": ("mla", "qn", 2 * n + 1), "qp": ("mla", "qp", 2 * n + 1),
            "ax": ("rg", "x", n)}.get(kind, (phase, kind, n))


NORMS = ["ln0", "ln1", "cq", "ckv", "ln2", "ln3", "rs1", "rs2", "rs3"]
HIDDEN = {"sc": MXG, "ff0": FFG, "ff1": FFG, "rg": MXG}
SIGNALS = {
    "relu": {"ff0": FFG, "ff1": FFG},
    "hidden_high": HIDDEN,
    "hidden_low": HIDDEN,
    "y_read": {p: TB for p in GROUPS},
    "var_ready": {p: TB for p in NORMS},
    "rstd_ready": {p: TB for p in NORMS},
    "norm_ready": {p: TB for p in NORMS if p[0] != "c"},
    "x_ready": {p: TB for p in ("ln0", "ln1", "ln2", "ln3")},
    "xT_high": {p: 4 for p in ("init", "ln0", "ln1", "ln2", "rs1", "rs2", "rs2kv")},
    "xT_low": {p: 4 for p in ("ln0", "ln1", "ln2", "rs1", "rs2", "rs2kv")},
    "row_bias": {"mla": TB * HEADS, "mo": TB * HEADS},
    "probs": {"mla": TB * HEADS, "mo": TB * HEADS},
    "o_high": {"mla": HEADS, "mo": HEADS},
    "o_low": {"mla": HEADS, "mo": HEADS},
}


def nth(signal, phase, i=0):
    count = 0
    for p, n in SIGNALS[signal].items():
        if p == phase:
            return count + i + 1
        count += n
    raise KeyError((signal, phase))


COL_WIDTHS = {"c": KT, "mod_b": 2 * NMOD, "norm_g0": KT, "norm_g1": KT, "kv_g": KT,
              "ln0_g": KT, "ln0_b": KT, "ln1_g": KT, "ln1_b": KT, "ln2_g": KT, "ln2_b": KT,
              "sc_w": 3 * KT, "rg_w": 4 * KT, "rg_cb": KT, "rg_ba": KT, "rg_bx": KT, "lam": KT,
              "g_q": QT, "g_kv": CT}
COL = {}
for _n, _w in COL_WIDTHS.items():
    COL[_n] = sum(COL_WIDTHS[k] for k in COL)
NCOL = sum(COL_WIDTHS.values())
MOD = {name: KT * n for n, name in enumerate(["shift0", "scale0", "gate0", "shift1", "scale1", "gate1",
                                              "kv_shift", "kv_scale"])}


def build(nc, weights, x_in, cols_in, consts_in, rows_in, out):
    with ExitStack() as ctx:
        def sb(name, shape, dt=F32):
            return ctx.enter_context(nc.sbuf_tensor(name, shape, dt))

        raw = sb("raw", [P, RAW, PIECE])
        w_high = sb("w_high", [P, RING, PIECE], F32R)
        w_low = sb("w_low", [P, RING, PIECE], F32R)
        x = sb("x", [P, TB, D])
        z = sb("z", [P, TB, D])
        xT_h = sb("xT_h", [P, KT, SEQ], F32R)
        xT_l = sb("xT_l", [P, KT, SEQ], F32R)
        stage = sb("stage", [P, 2, 512])
        rows = sb("rows", [P, 2, D])
        consts = sb("consts", [P, 2 * P + 2 * SEQ])
        ones = sb("ones", [P, P])
        cols = sb("cols", [P, NCOL])
        modcol = sb("modcol", [P, 2 * NMOD])
        macc = sb("macc", [P, 2, SEQ])
        buf_a = sb("buf_a", [P, 2, 512])
        buf_b = sb("buf_b", [P, 2, 512])
        hT_h = sb("hT_h", [P, HRING * GT, SEQ], F32R)
        hT_l = sb("hT_l", [P, HRING * GT, SEQ], F32R)
        kT = sb("kT", [P, KT, SEQ])
        area = sb("area", [P, KT, SEQ])
        small = sb("small", [P, 72])

        ident, tri = consts[:, 0:P], consts[:, P:2 * P]
        cosT, sinT = consts[:, 2 * P:2 * P + SEQ], consts[:, 2 * P + SEQ:]
        flat = lambda t: t[:, :, :].rearrange("p a b -> p (a b)")
        kT_f, area_f = flat(kT), flat(area)
        stats = small[:, 0:24].rearrange("p (b n) -> p b n", b=TB)
        mv = small[:, 24:28].rearrange("p (b n) -> p b n", b=TB)
        ve = small[:, 28:32]
        rstd = small[:, 32:36]
        minus_half = small[:, 36:37]
        nmx, ebias, rsum, rinv = (small[:, 40 + 4 * n:44 + 4 * n] for n in range(4))
        cs = sb("cs", [P, KT])
        cth = sb("cth", [P, KT])
        prm = sb("prm", [P, 12, KT])
        A0, A1, AK, HBA, HBX, C4 = (prm[:, n, :] for n in range(6))

        def col(name, n=0):
            return cols[:, COL[name] + n:COL[name] + n + 1]

        def colrange(name, n=KT, start=0):
            return cols[:, COL[name] + start:COL[name] + start + n]

        def mcol(name, n):
            return modcol[:, MOD[name] + n:MOD[name] + n + 1]

        def mrange(name):
            return modcol[:, MOD[name]:MOD[name] + KT]

        Y = [[ctx.enter_context(nc.psum_tensor(f"Y{b}{h}", [P, 512], F32)) for h in range(2)] for b in range(TB)]
        bank = [ctx.enter_context(nc.psum_tensor(f"bank{n}", [P, 512], F32)) for n in range(PBANKS)]
        mbank = ctx.enter_context(nc.psum_tensor("mbank", [P, 512], F32))

        def tok(b):
            return slice(b * P, (b + 1) * P)

        def sem(name):
            return ctx.enter_context(nc.semaphore(name))

        raw_in = [sem(f"raw_in{n}") for n in range(RAW)]
        w_high_ready = sem("w_high_ready")
        raw_done = sem("raw_done")
        product = sem("product")
        summed = sem("summed")
        evacuated = [sem(f"evacuated{n}") for n in range(PBANKS)]
        mod_summed, mod_read = sem("mod_summed"), sem("mod_read")
        S = {name: sem(name) for name in SIGNALS}
        relu, hidden_high, hidden_low = S["relu"], S["hidden_high"], S["hidden_low"]
        x_in_done, consts_in_done, cols_in_done = sem("x_in_done"), sem("consts_in_done"), sem("cols_in_done")
        gain_in, shift_in = sem("gain_in"), sem("shift_in")
        ones_ready, c_tanh, lam_exp_in, lam_exp = sem("ones_ready"), sem("c_tanh"), sem("lam_exp_in"), sem("lam_exp")
        prm_ready, diag_ready = sem("prm_ready"), sem("diag_ready")
        lora_ready, lora_high, lora_low, rope_ready = sem("lora_ready"), sem("lora_high"), sem("lora_low"), sem("rope_ready")
        conv_ready, uc_high, uc_low = sem("conv_ready"), sem("uc_high"), sem("uc_low")
        gate_tanh, decay_ready, ratio_ready, root_ready = sem("gate_tanh"), sem("decay_ready"), sem("ratio_ready"), sem("root_ready")
        rg_hidden = sem("rg_hidden")
        act_chain, dve_chain, pool_chain = sem("act_chain"), sem("dve_chain"), sem("pool_chain")
        out_ready, out_done = sem("out_ready"), sem("out_done")

        def bank_of(*key):
            return bank[UN[key] % PBANKS]

        def await_product(eng, *key):
            eng.wait_ge(product, UN[key] + 1)

        def await_evacuated(eng, *key):
            eng.wait_ge(evacuated[UN[key] % PBANKS], UN[key] // PBANKS + 1)

        def evacuates(*key):
            return evacuated[UN[key] % PBANKS]

        def await_piece_used(eng, n):
            phase, kind, i = PIECES[n][0]
            if kind == "down":
                eng.wait_ge(summed, DN[phase, i, TB - 1] + 1)
            else:
                eng.wait_ge(product, UN[last_unit(phase, kind, i)] + 1)

        def hslot(phase, g):
            return GT * (g % (2 if phase == "rg" else HRING))

        block = ctx.enter_context(nc.Block())

        @block.sync
        def _(sp):
            def load_row(slot, which, semaphore):
                sp.dma_start(rows[:, slot, :], rows_in[which, :].partition_broadcast(P)).then_inc(semaphore, 16)

            sp.dma_start(x[:, :, :], x_in.rearrange("(b p) d -> p b d", p=P)).then_inc(x_in_done, 16)
            sp.dma_start(consts[:, :], consts_in).then_inc(consts_in_done, 16)
            sp.dma_start(cols[:, :], cols_in).then_inc(cols_in_done, 16)
            start = 0
            for s, (kind, n) in enumerate(STREAM):
                if s >= RAW:
                    sp.wait_ge(raw_done, s - RAW + 1)
                src = weights[start:start + P * WIDTH[s]].rearrange("(p n) -> p n", p=P)
                sp.dma_start(raw[:, s % RAW, 0:WIDTH[s]], src).then_inc(raw_in[s % RAW], 16)
                start += P * WIDTH[s]
                key = PIECES[n][0] if kind == "w" else None
                which = {("sc", "down", 0): 0, ("ff0", "up", 8): 1, ("mla", "down", 2): 2, ("ff1", "up", 8): 3}.get(key)
                if which is not None:
                    if which in (1, 3):
                        sp.wait_ge(S["x_ready"], nth("x_ready", f"ln{which - 1}", TB - 1))
                    if which == 2:
                        await_product(sp, "mla", "S", HEADS - 1, TB - 1)
                    load_row(0, 2 * which, gain_in)
                    load_row(1, 2 * which + 1, shift_in)
            await_product(sp, "mo", "S", HEADS - 1, TB - 1)
            load_row(1, 8, shift_in)
            for b in range(TB):
                sp.wait_ge(out_ready, b + 1)
                sp.dma_start(out[b * P:(b + 1) * P, :], z[:, b, :]).then_inc(out_done, 16)
            sp.wait_ge(out_done, 16 * TB)

        @block.tensor
        def _(pe):
            mm = nc.tensor.matmul
            issued = [0, 0]

            def open_unit(*key):
                u = UN[key]
                assert u == issued[0], (key, UNITS[issued[0]])
                issued[0] += 1
                if u >= PBANKS:
                    pe.wait_ge(evacuated[u % PBANKS], u // PBANKS)
                return bank[u % PBANKS]

            def await_piece(n):
                pe.wait_ge(raw_done, AT["w", n] + 1)

            def up_tile(dst, n, tile, kts, xh, xl):
                for kt in range(kts):
                    c = (tile * kts + kt) * P
                    high, low = w_high[:, n % RING, c:c + P], w_low[:, n % RING, c:c + P]
                    mm(dst, high, xh[:, kt, :], start=kt == 0, stop=False)
                    mm(dst, high, xl[:, kt, :], start=False, stop=False)
                    last = mm(dst, low, xh[:, kt, :], start=False, stop=kt == kts - 1)
                return last

            def up(n, key, tile0=0, kts=KT, xh=xT_h, xl=xT_l):
                dst = open_unit(*key)
                await_piece(n)
                up_tile(dst[:, 0:SEQ], n, tile0, kts, xh, xl)
                up_tile(dst[:, SEQ:], n, tile0 + 1, kts, xh, xl).then_inc(product, 1)

            def across(n, key, kts, width, c0=0, stride=None, xh=xT_h, xl=xT_l, blocks=range(TB)):
                dst = open_unit(*key)
                await_piece(n)
                for i, b in enumerate(blocks):
                    out_b = dst[:, i * width:(i + 1) * width]
                    for kt in range(kts):
                        c = kt * (stride or width) + c0
                        high, low = w_high[:, n % RING, c:c + width], w_low[:, n % RING, c:c + width]
                        mm(out_b, xh[:, kt, tok(b)], high, start=kt == 0, stop=False)
                        mm(out_b, xh[:, kt, tok(b)], low, start=False, stop=False)
                        last = mm(out_b, xl[:, kt, tok(b)], high, start=False, stop=kt == kts - 1)
                last.then_inc(product, 1)

            def down(phase, g, b, th=hT_h, tl=hT_l):
                assert DN[phase, g, b] == issued[1]
                issued[1] += 1
                n = PI[phase, "down", g]
                if th is hT_h:
                    t0 = hslot(phase, g)
                    pe.wait_ge(hidden_low, nth("hidden_low", phase, g))
                else:
                    t0 = GT * g
                    pe.wait_ge(S["o_low"], nth("o_low", phase, GT * g + GT - 1))
                if g == 0:
                    phases = list(GROUPS)
                    if phase != phases[0]:
                        pe.wait_ge(S["y_read"], nth("y_read", phases[phases.index(phase) - 1], b))
                await_piece(n)
                for t in range(GT):
                    first, final = g == 0 and t == 0, g == GROUPS[phase] - 1 and t == GT - 1
                    high = [w_high[:, n % RING, t * D + h * 512:t * D + (h + 1) * 512] for h in range(2)]
                    low = [w_low[:, n % RING, t * D + h * 512:t * D + (h + 1) * 512] for h in range(2)]
                    for h in range(2):
                        mm(Y[b][h][:, :], th[:, t0 + t, tok(b)], high[h], start=first, stop=False)
                        mm(Y[b][h][:, :], th[:, t0 + t, tok(b)], low[h], start=False, stop=False)
                    for h in range(2):
                        last = mm(Y[b][h][:, :], tl[:, t0 + t, tok(b)], high[h], start=False, stop=final)
                last.then_inc(summed, 1)

            def tail(phase, th=hT_h, tl=hT_l):
                for b in range(TB):
                    for g in (GROUPS[phase] - 2, GROUPS[phase] - 1):
                        down(phase, g, b, th, tl)

            def transposes(name, src, signal=None):
                for b in range(TB):
                    if signal:
                        pe.wait_ge(S["norm_ready"], nth("norm_ready", signal, b))
                    for q in range(2):
                        dst = open_unit(name, b, q)
                        for i in range(4):
                            kt = 4 * q + i
                            last = nc.tensor.transpose(dst[:, i * P:(i + 1) * P], src[:, b, kt * P:(kt + 1) * P], ident)
                        last.then_inc(product, 1)

            def await_xT(phase):
                pe.wait_ge(S["xT_low"], nth("xT_low", phase, 3))

            def mod_sums(m):
                pe.wait_ge(raw_done, AT["mod", m] + 1)
                if m:
                    pe.wait_ge(mod_read, m)
                for i in range(2):
                    last = mm(mbank[:, i:i + 1], macc[:, m % 2, i * P:(i + 1) * P], ones[:, 0:1], start=True, stop=True)
                last.then_inc(mod_summed, 1)

            def feed_forward(phase, m0):
                for g in range(FFG):
                    up(PI[phase, "up", g], (phase, g))
                    if 0 < g < FFG - 1:
                        for b in range(TB):
                            down(phase, g - 1, b)
                    mod_sums(m0 + g)
                tail(phase)

            def gate_rows(layer):
                for n in range(2):
                    dst = open_unit("gate", layer, n)
                    pe.wait_ge(diag_ready, 2 * layer + n + 1)
                    diag = area_f if layer == 0 else kT_f
                    mm(dst[:, :], ones[:, :], diag[:, n * 512:(n + 1) * 512], start=True, stop=True).then_inc(product, 1)

            def attention(phase):
                qT = flat(rows).rearrange("p (h s) -> p h s", s=SEQ)
                for h in range(HEADS + 1):
                    if h < HEADS:
                        for b in range(TB):
                            keys = (b + 1) * P
                            dst = open_unit(phase, "S", h, b)
                            mla = phase == "mla"
                            last = mm(dst[:, 0:keys], qT[:, h, tok(b)], kT[:, h, 0:keys], start=True, stop=not mla)
                            if mla:
                                r = slice(ROPE * (h % 2), ROPE * (h % 2 + 1))
                                last = mm(dst[:, 0:keys], area[r, h // 2, tok(b)], area[r, 4, 0:keys], start=False, stop=True)
                            last.then_inc(product, 1)
                    if h:
                        g = h - 1
                        dst = open_unit(phase, "PT", g)
                        pe.wait_ge(S["probs"], nth("probs", phase, TB * g + 1))
                        p = buf_a[:, g % 2, :]
                        for i, (b, kb) in enumerate([(0, 0), (1, 0), (1, 1)]):
                            last = nc.tensor.transpose(dst[:, i * P:(i + 1) * P],
                                                       p[:, b * SEQ + kb * P:b * SEQ + (kb + 1) * P], ident)
                        last.then_inc(product, 1)
                        dst = open_unit(phase, "O", g)
                        await_evacuated(pe, phase, "PT", g)
                        pT = buf_b[:, g % 2, :]
                        mm(dst[:, 0:SEQ], z[:, 0, g * P:(g + 1) * P], pT[:, 0:SEQ], start=True, stop=False)
                        mm(dst[:, P:SEQ], z[:, 1, g * P:(g + 1) * P], pT[:, SEQ:SEQ + P], start=False, stop=True).then_inc(product, 1)

            pe.wait_ge(consts_in_done, 16)
            pe.wait_ge(x_in_done, 16)
            transposes("init", x)
            for b in range(TB):
                for q in range(2):
                    await_evacuated(pe, "init", b, q)
            for g in range(MXG):
                for kind in "ChB":
                    up(PI["sc", kind, g], ("sc", kind, g))
                if 0 < g < MXG - 1:
                    for b in range(TB):
                        down("sc", g - 1, b)
            tail("sc")

            transposes("ln0", z, "ln0")
            await_xT("ln0")
            pe.wait_ge(ones_ready, 1)
            feed_forward("ff0", 0)

            transposes("ln1", z, "ln1")
            await_xT("ln1")
            across(PI["mla", "dq", 0], ("mla", "cq", 0), KT, 2 * P)
            across(PI["mla", "dq", 1], ("mla", "cq", 1), KT, P)
            across(PI["mla", "dkv", 0], ("mla", "ckv"), KT, 2 * P)
            up(PI["mla", "kpe", 0], ("mla", "kpe"))
            cqn = flat(buf_a)[:, 0:TB * Q_LORA].rearrange("p (b n) -> p b n", b=TB)
            ckvn = buf_b[:, 0, :].rearrange("p (b n) -> p b n", b=TB)
            pe.wait_ge(lora_ready, 1)
            for b in range(TB):
                dst = open_unit("mla", "tq", b)
                for kt in range(QT):
                    last = nc.tensor.transpose(dst[:, kt * P:(kt + 1) * P], cqn[:, b, kt * P:(kt + 1) * P], ident)
                last.then_inc(product, 1)
            dst = open_unit("mla", "tkv")
            pe.wait_ge(lora_ready, 2)
            for kt in range(CT):
                for b in range(TB):
                    last = nc.tensor.transpose(dst[:, (kt * TB + b) * P:(kt * TB + b + 1) * P],
                                               ckvn[:, b, kt * P:(kt + 1) * P], ident)
            last.then_inc(product, 1)
            pe.wait_ge(lora_low, 3)
            ckv = (hT_h[:, QT:QT + CT, :], hT_l[:, QT:QT + CT, :])
            for n in range(4):
                up(PI["mla", "uk", 0], ("mla", "k", n), 2 * n, CT, *ckv)
            for b in range(TB):
                for n in range(2):
                    across(PI["mla", "uv", 0], ("mla", "v", b, n), CT, 512, n * 512, D, *ckv, blocks=[b])
            for kind in ("qn", "qp"):
                for n in range(4):
                    up(PI["mla", kind, n // 2], ("mla", kind, n), 2 * (n % 2), QT, hT_h, hT_l)
            await_evacuated(pe, "mla", "qn", 3)
            await_evacuated(pe, "mla", "v", 1, 1)
            pe.wait_ge(rope_ready, 5)
            attention("mla")
            for g in range(MXG - 2):
                for b in range(TB):
                    down("mla", g, b, xT_h, xT_l)
            tail("mla", xT_h, xT_l)

            transposes("ln2", z, "ln2")
            await_xT("ln2")
            feed_forward("ff1", FFG)

            transposes("rs1", z, "rs1")
            gate_rows(0)
            await_xT("rs1")
            for g in range(MXG + 2):
                if g < MXG:
                    up(PI["rg", "u", g], ("rg", "u", g))
                    up(PI["rg", "g", g], ("rg", "g", g))
                if 0 <= g - 1 < MXG:
                    pe.wait_ge(uc_low, g)
                    for i, kind in enumerate("ax"):
                        up(PI["rg", "ax", g - 1], ("rg", kind, g - 1), GT * i, GT, hT_h[:, 4:6, :], hT_l[:, 4:6, :])
                if 2 <= g < MXG:
                    for b in range(TB):
                        down("rg", g - 2, b)
            tail("rg")

            transposes("rs2", z, "rs2")
            await_xT("rs2")
            for kind in "qg":
                for g in range(MXG):
                    up(PI["mo", kind, g], ("mo", kind, g))
            transposes("rs2kv", z)
            await_xT("rs2kv")
            for g in range(MXG):
                up(PI["mo", "k", g], ("mo", "k", g))
            for g in range(MXG):
                across(PI["mo", "v", g], ("mo", "v", g), KT, 2 * P)
            for g in range(MXG):
                await_evacuated(pe, "mo", "q", g)
            for g in (1, 2, 3):
                await_evacuated(pe, "mo", "k", g)
                await_evacuated(pe, "mo", "v", g)
            attention("mo")
            gate_rows(1)
            for g in range(MXG - 2):
                for b in range(TB):
                    down("mo", g, b, xT_h, xT_l)
            tail("mo", xT_h, xT_l)
            assert issued == [len(UNITS), len(DN)]

        @block.gpsimd
        def _(pool):
            chain = [0]

            def link(instruction):
                chain[0] += 1
                instruction.then_inc(pool_chain, 1)
                pool.wait_ge(pool_chain, chain[0])

            nc.gpsimd.memset(ones[:, :], 1.0).then_inc(ones_ready, 1)
            link(nc.gpsimd.memset(minus_half, -0.5))

            def roots(name):
                for b in range(TB):
                    pool.wait_ge(S["var_ready"], nth("var_ready", name, b))
                    nc.gpsimd.tensor_tensor(rstd[:, b:b + 1], ve[:, b:b + 1], minus_half, ALU.pow).then_inc(S["rstd_ready"], 1)
                    if name[:2] == "ln":
                        pool_x(name, b)

            def pool_x(name, b):
                n = int(name[2])
                pool.wait_ge(gain_in, 16 * (n + 1))
                pool.wait_ge(shift_in, 16 * (n + 1))
                pool.wait_ge(S["norm_ready"], nth("norm_ready", name, b))
                link(nc.gpsimd.tensor_tensor(x[:, b, :], z[:, b, :], rows[:, 0, :], ALU.mult))
                nc.gpsimd.tensor_tensor(x[:, b, :], x[:, b, :], rows[:, 1, :], ALU.add).then_inc(S["x_ready"], 1)

            def diagonals(layer):
                dst = area_f if layer == 0 else kT_f
                for n in range(2):
                    for i in range(4):
                        t = 4 * n + i
                        last = nc.gpsimd.tensor_scalar(dst[:, t * P:(t + 1) * P], ident, mcol(f"gate{layer}", t), None, ALU.mult)
                    last.then_inc(diag_ready, 1)

            pool.wait_ge(consts_in_done, 16)
            for name in ("ln0", "ln1", "cq", "ckv", "ln2", "ln3"):
                roots(name)
            pool.wait_ge(mod_read, NMOD)
            diagonals(0)
            roots("rs1")
            roots("rs2")
            await_product(pool, "mo", "S", HEADS - 1, TB - 1)
            diagonals(1)
            roots("rs3")

        @block.scalar
        def _(act):
            done = [0]
            chain = [0]

            def link(instruction):
                chain[0] += 1
                instruction.then_inc(act_chain, 1)
                act.wait_ge(act_chain, chain[0])

            def split_ahead(key):
                while done[0] < len(PIECES) and done[0] <= PI[key] + AHEAD:
                    n = done[0]
                    s = AT["w", n]
                    act.wait_ge(raw_in[s % RAW], 16 * (s // RAW + 1))
                    if n >= RING:
                        await_piece_used(act, n - RING)
                    nc.scalar.copy(w_high[:, n % RING, 0:COLS[n]], raw[:, s % RAW, 0:COLS[n]]).then_inc(w_high_ready, 1)
                    done[0] += 1

            def hidden_high_of(phase, g):
                back = 2 if phase == "rg" else HRING
                if g >= back:
                    act.wait_ge(summed, DN[phase, g - back, TB - 1] + 1)
                t0 = hslot(phase, g)
                src = buf_b[:, g % 2, :].rearrange("p (t s) -> p t s", t=GT)
                nc.scalar.copy(hT_h[:, t0:t0 + GT, :], src).then_inc(hidden_high, 1)

            def norm_transposed(name):
                for b in range(TB):
                    for q in range(2):
                        await_evacuated(act, name, b, q)
                        src = stage[:, q, :].rearrange("p (t s) -> p t s", t=4)
                        nc.scalar.copy(xT_h[:, 4 * q:4 * q + 4, tok(b)], src).then_inc(S["xT_high"], 1)

            def feed_forward(phase):
                for g in range(FFG):
                    split_ahead((phase, "up", g))
                    await_product(act, phase, g)
                    if g >= 2:
                        await_evacuated(act, phase, g - 2)
                    nc.scalar.activation(buf_a[:, g % 2, :], bank_of(phase, g)[:, :], ACT.Relu).then_inc(relu, 1)
                    if g:
                        split_ahead((phase, "down", g - 1))
                    await_evacuated(act, phase, g)
                    hidden_high_of(phase, g)

            def attention(phase, scale):
                for h in range(HEADS + 1):
                    if h < HEADS:
                        for b in range(TB):
                            keys, c = (b + 1) * P, TB * (h % 2) + b
                            act.wait_ge(S["row_bias"], nth("row_bias", phase, TB * h + b))
                            if h >= 2:
                                await_product(act, phase, "PT", h - 2)
                            nc.scalar.activation(buf_a[:, h % 2, b * SEQ:b * SEQ + keys],
                                                 bank_of(phase, "S", h, b)[:, 0:keys], ACT.Exp,
                                                 bias=ebias[:, c:c + 1], scale=scale,
                                                 accum_out=rsum[:, c:c + 1]).then_inc(evacuates(phase, "S", h, b), 1)
                    if h:
                        g = h - 1
                        await_product(act, phase, "PT", g)
                        if g >= 2:
                            await_product(act, phase, "O", g - 2)
                        nc.scalar.copy(buf_b[:, g % 2, 0:3 * P], bank_of(phase, "PT", g)[:, 0:3 * P])\
                            .then_inc(evacuates(phase, "PT", g), 1)
                        await_evacuated(act, phase, "O", g)
                        nc.scalar.copy(xT_h[:, g, :], stage[:, g % 2, 0:SEQ]).then_inc(S["o_high"], 1)

            act.wait_ge(cols_in_done, 16)
            nc.scalar.activation(cth[:, :], colrange("c"), ACT.Tanh, scale=0.5).then_inc(c_tanh, 1)
            act.wait_ge(lam_exp_in, 1)
            nc.scalar.activation(prm[:, 7, :], prm[:, 6, :], ACT.Exp, scale=-1.0).then_inc(lam_exp, 1)

            for b in range(TB):
                for q in range(2):
                    await_product(act, "init", b, q)
                    src = bank_of("init", b, q)[:, :].rearrange("p (t s) -> p t s", t=4)
                    nc.scalar.copy(xT_h[:, 4 * q:4 * q + 4, tok(b)], src).then_inc(S["xT_high"], 1)
            for g in range(MXG):
                split_ahead(("sc", "C", g))
                await_product(act, "sc", "C", g)
                if g >= 2:
                    await_evacuated(act, "sc", "h", g - 2)
                nc.scalar.copy(kT_f[:, (g % 2) * 512:(g % 2 + 1) * 512], bank_of("sc", "C", g)[:, :])\
                    .then_inc(evacuates("sc", "C", g), 1)
                split_ahead(("sc", "h", g))
                split_ahead(("sc", "B", g))
                await_evacuated(act, "sc", "B", g)
                hidden_high_of("sc", g)
            split_ahead(("sc", "down", MXG - 1))
            norm_transposed("ln0")
            feed_forward("ff0")
            split_ahead(("ff0", "down", FFG - 1))
            norm_transposed("ln1")

            split_ahead(("mla", "dq", 0))
            split_ahead(("mla", "dkv", 0))
            for b in range(TB):
                await_evacuated(act, "mla", "tq", b)
                src = stage[:, b, 0:QT * P].rearrange("p (t s) -> p t s", t=QT)
                nc.scalar.copy(hT_h[:, 0:QT, tok(b)], src).then_inc(lora_high, 1)
            await_evacuated(act, "mla", "tkv")
            act.wait_ge(lora_low, 1)
            nc.scalar.copy(hT_h[:, QT:QT + CT, :], stage[:, 0, :].rearrange("p (t s) -> p t s", t=CT)).then_inc(lora_high, 1)
            split_ahead(("mla", "kpe", 0))
            for n in range(4):
                await_product(act, "mla", "k", n)
                nc.scalar.copy(kT[:, 2 * n:2 * n + 2, :], bank_of("mla", "k", n)[:, :].rearrange("p (t s) -> p t s", t=2))\
                    .then_inc(evacuates("mla", "k", n), 1)
            split_ahead(("mla", "uk", 0))
            act.wait_ge(S["x_ready"], nth("x_ready", "ln1", TB - 1))
            for b in range(TB):
                for n in range(2):
                    await_product(act, "mla", "v", b, n)
                    nc.scalar.copy(z[:, b, n * 512:(n + 1) * 512], bank_of("mla", "v", b, n)[:, :])\
                        .then_inc(evacuates("mla", "v", b, n), 1)
            split_ahead(("mla", "uv", 0))
            qT = flat(rows).rearrange("p (h s) -> p h s", s=SEQ)
            for n in range(4):
                await_product(act, "mla", "qn", n)
                nc.scalar.copy(qT[:, 2 * n:2 * n + 2, :], bank_of("mla", "qn", n)[:, :].rearrange("p (t s) -> p t s", t=2))\
                    .then_inc(evacuates("mla", "qn", n), 1)
                if n % 2:
                    split_ahead(("mla", "qn", n // 2))
            attention("mla", float(NOPE + ROPE) ** -0.5)
            for g in range(MXG):
                split_ahead(("mla", "down", g))
            norm_transposed("ln2")
            feed_forward("ff1")
            split_ahead(("ff1", "down", FFG - 1))
            norm_transposed("rs1")

            act.wait_ge(S["x_ready"], nth("x_ready", "ln3", TB - 1))
            for n in range(2):
                await_product(act, "gate", 0, n)
                nc.scalar.copy(rows[:, 0, n * 512:(n + 1) * 512], bank_of("gate", 0, n)[:, :]).then_inc(evacuates("gate", 0, n), 1)
            uT = flat(buf_a)[:, 0:GT * (SEQ + 3)].rearrange("p (t s) -> p t s", t=GT)
            thg = rows[:, 1, 0:512]
            for g in range(MXG + 1):
                if g < MXG:
                    split_ahead(("rg", "u", g))
                    await_product(act, "rg", "u", g)
                    act.wait_ge(conv_ready, g + 1)
                    nc.scalar.copy(uT[:, :, 3:], bank_of("rg", "u", g)[:, :].rearrange("p (t s) -> p t s", t=GT))\
                        .then_inc(evacuates("rg", "u", g), 1)
                    act.wait_ge(conv_ready, g + 2)
                    if g:
                        await_product(act, "rg", "x", g - 1)
                    nc.scalar.copy(hT_h[:, 4:6, :], kT[:, 2 * (g % 2):2 * (g % 2) + 2, :]).then_inc(uc_high, 1)
                    split_ahead(("rg", "g", g))
                    await_product(act, "rg", "g", g)
                    if g:
                        await_evacuated(act, "rg", "g", g - 1)
                    nc.scalar.activation(thg, bank_of("rg", "g", g)[:, :], ACT.Tanh, scale=0.5).then_inc(gate_tanh, 1)
                if g:
                    i = g - 1
                    split_ahead(("rg", "ax", i))
                    if i:
                        act.wait_ge(rg_hidden, i)
                    for n, (kind, half_bias) in enumerate((("a", HBA), ("x", HBX))):
                        await_product(act, "rg", kind, i)
                        for t in range(GT):
                            kt = GT * i + t
                            last = nc.scalar.activation(area_f[:, n * 512 + t * SEQ:n * 512 + (t + 1) * SEQ],
                                                        bank_of("rg", kind, i)[:, t * SEQ:(t + 1) * SEQ], ACT.Tanh,
                                                        scale=0.5, bias=half_bias[:, kt:kt + 1])
                        last.then_inc(evacuates("rg", kind, i), 1)
                    await_evacuated(act, "rg", "a", i)
                    for t in range(GT):
                        kt = GT * i + t
                        c4, src = C4[:, kt:kt + 1], area_f[:, t * SEQ:(t + 1) * SEQ]
                        nc.scalar.activation(stage[:, 0, t * SEQ:(t + 1) * SEQ], src, ACT.Exp, scale=c4, bias=c4)
                        last = nc.scalar.activation(area_f[:, 1024 + t * SEQ:1024 + (t + 1) * SEQ], src, ACT.Tanh, scale=c4, bias=c4)
                    last.then_inc(decay_ready, 1)
                    act.wait_ge(ratio_ready, i + 1)
                    nc.scalar.activation(area_f[:, 1024:1536], stage[:, 1, :], ACT.Sqrt).then_inc(root_ready, 1)
                    act.wait_ge(rg_hidden, i + 1)
                    hidden_high_of("rg", i)
            for g in range(MXG):
                split_ahead(("rg", "down", g))

            norm_transposed("rs2")
            for g in range(MXG):
                split_ahead(("mo", "q", g))
                await_product(act, "mo", "q", g)
                if g == 0:
                    act.wait_ge(S["y_read"], nth("y_read", "rg", TB - 1))
                nc.scalar.copy(qT[:, 2 * g:2 * g + 2, :], bank_of("mo", "q", g)[:, :].rearrange("p (t s) -> p t s", t=2))\
                    .then_inc(evacuates("mo", "q", g), 1)
            for g in range(MXG):
                split_ahead(("mo", "g", g))
                await_product(act, "mo", "g", g)
                if g >= 2:
                    await_evacuated(act, "mo", "g", g - 2)
                nc.scalar.activation(buf_a[:, g % 2, :], bank_of("mo", "g", g)[:, :], ACT.Tanh, scale=0.5).then_inc(gate_tanh, 1)
            norm_transposed("rs2kv")
            for g in range(MXG):
                split_ahead(("mo", "k", g))
                await_product(act, "mo", "k", g)
                nc.scalar.copy(kT[:, 2 * g:2 * g + 2, :], bank_of("mo", "k", g)[:, :].rearrange("p (t s) -> p t s", t=2))\
                    .then_inc(evacuates("mo", "k", g), 1)
            for g in range(MXG):
                split_ahead(("mo", "v", g))
                await_product(act, "mo", "v", g)
                nc.scalar.copy(z[:, :, g * SEQ:(g + 1) * SEQ], bank_of("mo", "v", g)[:, :].rearrange("p (b s) -> p b s", b=TB))\
                    .then_inc(evacuates("mo", "v", g), 1)
            attention("mo", float(P) ** -0.5)
            for n in range(2):
                await_product(act, "gate", 1, n)
                nc.scalar.copy(rows[:, 0, n * 512:(n + 1) * 512], bank_of("gate", 1, n)[:, :]).then_inc(evacuates("gate", 1, n), 1)
            assert done[0] == len(PIECES)

        @block.vector
        def _(dve):
            chain = [0]
            done = [0]
            tt, ts, stt = nc.vector.tensor_tensor, nc.vector.tensor_scalar, nc.vector.scalar_tensor_tensor

            def link(instruction):
                chain[0] += 1
                instruction.then_inc(dve_chain, 1)
                dve.wait_ge(dve_chain, chain[0])

            def f32(ap):
                return ap.bitcast(F32)

            def split_ahead(key):
                stop = AT["w", min(PI[key] + AHEAD, len(PIECES) - 1)]
                while done[0] <= stop:
                    s = done[0]
                    kind, n = STREAM[s]
                    slot = raw[:, s % RAW, :]
                    if kind == "w":
                        dve.wait_ge(w_high_ready, n + 1)
                        tt(w_low[:, n % RING, 0:COLS[n]], slot[:, 0:COLS[n]], f32(w_high[:, n % RING, 0:COLS[n]]),
                           ALU.subtract).then_inc(raw_done, 1)
                    else:
                        dve.wait_ge(raw_in[s % RAW], 16 * (s // RAW + 1))
                        if n >= 2:
                            dve.wait_ge(mod_summed, n - 1)
                        acc = macc[:, n % 2, :]
                        link(ts(acc, slot[:, 0:SEQ], cs[:, 0:1], None, ALU.mult))
                        for kt in range(1, KT):
                            step = stt(out=acc, in0=slot[:, kt * SEQ:(kt + 1) * SEQ], scalar=cs[:, kt:kt + 1],
                                       in1=acc, op0=ALU.mult, op1=ALU.add)
                            if kt < KT - 1:
                                link(step)
                        step.then_inc(raw_done, 1)
                    done[0] += 1

            def read_mod(m):
                dve.wait_ge(mod_summed, m + 1)
                tt(modcol[:, 2 * m:2 * m + 2], mbank[:, 0:2], colrange("mod_b", 2, 2 * m), ALU.add).then_inc(mod_read, 1)

            def hidden_low_of(phase, g):
                dve.wait_ge(hidden_high, nth("hidden_high", phase, g))
                t0 = hslot(phase, g)
                src = buf_b[:, g % 2, :].rearrange("p (t s) -> p t s", t=GT)
                tt(hT_l[:, t0:t0 + GT, :], src, f32(hT_h[:, t0:t0 + GT, :]), ALU.subtract).then_inc(hidden_low, 1)

            def mean_square_or_variance(parts, b, name, rms):
                for i, part in enumerate(parts):
                    last = nc.vector.bn_stats(stats[:, b, 6 * i:6 * i + 6], part)
                link(last)
                link(nc.vector.bn_aggr(mv[:, b, :], stats[:, b, 0:6 * len(parts)]))
                if rms:
                    link(stt(out=ve[:, b:b + 1], in0=mv[:, b, 0:1], scalar=mv[:, b, 0:1], in1=mv[:, b, 1:2], op0=ALU.mult, op1=ALU.add))
                    ts(ve[:, b:b + 1], ve[:, b:b + 1], RMS_EPS, None, ALU.add).then_inc(S["var_ready"], 1)
                else:
                    ts(ve[:, b:b + 1], mv[:, b, 1:2], LN_EPS, None, ALU.add).then_inc(S["var_ready"], 1)

            def halves(t, b):
                return [t[:, b, 0:512], t[:, b, 512:1024]]

            def await_rstd(name, b):
                dve.wait_ge(S["rstd_ready"], nth("rstd_ready", name, b))

            def layer_norm(name, phase, b, x_before):
                dve.wait_ge(summed, DN[phase, GROUPS[phase] - 1, b] + 1)
                if x_before:
                    dve.wait_ge(S["x_ready"], nth("x_ready", x_before, b))
                for h in range(2):
                    last = stt(out=z[:, b, h * 512:(h + 1) * 512], in0=x[:, b, h * 512:(h + 1) * 512], scalar=ALPHA,
                               in1=Y[b][h][:, :], op0=ALU.mult, op1=ALU.add)
                last.then_inc(S["y_read"], 1)
                dve.wait_ge(S["y_read"], nth("y_read", phase, b))
                mean_square_or_variance(halves(z, b), b, name, False)
                await_rstd(name, b)
                ts(z[:, b, :], z[:, b, :], mv[:, b, 0:1], rstd[:, b:b + 1], ALU.subtract, ALU.mult).then_inc(S["norm_ready"], 1)

            def rms_norm(name, b):
                mean_square_or_variance(halves(x, b), b, name, True)
                await_rstd(name, b)
                ts(z[:, b, :], x[:, b, :], rstd[:, b:b + 1], None, ALU.mult).then_inc(S["norm_ready"], 1)

            def gated_residual(phase, layer, b):
                if b == 0:
                    for n in range(2):
                        await_evacuated(dve, "gate", layer, n)
                dve.wait_ge(summed, DN[phase, GROUPS[phase] - 1, b] + 1)
                for h in range(2):
                    last = tt(z[:, b, h * 512:(h + 1) * 512], Y[b][h][:, :], rows[:, 0, h * 512:(h + 1) * 512], ALU.mult)
                last.then_inc(S["y_read"], 1)
                dve.wait_ge(S["y_read"], nth("y_read", phase, b))
                link(tt(x[:, b, :], x[:, b, :], z[:, b, :], ALU.add))

            def split_transposed(name, b, gain, shift):
                for q in range(2):
                    await_product(dve, name, b, q)
                    src = bank_of(name, b, q)
                    for i in range(4):
                        kt = 4 * q + i
                        last = ts(stage[:, q, i * P:(i + 1) * P], src[:, i * P:(i + 1) * P], gain(kt), shift(kt), ALU.mult, ALU.add)
                    last.then_inc(evacuates(name, b, q), 1)
                for q in range(2):
                    dve.wait_ge(S["xT_high"], nth("xT_high", name, 2 * b + q))
                    tt(xT_l[:, 4 * q:4 * q + 4, tok(b)], stage[:, q, :].rearrange("p (t s) -> p t s", t=4),
                       f32(xT_h[:, 4 * q:4 * q + 4, tok(b)]), ALU.subtract).then_inc(S["xT_low"], 1)
                dve.wait_ge(S["xT_low"], nth("xT_low", name, 2 * b + 1))

            def ln_then_transpose(name, phase, x_before):
                for b in range(TB):
                    layer_norm(name, phase, b, x_before)
                    split_transposed(name, b, lambda kt: col(f"{name}_g", kt), lambda kt: col(f"{name}_b", kt))

            def feed_forward(phase, m0):
                for g in range(FFG):
                    split_ahead((phase, "up", g))
                    dve.wait_ge(relu, nth("relu", phase, g))
                    stt(out=buf_b[:, g % 2, :], in0=bank_of(phase, g)[:, :], scalar=0.0, in1=buf_a[:, g % 2, :],
                        op0=ALU.max, op1=ALU.mult).then_inc(evacuates(phase, g), 1)
                    if g:
                        read_mod(m0 + g - 1)
                        split_ahead((phase, "down", g - 1))
                    hidden_low_of(phase, g)
                read_mod(m0 + FFG - 1)
                split_ahead((phase, "down", FFG - 1))

            def attention(phase, scale):
                for h in range(HEADS + 1):
                    if h < HEADS:
                        for b in range(TB):
                            keys, c = (b + 1) * P, TB * (h % 2) + b
                            await_product(dve, phase, "S", h, b)
                            s = bank_of(phase, "S", h, b)
                            if phase == "mla":
                                link(nc.vector.memset(s[0:64, keys - 64:keys], NEG_INF))
                            else:
                                link(tt(s[:, keys - P:keys], s[:, keys - P:keys], tri, ALU.add))
                            link(nc.vector.reduce_max(nmx[:, c:c + 1], s[:, 0:keys], AXX, negate=True))
                            ts(ebias[:, c:c + 1], nmx[:, c:c + 1], scale, None, ALU.mult).then_inc(S["row_bias"], 1)
                        for b in range(TB):
                            keys, c = (b + 1) * P, TB * (h % 2) + b
                            await_evacuated(dve, phase, "S", h, b)
                            link(nc.vector.reciprocal(rinv[:, c:c + 1], rsum[:, c:c + 1]))
                            p = buf_a[:, h % 2, b * SEQ:b * SEQ + keys]
                            ts(p, p, rinv[:, c:c + 1], None, ALU.mult).then_inc(S["probs"], 1)
                    if h:
                        g = h - 1
                        await_product(dve, phase, "O", g)
                        o, st = bank_of(phase, "O", g)[:, 0:SEQ], stage[:, g % 2, 0:SEQ]
                        if phase == "mla":
                            nc.vector.tensor_copy(st, o).then_inc(evacuates(phase, "O", g), 1)
                        else:
                            stt(out=st, in0=o, scalar=0.5, in1=area[:, g, :], op0=ALU.mult, op1=ALU.mult)\
                                .then_inc(evacuates(phase, "O", g), 1)
                        dve.wait_ge(S["o_high"], nth("o_high", phase, g))
                        tt(xT_l[:, g, :], st, f32(xT_h[:, g, :]), ALU.subtract).then_inc(S["o_low"], 1)

            dve.wait_ge(cols_in_done, 16)
            lam, r2, s, d, poly, s2 = colrange("lam"), prm[:, 8, :], prm[:, 9, :], prm[:, 10, :], prm[:, 11, :], prm[:, 5, :]
            link(ts(r2, lam, -1.0, 0.0, ALU.mult, ALU.max))
            link(ts(prm[:, 7, :], lam, 0.0, None, ALU.max))
            tt(prm[:, 6, :], prm[:, 7, :], r2, ALU.add).then_inc(lam_exp_in, 1)
            ts(HBA, colrange("rg_ba"), 0.5, None, ALU.mult)
            link(ts(HBX, colrange("rg_bx"), 0.5, None, ALU.mult))
            dve.wait_ge(c_tanh, 1)
            link(stt(out=cs[:, :], in0=cth[:, :], scalar=1.0, in1=colrange("c"), op0=ALU.add, op1=ALU.mult))
            link(ts(cs[:, :], cs[:, :], 0.5, None, ALU.mult))
            dve.wait_ge(lam_exp, 1)
            e = prm[:, 7, :]
            link(ts(d, e, 2.0, None, ALU.add))
            link(nc.vector.reciprocal(d, d))
            link(tt(s, e, d, ALU.mult))
            link(tt(s2, s, s, ALU.mult))
            link(ts(poly, s2, 1.0 / 15, None, ALU.mult))
            for odd in (13, 11, 9, 7, 5, 3):
                link(stt(out=poly, in0=poly, scalar=1.0 / odd, in1=s2, op0=ALU.add, op1=ALU.mult))
            link(stt(out=poly, in0=poly, scalar=1.0, in1=s, op0=ALU.add, op1=ALU.mult))
            link(ts(r2, r2, -2.0 * RG_C / 4, None, ALU.mult))
            link(stt(out=C4, in0=poly, scalar=-RG_C, in1=r2, op0=ALU.mult, op1=ALU.add))

            for b in range(TB):
                for q in range(2):
                    dve.wait_ge(S["xT_high"], nth("xT_high", "init", 2 * b + q))
                    tt(xT_l[:, 4 * q:4 * q + 4, tok(b)], bank_of("init", b, q)[:, :].rearrange("p (t s) -> p t s", t=4),
                       f32(xT_h[:, 4 * q:4 * q + 4, tok(b)]), ALU.subtract).then_inc(evacuates("init", b, q), 1)

            ch = area_f[:, 0:GT * (SEQ + 2)].rearrange("p (t s) -> p t s", t=GT)
            conv = area_f[:, 1024:1536].rearrange("p (t s) -> p t s", t=GT)
            link(nc.vector.memset(ch[:, :, 0:2], 0.0))
            for g in range(MXG):
                split_ahead(("sc", "C", g))
                await_evacuated(dve, "sc", "C", g)
                await_product(dve, "sc", "h", g)
                tt(ch[:, :, 2:], bank_of("sc", "h", g)[:, :].rearrange("p (t s) -> p t s", t=GT),
                   kT_f[:, (g % 2) * 512:(g % 2 + 1) * 512].rearrange("p (t s) -> p t s", t=GT), ALU.mult)\
                    .then_inc(evacuates("sc", "h", g), 1)
                split_ahead(("sc", "h", g))
                await_evacuated(dve, "sc", "h", g)
                for t in range(GT):
                    last = ts(conv[:, t, :], ch[:, t, 2:2 + SEQ], col("sc_w", 2 * KT + GT * g + t), None, ALU.mult)
                link(last)
                for k in (1, 0):
                    for t in range(GT):
                        last = stt(out=conv[:, t, :], in0=ch[:, t, k:k + SEQ], scalar=col("sc_w", k * KT + GT * g + t),
                                   in1=conv[:, t, :], op0=ALU.mult, op1=ALU.add)
                    link(last)
                split_ahead(("sc", "B", g))
                await_product(dve, "sc", "B", g)
                tt(buf_b[:, g % 2, :], bank_of("sc", "B", g)[:, :], area_f[:, 1024:1536], ALU.mult).then_inc(evacuates("sc", "B", g), 1)
                hidden_low_of("sc", g)
            split_ahead(("sc", "down", MXG - 1))
            ln_then_transpose("ln0", "sc", None)
            feed_forward("ff0", 0)
            ln_then_transpose("ln1", "ff0", "ln0")

            split_ahead(("mla", "dq", 0))
            cq, cq2, ckv = bank_of("mla", "cq", 0), bank_of("mla", "cq", 1), bank_of("mla", "ckv")
            cqn = flat(buf_a)[:, 0:TB * Q_LORA].rearrange("p (b n) -> p b n", b=TB)
            ckvn = buf_b[:, 0, :].rearrange("p (b n) -> p b n", b=TB)
            await_product(dve, "mla", "cq", 1)
            for b in range(TB):
                mean_square_or_variance([cq[:, b * SEQ:(b + 1) * SEQ], cq2[:, b * P:(b + 1) * P]], b, "cq", True)
            for b in range(TB):
                await_rstd("cq", b)
                last = ts(cqn[:, b, 0:SEQ], cq[:, b * SEQ:(b + 1) * SEQ], rstd[:, b:b + 1], None, ALU.mult)
            last.then_inc(evacuates("mla", "cq", 0), 1)
            for b in range(TB):
                last = ts(cqn[:, b, SEQ:], cq2[:, b * P:(b + 1) * P], rstd[:, b:b + 1], None, ALU.mult)
            last.then_inc(evacuates("mla", "cq", 1), 1)
            await_evacuated(dve, "mla", "cq", 1)
            nc.vector.engine_nop().then_inc(lora_ready, 1)
            split_ahead(("mla", "dkv", 0))
            await_product(dve, "mla", "ckv")
            for b in range(TB):
                mean_square_or_variance([ckv[:, b * SEQ:(b + 1) * SEQ]], b, "ckv", True)
            for b in range(TB):
                await_rstd("ckv", b)
                last = ts(ckvn[:, b, :], ckv[:, b * SEQ:(b + 1) * SEQ], rstd[:, b:b + 1], None, ALU.mult)
            last.then_inc(evacuates("mla", "ckv"), 1)
            await_evacuated(dve, "mla", "ckv")
            nc.vector.engine_nop().then_inc(lora_ready, 1)

            def rope(n, *key):
                await_product(dve, *key)
                src = bank_of(*key)
                tt(area[:, 5, :], src[:, 0:SEQ], cosT, ALU.mult)
                tt(area[:, 6, :], src[:, SEQ:], sinT, ALU.mult).then_inc(evacuates(*key), 1)
                await_evacuated(dve, *key)
                tt(area[:, n, :], area[:, 5, :], area[:, 6, :], ALU.add).then_inc(rope_ready, 1)

            rope(4, "mla", "kpe")
            for b in range(TB):
                await_product(dve, "mla", "tq", b)
                for kt in range(QT):
                    last = ts(stage[:, b, kt * P:(kt + 1) * P], bank_of("mla", "tq", b)[:, kt * P:(kt + 1) * P], col("g_q", kt), None, ALU.mult)
                last.then_inc(evacuates("mla", "tq", b), 1)
            for b in range(TB):
                dve.wait_ge(lora_high, b + 1)
                tt(hT_l[:, 0:QT, tok(b)], stage[:, b, 0:QT * P].rearrange("p (t s) -> p t s", t=QT),
                   f32(hT_h[:, 0:QT, tok(b)]), ALU.subtract).then_inc(lora_low, 1)
            dve.wait_ge(lora_low, 1)
            await_product(dve, "mla", "tkv")
            for kt in range(CT):
                last = ts(stage[:, 0, kt * SEQ:(kt + 1) * SEQ], bank_of("mla", "tkv")[:, kt * SEQ:(kt + 1) * SEQ], col("g_kv", kt), None, ALU.mult)
            last.then_inc(evacuates("mla", "tkv"), 1)
            dve.wait_ge(lora_high, 3)
            tt(hT_l[:, QT:QT + CT, :], stage[:, 0, :].rearrange("p (t s) -> p t s", t=CT),
               f32(hT_h[:, QT:QT + CT, :]), ALU.subtract).then_inc(lora_low, 1)
            for kind in ("kpe", "uk", "uv"):
                split_ahead(("mla", kind, 0))
            split_ahead(("mla", "qn", 1))
            dve.wait_ge(rope_ready, 1)
            for n in range(4):
                rope(n, "mla", "qp", n)
                dve.wait_ge(rope_ready, n + 2)
            attention("mla", float(NOPE + ROPE) ** -0.5)
            for g in range(MXG):
                split_ahead(("mla", "down", g))
            ln_then_transpose("ln2", "mla", "ln1")
            feed_forward("ff1", FFG)

            dve.wait_ge(mod_read, NMOD)
            for dst, scale, gain in ((A0, "scale0", "norm_g0"), (A1, "scale1", "norm_g1"), (AK, "kv_scale", "kv_g")):
                last = stt(out=dst, in0=mrange(scale), scalar=1.0, in1=colrange(gain), op0=ALU.add, op1=ALU.mult)
            link(last)
            for b in range(TB):
                layer_norm("ln3", "ff1", b, "ln2")
            for b in range(TB):
                dve.wait_ge(S["x_ready"], nth("x_ready", "ln3", b))
                rms_norm("rs1", b)
                split_transposed("rs1", b, lambda kt: A0[:, kt:kt + 1], lambda kt: mcol("shift0", kt))

            uT = flat(buf_a)[:, 0:GT * (SEQ + 3)].rearrange("p (t s) -> p t s", t=GT)
            nc.vector.memset(uT[:, :, 0:3], 0.0).then_inc(conv_ready, 1)
            hs = rows[:, 1, 512:1024]
            for g in range(MXG + 1):
                if g < MXG:
                    uc = kT[:, 2 * (g % 2):2 * (g % 2) + 2, :]
                    sg = kT_f[:, 1024 + (g % 2) * 512:1024 + (g % 2 + 1) * 512]
                    split_ahead(("rg", "u", g))
                    await_evacuated(dve, "rg", "u", g)
                    for t in range(GT):
                        kt = GT * g + t
                        last = ts(uc[:, t, :], uT[:, t, 3:3 + SEQ], col("rg_w", 3 * KT + kt), col("rg_cb", kt), ALU.mult, ALU.add)
                    link(last)
                    for k in (2, 1, 0):
                        for t in range(GT):
                            last = stt(out=uc[:, t, :], in0=uT[:, t, k:k + SEQ], scalar=col("rg_w", k * KT + GT * g + t),
                                       in1=uc[:, t, :], op0=ALU.mult, op1=ALU.add)
                        if k:
                            link(last)
                    last.then_inc(conv_ready, 1)
                    dve.wait_ge(conv_ready, g + 2)
                    dve.wait_ge(uc_high, g + 1)
                    tt(hT_l[:, 4:6, :], uc, f32(hT_h[:, 4:6, :]), ALU.subtract).then_inc(uc_low, 1)
                    split_ahead(("rg", "g", g))
                    dve.wait_ge(gate_tanh, g + 1)
                    stt(out=sg, in0=thg_of(rows), scalar=1.0, in1=bank_of("rg", "g", g)[:, :], op0=ALU.add, op1=ALU.mult)\
                        .then_inc(evacuates("rg", "g", g), 1)
                if g:
                    i = g - 1
                    uc = kT_f[:, (i % 2) * 512:(i % 2 + 1) * 512]
                    sg = kT_f[:, 1024 + (i % 2) * 512:1024 + (i % 2 + 1) * 512]
                    th_x, th_l, ratio = area_f[:, 512:1024], area_f[:, 1024:1536], stage[:, 1, :]
                    split_ahead(("rg", "ax", i))
                    dve.wait_ge(decay_ready, i + 1)
                    link(ts(ratio, th_l, -1.0, 1.0, ALU.mult, ALU.add))
                    link(nc.vector.reciprocal(ratio, ratio))
                    stt(out=ratio, in0=th_l, scalar=-0.5, in1=ratio, op0=ALU.mult, op1=ALU.mult).then_inc(ratio_ready, 1)
                    await_evacuated(dve, "rg", "x", i)
                    link(stt(out=th_x, in0=th_x, scalar=1.0, in1=uc, op0=ALU.add, op1=ALU.mult))
                    dve.wait_ge(root_ready, i + 1)
                    link(tt(th_x, th_x, th_l, ALU.mult))
                    for t in range(GT):
                        last = nc.vector.tensor_tensor_scan(hs[:, t * SEQ:(t + 1) * SEQ], stage[:, 0, t * SEQ:(t + 1) * SEQ],
                                                            th_x[:, t * SEQ:(t + 1) * SEQ], 0.0, ALU.mult, ALU.add)
                    link(last)
                    stt(out=buf_b[:, i % 2, :], in0=hs, scalar=0.5, in1=sg, op0=ALU.mult, op1=ALU.mult).then_inc(rg_hidden, 1)
                    hidden_low_of("rg", i)
            for g in range(MXG):
                split_ahead(("rg", "down", g))
            for b in range(TB):
                gated_residual("rg", 0, b)
                rms_norm("rs2", b)
                split_transposed("rs2", b, lambda kt: A1[:, kt:kt + 1], lambda kt: mcol("shift1", kt))

            for g in range(MXG):
                split_ahead(("mo", "q", g))
            for g in range(MXG):
                split_ahead(("mo", "g", g))
                dve.wait_ge(gate_tanh, MXG + g + 1)
                stt(out=area_f[:, g * 512:(g + 1) * 512], in0=buf_a[:, g % 2, :], scalar=1.0, in1=bank_of("mo", "g", g)[:, :],
                    op0=ALU.add, op1=ALU.mult).then_inc(evacuates("mo", "g", g), 1)
            for b in range(TB):
                split_transposed("rs2kv", b, lambda kt: AK[:, kt:kt + 1], lambda kt: mcol("kv_shift", kt))
            for kind in "kv":
                for g in range(MXG):
                    split_ahead(("mo", kind, g))
            attention("mo", float(P) ** -0.5)
            for b in range(TB):
                gated_residual("mo", 1, b)
                rms_norm("rs3", b)
                dve.wait_ge(S["norm_ready"], nth("norm_ready", "rs3", b))
                dve.wait_ge(shift_in, 16 * 5)
                tt(z[:, b, :], z[:, b, :], rows[:, 1, :], ALU.mult).then_inc(out_ready, 1)
            assert done[0] == len(STREAM)


def thg_of(rows):
    return rows[:, 1, 0:512]


def tiles(w, kts, width=P):
    k, n = w.shape
    return w.reshape(kts, P, n // width, width).transpose(1, 2, 0, 3).reshape(P, -1)


def k_major(w, kts):
    return w.reshape(kts, P, w.shape[1]).transpose(1, 0, 2).reshape(P, -1)


def piece_of(i, phase, kind, g):
    sl = slice(g * GT * P, (g + 1) * GT * P)
    if kind == "down":
        w = {"sc": i["sc_w_out"][0], "ff0": i["ff_w2"][0], "mla": i["mla_w_o"][0], "ff1": i["ff_w2"][1],
             "rg": i["rg_w_out_2"][0], "mo": i["att_w_out_2"][0]}[phase]
        return k_major(w[sl, :], GT)
    if phase == "sc":
        return tiles(i["sc_w_in"][0][:, "BCh".index(kind) * D:][:, sl], KT)
    if kind == "up":
        return tiles(i["ff_w1"][int(phase[2])][:, sl], KT)
    if phase == "mla":
        if kind == "dq":
            return k_major(i["mla_w_dq"][0][:, 0:2 * P] if g == 0 else i["mla_w_dq"][0][:, 2 * P:], KT)
        dkv = i["mla_w_dkv"][0]
        if kind == "dkv":
            return k_major(dkv[:, 0:KV_LORA], KT)
        if kind == "kpe":
            a, b = dkv[:, KV_LORA:KV_LORA + ROPE // 2], dkv[:, KV_LORA + ROPE // 2:]
            return tiles(np.concatenate([a, b, a, b, b, a, b, a], axis=1), KT)
        if kind == "uk":
            return tiles(i["mla_w_uk"][0].reshape(KV_LORA, HEADS * P), CT)
        if kind == "uv":
            return k_major(i["mla_w_uv"][0].reshape(KV_LORA, HEADS * P), CT)
        uq = i["mla_w_uq"][0].reshape(Q_LORA, HEADS, NOPE + ROPE)
        if kind == "qn":
            return tiles(uq[:, 4 * g:4 * g + 4, 0:NOPE].reshape(Q_LORA, 4 * P), QT)
        parts = []
        for pair in (2 * g, 2 * g + 1):
            halves = [[uq[:, h, NOPE:NOPE + ROPE // 2], uq[:, h, NOPE + ROPE // 2:]] for h in (2 * pair, 2 * pair + 1)]
            parts += [halves[0][0], halves[0][1], halves[1][0], halves[1][1]]
            parts += [halves[0][1], halves[0][0], halves[1][1], halves[1][0]]
        return tiles(np.concatenate(parts, axis=1), QT)
    if kind == "ax":
        return np.concatenate([tiles(i["rg_w_a_2"][0][g], GT), tiles(i["rg_w_x_2"][0][g], GT)], axis=1)
    w = {"rg": i["rg_w_in_2"][0], "mo": i["att_w_in_2"][0] if kind in "qg" else i["w_kv_2"]}[phase]
    w = w[:, ("ug" if phase == "rg" else "qg" if kind in "qg" else "kv").index(kind) * D:][:, sl]
    return k_major(w, KT) if kind == "v" else tiles(w, KT)


def pack_weights(i):
    mod = np.concatenate([i["mod_w_2"][0], i["mod_w_2"][1], i["kv_mod_w_2"]], axis=1)
    parts = []
    for kind, n in STREAM:
        if kind == "mod":
            a = k_major(mod[:, n * 2 * P:(n + 1) * 2 * P], KT)
        else:
            a = piece_of(i, *PIECES[n][0])
            assert a.shape == (P, COLS[n]), (PIECES[n], a.shape)
        parts.append(a.reshape(-1))
    return np.concatenate(parts)


def pack_cols(i):
    def c(v):
        return v.reshape(-1, P).T

    of = {"c": c(i["c_2"]), "mod_b": np.concatenate([c(i["mod_b_2"][0]), c(i["mod_b_2"][1]), c(i["kv_mod_b_2"])], axis=1),
          "norm_g0": c(i["norm_g_2"][0]), "norm_g1": c(i["norm_g_2"][1]), "kv_g": c(i["kv_norm_g_2"]),
          "ln0_g": c(i["ln_mix_g"][0]), "ln0_b": c(i["ln_mix_b"][0]), "ln1_g": c(i["ln_ff_g"][0]), "ln1_b": c(i["ln_ff_b"][0]),
          "ln2_g": c(i["ln_mix_g"][1]), "ln2_b": c(i["ln_mix_b"][1]),
          "sc_w": c(i["sc_conv_w"][0]), "rg_w": c(i["rg_conv_w_2"][0]), "rg_cb": c(i["rg_conv_b_2"]),
          "rg_ba": c(i["rg_b_a_2"]), "rg_bx": c(i["rg_b_x_2"]), "lam": c(i["rg_lambda_2"]),
          "g_q": c(i["mla_g_q"]), "g_kv": c(i["mla_g_kv"])}
    return np.ascontiguousarray(np.concatenate([of[name] for name in COL_WIDTHS], axis=1))


def constants():
    r = np.arange(P)
    tri = np.where(r[None, :] > r[:, None], np.float32(NEG_INF), np.float32(0))
    freq = np.float32(10000.0) ** (-np.arange(0, ROPE, 2, dtype=np.float32) / np.float32(ROPE))
    angle = (np.arange(SEQ, dtype=np.float32)[:, None] * freq[None, :]).T
    cos, sin = np.cos(angle)[r % (ROPE // 2)], np.sin(angle)[r % (ROPE // 2)]
    sin = np.where((r % ROPE < ROPE // 2)[:, None], -sin, sin)
    return np.concatenate([np.eye(P), tri, cos, sin], axis=1).astype(np.float32)


def kernel(**inputs):
    import concourse.bacc as bacc
    from concourse.bass_utils import run_bass_kernel_spmd

    i = {name: np.asarray(a) for name, a in inputs.items()}
    rows = np.stack([i["ln_mix_g"][0], i["ln_mix_b"][0], i["ln_ff_g"][0], i["ln_ff_b"][0],
                     i["ln_mix_g"][1], i["ln_mix_b"][1], i["ln_ff_g"][1], i["ln_ff_b"][1], i["final_norm_g_2"]])
    arrays = {"weights": pack_weights(i), "x_in": np.ascontiguousarray(i["x"][0]), "cols_in": pack_cols(i),
              "consts_in": constants(), "rows_in": rows}
    nc = bacc.Bacc("TRN2", target_bir_lowering=False, num_devices=1)
    args = [nc.dram_tensor(name, a.shape, F32, kind="ExternalInput").ap() for name, a in arrays.items()]
    out = nc.dram_tensor("out", (SEQ, D), F32, kind="ExternalOutput").ap()
    build(nc, *args, out)
    r = run_bass_kernel_spmd(nc, [arrays], core_ids=[0])
    return r.results[0]["out"].reshape(1, SEQ, D)
```

```python
from contextlib import ExitStack

import concourse.bass as bass
import numpy as np
from concourse import mybir

F32 = mybir.dt.float32
F32R = mybir.dt.float32r
ALU = mybir.AluOpType
ACT = mybir.ActivationFunctionType
AXX = mybir.AxisListType.X

P = 128
SEQ, D, D_FF = 256, 1024, 4096
TB = SEQ // P
KT = D // P
HEADS = 8
NOPE, ROPE = 128, 64
Q_LORA, KV_LORA = 384, 256
QT, CT = Q_LORA // P, KV_LORA // P
RG_C = 8.0
ALPHA = 4.0 ** 0.25
LN_EPS, RMS_EPS = 1e-5, 1e-6
NEG_INF = -1e30
GT = 2
FFG = D_FF // (GT * P)
MXG = D // (GT * P)
NMOD = 2 * FFG

PIECE = 2048
RAW = 3
RING = 6
AHEAD = 4
PBANKS = 3
HRING = 3


def piece_table():
    t = []

    def add(phase, kind, n, cols=PIECE):
        t.append(((phase, kind, n), cols))

    for g in range(MXG):
        for kind in "ChB":
            add("sc", kind, g)
        if g:
            add("sc", "down", g - 1)
    add("sc", "down", MXG - 1)

    def ff(phase):
        for g in range(FFG):
            add(phase, "up", g)
            if g:
                add(phase, "down", g - 1)
        add(phase, "down", FFG - 1)

    ff("ff0")
    for n in range(2):
        add("mla", "dq", n, KT // 2 * Q_LORA)
    add("mla", "dkv", 0)
    add("mla", "kpe", 0)
    add("mla", "uk", 0)
    add("mla", "uv", 0)
    for g in range(MXG):
        add("mla", "q", g, 2 * GT * QT * P)
    for g in range(MXG):
        add("mla", "down", g)
    ff("ff1")
    for g in range(MXG + 2):
        if g < MXG:
            add("rg", "u", g)
            add("rg", "g", g)
        if 0 <= g - 1 < MXG:
            add("rg", "ax", g - 1, 2 * GT * 2 * P)
        if g >= 2:
            add("rg", "down", g - 2)
    for kind in ("k", "v", "qg"):
        for g in range(MXG):
            for k in kind:
                add("mo", k, g)
    for g in range(MXG):
        add("mo", "down", g)
    return t


PIECES = piece_table()
COLS = [c for _, c in PIECES]
PI = {key: n for n, (key, _) in enumerate(PIECES)}


def stream_table():
    t, m = [], 0
    for n, ((phase, kind, g), _) in enumerate(PIECES):
        t.append(("w", n))
        if kind == "up":
            t.append(("mod", m))
            m += 1
    return t


STREAM = stream_table()
AT = {item: n for n, item in enumerate(STREAM)}
WIDTH = [COLS[n] if kind == "w" else PIECE for kind, n in STREAM]


def unit_table():
    t = []

    def norm(name):
        t.extend((name, b, q) for b in range(TB) for q in range(2))

    def attention(phase, projections):
        for g in range(MXG + 1):
            if g < MXG:
                t.extend((phase, kind, g) for kind in projections)
            if g:
                t.extend((phase, kind, h) for kind in ("PT", "O") for h in (GT * g - 2, GT * g - 1))

    norm("init")
    for g in range(MXG):
        t.extend(("sc", kind, g) for kind in "ChB")
    norm("ln0")
    t.extend(("ff0", g) for g in range(FFG))
    norm("ln1")
    t.append(("mla", "kpe"))
    t.extend([("mla", "tq", 0), ("mla", "tq", 1), ("mla", "tkv")])
    t.extend(("mla", "k", n) for n in range(4))
    t.extend(("mla", "v", b, n) for b in range(TB) for n in range(2))
    attention("mla", ("qn", "qp"))
    norm("ln2")
    t.extend(("ff1", g) for g in range(FFG))
    norm("rs1")
    t.extend([("gate", 0, 0), ("gate", 0, 1)])
    for g in range(MXG + 1):
        if g < MXG:
            t.extend([("rg", "u", g), ("rg", "g", g)])
        if g:
            t.extend([("rg", "a", g - 1), ("rg", "x", g - 1)])
    norm("rs2kv")
    t.extend(("mo", "k", g) for g in range(MXG))
    t.extend(("mo", "v", g) for g in range(MXG))
    norm("rs2")
    attention("mo", "qg")
    t.extend([("gate", 1, 0), ("gate", 1, 1)])
    return t


UNITS = unit_table()
UN = {key: n for n, key in enumerate(UNITS)}

def down_table():
    t = []
    for phase, groups in (("sc", MXG), ("ff0", FFG), ("mla", MXG), ("ff1", FFG), ("rg", MXG), ("mo", MXG)):
        t.extend((phase, g, b) for g in range(groups - 2) for b in range(TB))
        t.extend((phase, g, b) for b in range(TB) for g in (groups - 2, groups - 1))
    return t


DN = {key: n for n, key in enumerate(down_table())}
GROUPS = {"sc": MXG, "ff0": FFG, "mla": MXG, "ff1": FFG, "rg": MXG, "mo": MXG}


def last_unit(phase, kind, n):
    if kind == "up":
        return (phase, n)
    if phase == "mla" and kind == "q":
        return ("mla", "qp", n)
    return {"kpe": ("mla", "kpe"), "uk": ("mla", "k", 3), "uv": ("mla", "v", 1, 1),
            "ax": ("rg", "x", n)}.get(kind, (phase, kind, n))


NORMS = {"ln0": TB, "ln1": TB, "latent": 2 * TB, "ln2": TB, "ln3": 2 * TB, "rs2": TB, "rs3": TB}
HIDDEN = {"sc": MXG, "ff0": FFG, "ff1": FFG, "rg": MXG}
SIGNALS = {
    "relu": {"ff0": FFG, "ff1": FFG},
    "hidden_high": HIDDEN,
    "hidden_low": HIDDEN,
    "y_read": {p: TB for p in GROUPS},
    "var_ready": NORMS,
    "rstd_ready": NORMS,
    "norm_ready": {p: n for p, n in NORMS.items() if p != "latent"},
    "xT_high": {p: 4 for p in ("init", "ln0", "ln1", "ln2", "rs1", "rs2kv", "rs2")},
    "xT_low": {p: 4 for p in ("rs1", "rs2kv", "rs2")},
    "scores": {"mla": TB * HEADS, "mo": TB * HEADS},
    "row_max": {"mla": TB * HEADS, "mo": TB * HEADS},
    "exps": {"mla": TB * HEADS, "mo": TB * HEADS},
    "probs": {"mla": TB * HEADS, "mo": TB * HEADS},
    "o_high": {"mla": HEADS, "mo": HEADS},
    "o_low": {"mla": HEADS, "mo": HEADS},
}


def nth(signal, phase, i=0):
    count = 0
    if SIGNALS[signal].get("ln3") == 2 * TB:
        phase, i = {"ln3": ("ln3", 2 * i), "rs1": ("ln3", 2 * i + 1)}.get(phase, (phase, i))
    for p, n in SIGNALS[signal].items():
        if p == phase:
            return count + i + 1
        count += n
    raise KeyError((signal, phase))


COL_WIDTHS = {"c": KT, "mod_b": 2 * NMOD, "norm_g0": KT, "norm_g1": KT, "kv_g": KT,
              "ln0_g": KT, "ln0_b": KT, "ln1_g": KT, "ln1_b": KT, "ln2_g": KT, "ln2_b": KT,
              "sc_w": 3 * KT, "rg_w": 4 * KT, "rg_cb": KT, "rg_ba": KT, "rg_bx": KT, "lam": KT,
              "g_q": QT, "g_kv": CT}
COL = {}
for _n, _w in COL_WIDTHS.items():
    COL[_n] = sum(COL_WIDTHS[k] for k in COL)
NCOL = sum(COL_WIDTHS.values())
MOD = {name: KT * n for n, name in enumerate(["shift0", "scale0", "gate0", "shift1", "scale1", "gate1",
                                              "kv_shift", "kv_scale"])}


def build(nc, weights, x_in, cols_in, consts_in, rows_in, out):
    with ExitStack() as ctx:
        def sb(name, shape, dt=F32):
            return ctx.enter_context(nc.sbuf_tensor(name, shape, dt))

        raw = sb("raw", [P, RAW, PIECE])
        w_high = sb("w_high", [P, RING, PIECE], F32R)
        w_low = sb("w_low", [P, RING, PIECE], F32R)
        x = sb("x", [P, TB, D])
        z = sb("z", [P, TB, D])
        xT_h = sb("xT_h", [P, KT, SEQ], F32R)
        xT_l = sb("xT_l", [P, KT, SEQ], F32R)
        stage = sb("stage", [P, 2, 512])
        rows = sb("rows", [P, 2, D])
        consts = sb("consts", [P, 2 * P + 2 * SEQ])
        ones = sb("ones", [P, P])
        cols = sb("cols", [P, NCOL])
        modcol = sb("modcol", [P, 2 * NMOD])
        macc = sb("macc", [P, 2, SEQ])
        buf_a = sb("buf_a", [P, 2, 512])
        buf_b = sb("buf_b", [P, 2, 512])
        hT_h = sb("hT_h", [P, HRING * GT, SEQ], F32R)
        hT_l = sb("hT_l", [P, HRING * GT, SEQ], F32R)
        kT = sb("kT", [P, KT, SEQ])
        area = sb("area", [P, KT, SEQ])
        small = sb("small", [P, 77])

        ident, tri = consts[:, 0:P], consts[:, P:2 * P]
        cosT, sinT = consts[:, 2 * P:2 * P + SEQ], consts[:, 2 * P + SEQ:]
        flat = lambda t: t[:, :, :].rearrange("p a b -> p (a b)")
        kT_f, area_f = flat(kT), flat(area)
        stats = small[:, 0:48].rearrange("p (b n) -> p b n", b=2 * TB)
        mv = small[:, 48:56].rearrange("p (b n) -> p b n", b=2 * TB)
        ve = small[:, 56:60]
        rstd = small[:, 60:64]
        minus_half = small[:, 64:65]
        nmx, rsum, rinv = (small[:, 65 + 4 * n:69 + 4 * n] for n in range(3))
        cs = sb("cs", [P, KT])
        cth = sb("cth", [P, KT])
        prm = sb("prm", [P, 12, KT])
        A0, A1, AK, HBA, HBX, C4 = (prm[:, n, :] for n in range(6))

        def col(name, n=0):
            return cols[:, COL[name] + n:COL[name] + n + 1]

        def colrange(name, n=KT, start=0):
            return cols[:, COL[name] + start:COL[name] + start + n]

        def mcol(name, n):
            return modcol[:, MOD[name] + n:MOD[name] + n + 1]

        def mrange(name):
            return modcol[:, MOD[name]:MOD[name] + KT]

        Y = [[ctx.enter_context(nc.psum_tensor(f"Y{b}{h}", [P, 512], F32)) for h in range(2)] for b in range(TB)]
        bank = [ctx.enter_context(nc.psum_tensor(f"bank{n}", [P, 512], F32)) for n in range(PBANKS)]
        mbank = ctx.enter_context(nc.psum_tensor("mbank", [P, 512], F32))

        def mod_acc(m):
            return macc if m % 2 == 0 else stage[:, 1, :].rearrange("p (k s) -> p k s", k=2)

        def tok(b):
            return slice(b * P, (b + 1) * P)

        def sem(name):
            return ctx.enter_context(nc.semaphore(name))

        raw_in = [sem(f"raw_in{n}") for n in range(RAW)]
        w_high_ready = sem("w_high_ready")
        raw_done = sem("raw_done")
        product = sem("product")
        summed = sem("summed")
        evacuated = [sem(f"evacuated{n}") for n in range(PBANKS)]
        latent = sem("latent")
        mod_summed, mod_read = sem("mod_summed"), sem("mod_read")
        S = {name: sem(name) for name in SIGNALS}
        relu, hidden_high, hidden_low = S["relu"], S["hidden_high"], S["hidden_low"]
        x_in_done, consts_in_done, cols_in_done = sem("x_in_done"), sem("consts_in_done"), sem("cols_in_done")
        gain_in, shift_in = sem("gain_in"), sem("shift_in")
        ones_ready, c_tanh, lam_exp_in, lam_exp = sem("ones_ready"), sem("c_tanh"), sem("lam_exp_in"), sem("lam_exp")
        prm_ready, diag_ready = sem("prm_ready"), sem("diag_ready")
        lora_ready, lora_high, lora_low, rope_ready = sem("lora_ready"), sem("lora_high"), sem("lora_low"), sem("rope_ready")
        conv_ready, uc_high, uc_low = sem("conv_ready"), sem("uc_high"), sem("uc_low")
        gate_tanh, decay_ready, ratio_ready, root_ready = sem("gate_tanh"), sem("decay_ready"), sem("ratio_ready"), sem("root_ready")
        square_ready, rg_hidden = sem("square_ready"), sem("rg_hidden")
        act_chain, dve_chain, pool_chain = sem("act_chain"), sem("dve_chain"), sem("pool_chain")
        out_ready, out_done = sem("out_ready"), sem("out_done")

        def bank_of(*key):
            return bank[UN[key] % PBANKS]

        def await_product(eng, *key):
            eng.wait_ge(product, UN[key] + 1)

        def await_evacuated(eng, *key):
            eng.wait_ge(evacuated[UN[key] % PBANKS], UN[key] // PBANKS + 1)

        def evacuates(*key):
            return evacuated[UN[key] % PBANKS]

        def await_piece_used(eng, n):
            phase, kind, i = PIECES[n][0]
            if kind == "down":
                eng.wait_ge(summed, DN[phase, i, TB - 1] + 1)
            elif kind in ("dq", "dkv"):
                eng.wait_ge(latent, 2 * TB if kind == "dkv" else 2 * TB - 1)
            else:
                eng.wait_ge(product, UN[last_unit(phase, kind, i)] + 1)

        def hslot(phase, g):
            return GT * (g % (2 if phase == "rg" else HRING))

        def head_tiles(phase, h):
            if phase == "mo" and h < GT * HRING:
                return hT_h, hT_l, h
            return xT_h, xT_l, h % (GT * HRING) if phase == "mo" else h

        area_v = area_f.rearrange("p (b n) -> p b n", b=TB)
        q_all = flat(rows).rearrange("p (h s) -> p h s", s=SEQ)

        def q_tile(phase, h):
            return q_all[:, h if phase == "mla" else h % (2 * GT), :]

        def o_gate(h):
            return q_all[:, 2 * GT + h % (2 * GT), :]

        block = ctx.enter_context(nc.Block())

        @block.sync
        def _(sp):
            def load_row(slot, which, semaphore):
                sp.dma_start(rows[:, slot, :], rows_in[which, :].partition_broadcast(P)).then_inc(semaphore, 16)

            sp.dma_start(x[:, :, :], x_in.rearrange("(b p) d -> p b d", p=P)).then_inc(x_in_done, 16)
            sp.dma_start(consts[:, :], consts_in).then_inc(consts_in_done, 16)
            sp.dma_start(cols[:, :], cols_in).then_inc(cols_in_done, 16)
            start = 0
            for s, (kind, n) in enumerate(STREAM):
                if s >= RAW:
                    sp.wait_ge(raw_done, s - RAW + 1)
                src = weights[start:start + P * WIDTH[s]].rearrange("(p n) -> p n", p=P)
                sp.dma_start(raw[:, s % RAW, 0:WIDTH[s]], src).then_inc(raw_in[s % RAW], 16)
                start += P * WIDTH[s]
                key = PIECES[n][0] if kind == "w" else None
                which = {("sc", "down", 0): 0, ("ff0", "up", 8): 1, ("ff1", "up", 0): 2, ("ff1", "up", 8): 3}.get(key)
                if which is not None:
                    if which in (1, 3):
                        sp.wait_ge(S["norm_ready"], nth("norm_ready", f"ln{which - 1}", TB - 1))
                    if which == 2:
                        sp.wait_ge(S["scores"], nth("scores", "mla", TB * HEADS - 1))
                    load_row(0, 2 * which, gain_in)
                    load_row(1, 2 * which + 1, shift_in)
            await_evacuated(sp, "mo", "O", HEADS - 1)
            load_row(1, 8, shift_in)
            for b in range(TB):
                sp.wait_ge(out_ready, b + 1)
                sp.dma_start(out[b * P:(b + 1) * P, :], z[:, b, :]).then_inc(out_done, 16)
            sp.wait_ge(out_done, 16 * TB)

        @block.tensor
        def _(pe):
            mm = nc.tensor.matmul
            issued = [0, 0]

            def open_unit(*key):
                u = UN[key]
                assert u == issued[0], (key, UNITS[issued[0]])
                issued[0] += 1
                if u >= PBANKS:
                    pe.wait_ge(evacuated[u % PBANKS], u // PBANKS)
                return bank[u % PBANKS]

            def await_piece(n):
                pe.wait_ge(raw_done, AT["w", n] + 1)

            def up_tile(dst, n, tile, kts, xh, xl):
                for kt in range(kts):
                    c = (tile * kts + kt) * P
                    high, low = w_high[:, n % RING, c:c + P], w_low[:, n % RING, c:c + P]
                    mm(dst, high, xh[:, kt, :], start=kt == 0, stop=False)
                    mm(dst, high, xl[:, kt, :], start=False, stop=False)
                    last = mm(dst, low, xh[:, kt, :], start=False, stop=kt == kts - 1)
                return last

            def up(n, key, tile0=0, kts=KT, xh=xT_h, xl=xT_l):
                dst = open_unit(*key)
                await_piece(n)
                up_tile(dst[:, 0:SEQ], n, tile0, kts, xh, xl)
                up_tile(dst[:, SEQ:], n, tile0 + 1, kts, xh, xl).then_inc(product, 1)

            def token_major(dst, n, kts, width, c0, stride, b, xh, xl, first, final):
                for kt in range(kts):
                    c = kt * stride + c0
                    high, low = w_high[:, n % RING, c:c + width], w_low[:, n % RING, c:c + width]
                    mm(dst, xh[:, kt, tok(b)], high, start=first and kt == 0, stop=False)
                    mm(dst, xh[:, kt, tok(b)], low, start=False, stop=False)
                    last = mm(dst, xl[:, kt, tok(b)], high, start=False, stop=final and kt == kts - 1)
                return last

            def across(n, key, kts, width, c0=0, stride=None, xh=xT_h, xl=xT_l, blocks=range(TB)):
                dst = open_unit(*key)
                await_piece(n)
                for i, b in enumerate(blocks):
                    last = token_major(dst[:, i * width:(i + 1) * width], n, kts, width, c0, stride or width, b, xh, xl, True, True)
                last.then_inc(product, 1)

            def down(phase, g, b, th=hT_h, tl=hT_l):
                assert DN[phase, g, b] == issued[1]
                issued[1] += 1
                n = PI[phase, "down", g]
                if th is hT_h:
                    t0 = hslot(phase, g)
                    pe.wait_ge(hidden_low, nth("hidden_low", phase, g))
                else:
                    pe.wait_ge(S["o_low"], nth("o_low", phase, GT * g + GT - 1))
                    th, tl, t0 = head_tiles(phase, GT * g)
                if g == 0:
                    phases = list(GROUPS)
                    if phase != phases[0]:
                        pe.wait_ge(S["y_read"], nth("y_read", phases[phases.index(phase) - 1], b))
                await_piece(n)
                for t in range(GT):
                    first, final = g == 0 and t == 0, g == GROUPS[phase] - 1 and t == GT - 1
                    high = [w_high[:, n % RING, t * D + h * 512:t * D + (h + 1) * 512] for h in range(2)]
                    low = [w_low[:, n % RING, t * D + h * 512:t * D + (h + 1) * 512] for h in range(2)]
                    for h in range(2):
                        mm(Y[b][h][:, :], th[:, t0 + t, tok(b)], high[h], start=first, stop=False)
                        mm(Y[b][h][:, :], th[:, t0 + t, tok(b)], low[h], start=False, stop=False)
                    for h in range(2):
                        last = mm(Y[b][h][:, :], tl[:, t0 + t, tok(b)], high[h], start=False, stop=final)
                last.then_inc(summed, 1)

            def tail(phase, th=hT_h, tl=hT_l):
                for b in range(TB):
                    for g in (GROUPS[phase] - 2, GROUPS[phase] - 1):
                        down(phase, g, b, th, tl)

            def transposes(name, src, signal=None, blocks=range(TB)):
                for b in blocks:
                    if signal:
                        pe.wait_ge(S["norm_ready"], nth("norm_ready", signal, b))
                    for q in range(2):
                        dst = open_unit(name, b, q)
                        for i in range(4):
                            kt = 4 * q + i
                            last = nc.tensor.transpose(dst[:, i * P:(i + 1) * P], src[:, b, kt * P:(kt + 1) * P], ident)
                        last.then_inc(product, 1)

            def await_xT(phase, b=TB - 1):
                if phase[:2] == "rs":
                    pe.wait_ge(S["xT_low"], nth("xT_low", phase, 2 * b + 1))
                else:
                    for q in range(2):
                        await_evacuated(pe, phase, b, q)

            def mod_sums(m):
                pe.wait_ge(raw_done, AT["mod", m] + 1)
                if m:
                    pe.wait_ge(mod_read, m)
                for i in range(2):
                    for k in range(2):
                        last = mm(mbank[:, i:i + 1], mod_acc(m)[:, k, i * P:(i + 1) * P], ones[:, 0:1], start=k == 0, stop=k == 1)
                last.then_inc(mod_summed, 1)

            def feed_forward(phase, m0):
                for g in range(FFG):
                    mod_sums(m0 + g)
                    up(PI[phase, "up", g], (phase, g))
                    if 0 < g < FFG - 1:
                        for b in range(TB):
                            down(phase, g - 1, b)
                tail(phase)

            def gate_rows(layer):
                for n in range(2):
                    dst = open_unit("gate", layer, n)
                    pe.wait_ge(diag_ready, 2 * layer + n + 1)
                    diag = area_f if layer == 0 else kT_f
                    mm(dst[:, :], ones[:, :], diag[:, n * 512:(n + 1) * 512], start=True, stop=True).then_inc(product, 1)

            def scores(phase, h):
                q = q_tile(phase, h)
                for b in range(TB):
                    keys = (b + 1) * P
                    dst, mla = Y[b][h % 2], phase == "mla"
                    last = mm(dst[:, 0:keys], q[:, tok(b)], kT[:, h, 0:keys], start=True, stop=not mla)
                    if mla:
                        r = slice(ROPE * (h % 2), ROPE * (h % 2 + 1))
                        last = mm(dst[:, 0:keys], area[r, h // 2, tok(b)], area[r, 4, 0:keys], start=False, stop=True)
                    last.then_inc(S["scores"], 1)

            def values(phase, heads):
                v = z if phase == "mla" else area_v
                for h in heads:
                    dst = open_unit(phase, "PT", h)
                    pe.wait_ge(S["probs"], nth("probs", phase, TB * h + 1))
                    p = buf_a[:, h % 2, :]
                    for i, (b, kb) in enumerate([(0, 0), (1, 0), (1, 1)]):
                        last = nc.tensor.transpose(dst[:, i * P:(i + 1) * P],
                                                   p[:, b * SEQ + kb * P:b * SEQ + (kb + 1) * P], ident)
                    last.then_inc(product, 1)
                for h in heads:
                    dst = open_unit(phase, "O", h)
                    await_evacuated(pe, phase, "PT", h)
                    pT = buf_b[:, h % 2, :]
                    mm(dst[:, 0:SEQ], v[:, 0, h * P:(h + 1) * P], pT[:, 0:SEQ], start=True, stop=False)
                    mm(dst[:, P:SEQ], v[:, 1, h * P:(h + 1) * P], pT[:, SEQ:SEQ + P], start=False, stop=True).then_inc(product, 1)

            def attention(phase, project, await_q):
                for g in range(MXG + 1):
                    if g:
                        await_q(g - 1)
                        for h in (GT * g - 2, GT * g - 1):
                            scores(phase, h)
                    if g < MXG:
                        project(g)
                    if g:
                        values(phase, (GT * g - 2, GT * g - 1))

            pe.wait_ge(consts_in_done, 16)
            pe.wait_ge(x_in_done, 16)
            transposes("init", x)
            for b in range(TB):
                for q in range(2):
                    await_evacuated(pe, "init", b, q)
            for g in range(MXG):
                for kind in "ChB":
                    up(PI["sc", kind, g], ("sc", kind, g))
                if 0 < g < MXG - 1:
                    for b in range(TB):
                        down("sc", g - 1, b)
            tail("sc")

            transposes("ln0", x, "ln0")
            await_xT("ln0", 0)
            await_xT("ln0")
            pe.wait_ge(ones_ready, 1)
            feed_forward("ff0", 0)

            for b in range(TB):
                transposes("ln1", x, "ln1", [b])
                await_xT("ln1", b)
                pe.wait_ge(S["y_read"], nth("y_read", "ff0", b))
                for n in range(2):
                    i = PI["mla", "dq", n]
                    await_piece(i)
                    last = token_major(Y[b][0][:, 0:Q_LORA], i, KT // 2, Q_LORA, 0, Q_LORA, b, xT_h[:, 4 * n:4 * n + 4, :],
                                       xT_l[:, 4 * n:4 * n + 4, :], n == 0, n == 1)
                last.then_inc(latent, 1)
                i = PI["mla", "dkv", 0]
                await_piece(i)
                token_major(Y[b][1][:, 0:KV_LORA], i, KT, KV_LORA, 0, KV_LORA, b, xT_h, xT_l, True, True).then_inc(latent, 1)
            up(PI["mla", "kpe", 0], ("mla", "kpe"))
            cqn = flat(buf_a)[:, 0:TB * Q_LORA].rearrange("p (b n) -> p b n", b=TB)
            ckvn = buf_b[:, 0, :].rearrange("p (b n) -> p b n", b=TB)
            for b in range(TB):
                dst = open_unit("mla", "tq", b)
                pe.wait_ge(lora_ready, 2 * b + 1)
                for kt in range(QT):
                    last = nc.tensor.transpose(dst[:, kt * P:(kt + 1) * P], cqn[:, b, kt * P:(kt + 1) * P], ident)
                last.then_inc(product, 1)
            dst = open_unit("mla", "tkv")
            pe.wait_ge(lora_ready, 2 * TB)
            for kt in range(CT):
                for b in range(TB):
                    last = nc.tensor.transpose(dst[:, (kt * TB + b) * P:(kt * TB + b + 1) * P],
                                               ckvn[:, b, kt * P:(kt + 1) * P], ident)
            last.then_inc(product, 1)
            pe.wait_ge(lora_low, 3)
            ckv = (hT_h[:, QT:QT + CT, :], hT_l[:, QT:QT + CT, :])
            for n in range(4):
                up(PI["mla", "uk", 0], ("mla", "k", n), 2 * n, CT, *ckv)
            for b in range(TB):
                for n in range(2):
                    across(PI["mla", "uv", 0], ("mla", "v", b, n), CT, 512, n * 512, D, *ckv, blocks=[b])

            def project(g):
                for i, kind in enumerate(("qn", "qp")):
                    up(PI["mla", "q", g], ("mla", kind, g), GT * i, QT, hT_h, hT_l)

            def await_q(g):
                await_evacuated(pe, "mla", "qn", g)
                pe.wait_ge(rope_ready, g + 2)
                if g == 0:
                    for b, n in ((0, 1), (1, 0), (1, 1)):
                        await_evacuated(pe, "mla", "v", b, n)

            attention("mla", project, await_q)
            for g in range(MXG - 2):
                for b in range(TB):
                    down("mla", g, b, xT_h, xT_l)
            tail("mla", xT_h, xT_l)

            transposes("ln2", x, "ln2")
            await_xT("ln2")
            feed_forward("ff1", FFG)

            transposes("rs1", z, "rs1")
            gate_rows(0)
            await_xT("rs1")
            for g in range(MXG + 2):
                if g < MXG:
                    up(PI["rg", "u", g], ("rg", "u", g))
                    up(PI["rg", "g", g], ("rg", "g", g))
                if 0 <= g - 1 < MXG:
                    pe.wait_ge(uc_low, g)
                    for i, kind in enumerate("ax"):
                        up(PI["rg", "ax", g - 1], ("rg", kind, g - 1), GT * i, GT, hT_h[:, 4:6, :], hT_l[:, 4:6, :])
                if 2 <= g < MXG:
                    for b in range(TB):
                        down("rg", g - 2, b)
            tail("rg")

            transposes("rs2kv", z, "rs2")
            await_xT("rs2kv")
            for g in range(MXG):
                up(PI["mo", "k", g], ("mo", "k", g))
            for g in range(MXG):
                across(PI["mo", "v", g], ("mo", "v", g), KT, 2 * P)
            transposes("rs2", z)
            await_xT("rs2")

            def project_moba(g):
                for kind in "qg":
                    up(PI["mo", kind, g], ("mo", kind, g))

            def await_q_moba(g):
                await_evacuated(pe, "mo", "q", g)
                if g == 0:
                    for i in (1, 2, 3):
                        await_evacuated(pe, "mo", "v", i)

            attention("mo", project_moba, await_q_moba)
            gate_rows(1)
            for g in range(MXG - 2):
                for b in range(TB):
                    down("mo", g, b, xT_h, xT_l)
            tail("mo", xT_h, xT_l)
            assert issued == [len(UNITS), len(DN)]

        @block.gpsimd
        def _(pool):
            chain = [0]

            def link(instruction):
                chain[0] += 1
                instruction.then_inc(pool_chain, 1)
                pool.wait_ge(pool_chain, chain[0])

            nc.gpsimd.memset(ones[:, :], 1.0).then_inc(ones_ready, 1)
            link(nc.gpsimd.memset(minus_half, -0.5))

            def roots(*names, blocks=TB):
                for b, name in [(b, name) for b in range(blocks) for name in names]:
                    pool.wait_ge(S["var_ready"], nth("var_ready", name, b))
                    nc.gpsimd.tensor_tensor(rstd[:, b:b + 1], ve[:, b:b + 1], minus_half, ALU.pow).then_inc(S["rstd_ready"], 1)

            def diagonals(layer):
                dst = area_f if layer == 0 else kT_f
                for n in range(2):
                    for i in range(4):
                        t = 4 * n + i
                        last = nc.gpsimd.tensor_scalar(dst[:, t * P:(t + 1) * P], ident, mcol(f"gate{layer}", t), None, ALU.mult)
                    last.then_inc(diag_ready, 1)

            pool.wait_ge(consts_in_done, 16)
            roots("ln0")
            roots("ln1")
            roots("latent", blocks=2 * TB)
            roots("ln2")
            roots("ln3", "rs1")
            pool.wait_ge(mod_read, NMOD)
            diagonals(0)
            roots("rs2")
            pool.wait_ge(S["scores"], nth("scores", "mo", TB * HEADS - 1))
            diagonals(1)
            roots("rs3")

        @block.scalar
        def _(act):
            done = [0]
            chain = [0]

            def link(instruction):
                chain[0] += 1
                instruction.then_inc(act_chain, 1)
                act.wait_ge(act_chain, chain[0])

            def split_ahead(key):
                while done[0] < len(PIECES) and done[0] <= PI[key] + AHEAD:
                    n = done[0]
                    s = AT["w", n]
                    act.wait_ge(raw_in[s % RAW], 16 * (s // RAW + 1))
                    if n >= RING:
                        await_piece_used(act, n - RING)
                    nc.scalar.copy(w_high[:, n % RING, 0:COLS[n]], raw[:, s % RAW, 0:COLS[n]]).then_inc(w_high_ready, 1)
                    done[0] += 1

            def hidden_high_of(phase, g):
                back = 2 if phase == "rg" else HRING
                if g >= back:
                    act.wait_ge(summed, DN[phase, g - back, TB - 1] + 1)
                t0 = hslot(phase, g)
                src = buf_b[:, g % 2, :].rearrange("p (t s) -> p t s", t=GT)
                nc.scalar.copy(hT_h[:, t0:t0 + GT, :], src).then_inc(hidden_high, 1)

            def norm_transposed(name):
                for b in range(TB):
                    for q in range(2):
                        if name[:2] == "rs":
                            await_evacuated(act, name, b, q)
                            src = stage[:, q, :]
                        else:
                            await_product(act, name, b, q)
                            src = bank_of(name, b, q)[:, :]
                        nc.scalar.copy(xT_h[:, 4 * q:4 * q + 4, tok(b)], src.rearrange("p (t s) -> p t s", t=4)).then_inc(S["xT_high"], 1)

            def feed_forward(phase):
                for g in range(FFG):
                    split_ahead((phase, "up", g))
                    if g:
                        split_ahead((phase, "down", g - 1))
                    await_product(act, phase, g)
                    if g >= 2:
                        await_evacuated(act, phase, g - 2)
                    nc.scalar.activation(buf_a[:, g % 2, :], bank_of(phase, g)[:, :], ACT.Relu).then_inc(relu, 1)
                    await_evacuated(act, phase, g)
                    hidden_high_of(phase, g)

            def exponentials(phase, h):
                for b in range(TB):
                    keys, c = (b + 1) * P, TB * (h % 2) + b
                    act.wait_ge(S["row_max"], nth("row_max", phase, TB * h + b))
                    if h >= 2:
                        await_product(act, phase, "PT", h - 2)
                    nc.scalar.activation(buf_a[:, h % 2, b * SEQ:b * SEQ + keys], Y[b][h % 2][:, 0:keys], ACT.Exp,
                                         bias=nmx[:, c:c + 1], accum_out=rsum[:, c:c + 1]).then_inc(S["exps"], 1)

            def outputs_high(phase, heads):
                for h in heads:
                    await_product(act, phase, "PT", h)
                    if h >= 2:
                        await_product(act, phase, "O", h - 2)
                    nc.scalar.copy(buf_b[:, h % 2, 0:3 * P], bank_of(phase, "PT", h)[:, 0:3 * P])\
                        .then_inc(evacuates(phase, "PT", h), 1)
                for h in heads:
                    await_evacuated(act, phase, "O", h)
                    th, _, t = head_tiles(phase, h)
                    nc.scalar.copy(th[:, t, :], stage[:, h % 2, 0:SEQ]).then_inc(S["o_high"], 1)

            act.wait_ge(cols_in_done, 16)
            nc.scalar.activation(cth[:, :], colrange("c"), ACT.Tanh, scale=0.5).then_inc(c_tanh, 1)
            act.wait_ge(lam_exp_in, 1)
            nc.scalar.activation(prm[:, 7, :], prm[:, 6, :], ACT.Exp, scale=-1.0).then_inc(lam_exp, 1)

            for b in range(TB):
                for q in range(2):
                    await_product(act, "init", b, q)
                    src = bank_of("init", b, q)[:, :].rearrange("p (t s) -> p t s", t=4)
                    nc.scalar.copy(xT_h[:, 4 * q:4 * q + 4, tok(b)], src).then_inc(S["xT_high"], 1)
            for g in range(MXG):
                split_ahead(("sc", "C", g))
                await_product(act, "sc", "C", g)
                if g >= 2:
                    await_evacuated(act, "sc", "h", g - 2)
                nc.scalar.copy(kT_f[:, (g % 2) * 512:(g % 2 + 1) * 512], bank_of("sc", "C", g)[:, :])\
                    .then_inc(evacuates("sc", "C", g), 1)
                split_ahead(("sc", "h", g))
                split_ahead(("sc", "B", g))
                await_evacuated(act, "sc", "B", g)
                hidden_high_of("sc", g)
            split_ahead(("sc", "down", MXG - 1))
            norm_transposed("ln0")
            feed_forward("ff0")
            split_ahead(("ff0", "down", FFG - 1))
            norm_transposed("ln1")

            split_ahead(("mla", "dkv", 0))
            for b in range(TB):
                await_evacuated(act, "mla", "tq", b)
                src = stage[:, b, 0:QT * P].rearrange("p (t s) -> p t s", t=QT)
                nc.scalar.copy(hT_h[:, 0:QT, tok(b)], src).then_inc(lora_high, 1)
            await_evacuated(act, "mla", "tkv")
            act.wait_ge(lora_low, 1)
            nc.scalar.copy(hT_h[:, QT:QT + CT, :], stage[:, 0, :].rearrange("p (t s) -> p t s", t=CT)).then_inc(lora_high, 1)
            split_ahead(("mla", "kpe", 0))
            for n in range(4):
                await_product(act, "mla", "k", n)
                nc.scalar.copy(kT[:, 2 * n:2 * n + 2, :], bank_of("mla", "k", n)[:, :].rearrange("p (t s) -> p t s", t=2))\
                    .then_inc(evacuates("mla", "k", n), 1)
            split_ahead(("mla", "uk", 0))
            for b in range(TB):
                for n in range(2):
                    await_product(act, "mla", "v", b, n)
                    nc.scalar.copy(z[:, b, n * 512:(n + 1) * 512], bank_of("mla", "v", b, n)[:, :])\
                        .then_inc(evacuates("mla", "v", b, n), 1)
            split_ahead(("mla", "uv", 0))
            for g in range(MXG + 1):
                heads = (GT * g - 2, GT * g - 1)
                if g:
                    for h in heads:
                        exponentials("mla", h)
                if g < MXG:
                    await_product(act, "mla", "qn", g)
                    nc.scalar.mul(q_all[:, GT * g:GT * (g + 1), :], bank_of("mla", "qn", g)[:, :].rearrange("p (t s) -> p t s", t=2),
                                  float(NOPE + ROPE) ** -0.5).then_inc(evacuates("mla", "qn", g), 1)
                    split_ahead(("mla", "q", g))
                if g:
                    outputs_high("mla", heads)
            for g in range(MXG):
                split_ahead(("mla", "down", g))
            norm_transposed("ln2")
            feed_forward("ff1")
            split_ahead(("ff1", "down", FFG - 1))
            norm_transposed("rs1")

            act.wait_ge(S["norm_ready"], nth("norm_ready", "ln3", TB - 1))
            for n in range(2):
                await_product(act, "gate", 0, n)
                nc.scalar.copy(rows[:, 0, n * 512:(n + 1) * 512], bank_of("gate", 0, n)[:, :]).then_inc(evacuates("gate", 0, n), 1)
            uT = flat(buf_a)[:, 0:GT * (SEQ + 3)].rearrange("p (t s) -> p t s", t=GT)
            thg = rows[:, 1, 0:512]
            for g in range(MXG + 1):
                if g < MXG:
                    split_ahead(("rg", "u", g))
                    await_product(act, "rg", "u", g)
                    act.wait_ge(conv_ready, g + 1)
                    nc.scalar.copy(uT[:, :, 3:], bank_of("rg", "u", g)[:, :].rearrange("p (t s) -> p t s", t=GT))\
                        .then_inc(evacuates("rg", "u", g), 1)
                    act.wait_ge(conv_ready, g + 2)
                    if g:
                        await_product(act, "rg", "x", g - 1)
                    nc.scalar.copy(hT_h[:, 4:6, :], kT[:, 2 * (g % 2):2 * (g % 2) + 2, :]).then_inc(uc_high, 1)
                    split_ahead(("rg", "g", g))
                    await_product(act, "rg", "g", g)
                    if g:
                        await_evacuated(act, "rg", "g", g - 1)
                    nc.scalar.activation(thg, bank_of("rg", "g", g)[:, :], ACT.Tanh, scale=0.5).then_inc(gate_tanh, 1)
                if g:
                    i = g - 1
                    split_ahead(("rg", "ax", i))
                    if i:
                        act.wait_ge(rg_hidden, i)
                    for n, (kind, half_bias) in enumerate((("a", HBA), ("x", HBX))):
                        await_product(act, "rg", kind, i)
                        for t in range(GT):
                            kt = GT * i + t
                            last = nc.scalar.activation(area_f[:, n * 512 + t * SEQ:n * 512 + (t + 1) * SEQ],
                                                        bank_of("rg", kind, i)[:, t * SEQ:(t + 1) * SEQ], ACT.Tanh,
                                                        scale=0.5, bias=half_bias[:, kt:kt + 1])
                        last.then_inc(evacuates("rg", kind, i), 1)
                    await_evacuated(act, "rg", "a", i)
                    for t in range(GT):
                        kt = GT * i + t
                        c4, src = C4[:, kt:kt + 1], area_f[:, t * SEQ:(t + 1) * SEQ]
                        nc.scalar.activation(stage[:, 0, t * SEQ:(t + 1) * SEQ], src, ACT.Exp, scale=c4, bias=c4)
                        last = nc.scalar.activation(area_f[:, 1024 + t * SEQ:1024 + (t + 1) * SEQ], src, ACT.Tanh, scale=c4, bias=c4)
                    last.then_inc(decay_ready, 1)
                    act.wait_ge(decay_ready, i + 1)
                    nc.scalar.activation(area_f[:, 1536:2048], stage[:, 0, :], ACT.Square).then_inc(square_ready, 1)
                    act.wait_ge(ratio_ready, i + 1)
                    nc.scalar.activation(area_f[:, 1024:1536], stage[:, 1, :], ACT.Sqrt, scale=-0.25).then_inc(root_ready, 1)
                    act.wait_ge(rg_hidden, i + 1)
                    hidden_high_of("rg", i)
            for g in range(MXG):
                split_ahead(("rg", "down", g))

            norm_transposed("rs2kv")
            for g in range(MXG):
                split_ahead(("mo", "k", g))
                await_product(act, "mo", "k", g)
                nc.scalar.copy(kT[:, 2 * g:2 * g + 2, :], bank_of("mo", "k", g)[:, :].rearrange("p (t s) -> p t s", t=2))\
                    .then_inc(evacuates("mo", "k", g), 1)
            for g in range(MXG):
                split_ahead(("mo", "v", g))
                await_product(act, "mo", "v", g)
                nc.scalar.copy(area_v[:, :, g * SEQ:(g + 1) * SEQ], bank_of("mo", "v", g)[:, :].rearrange("p (b s) -> p b s", b=TB))\
                    .then_inc(evacuates("mo", "v", g), 1)
            norm_transposed("rs2")
            for g in range(MXG + 1):
                heads = (GT * g - 2, GT * g - 1)
                if g:
                    for h in heads:
                        exponentials("mo", h)
                if g < MXG:
                    split_ahead(("mo", "q", g))
                    await_product(act, "mo", "q", g)
                    if g == 0:
                        act.wait_ge(S["y_read"], nth("y_read", "rg", TB - 1))
                    t0 = GT * (g % 2)
                    nc.scalar.mul(q_all[:, t0:t0 + GT, :], bank_of("mo", "q", g)[:, :].rearrange("p (t s) -> p t s", t=2),
                                  float(P) ** -0.5).then_inc(evacuates("mo", "q", g), 1)
                    split_ahead(("mo", "g", g))
                    await_product(act, "mo", "g", g)
                    if g:
                        await_evacuated(act, "mo", "g", g - 1)
                    nc.scalar.activation(stage[:, :, SEQ:], bank_of("mo", "g", g)[:, :].rearrange("p (t s) -> p t s", t=2),
                                         ACT.Tanh, scale=0.5).then_inc(gate_tanh, 1)
                if g:
                    outputs_high("mo", heads)
            split_ahead(("mo", "down", 0))
            for n in range(2):
                await_product(act, "gate", 1, n)
                nc.scalar.copy(rows[:, 0, n * 512:(n + 1) * 512], bank_of("gate", 1, n)[:, :]).then_inc(evacuates("gate", 1, n), 1)
            assert done[0] == len(PIECES)

        @block.vector
        def _(dve):
            chain = [0]
            done = [0]
            tt, ts, stt = nc.vector.tensor_tensor, nc.vector.tensor_scalar, nc.vector.scalar_tensor_tensor

            def link(instruction):
                chain[0] += 1
                instruction.then_inc(dve_chain, 1)
                dve.wait_ge(dve_chain, chain[0])

            def f32(ap):
                return ap.bitcast(F32)

            def split_ahead(key):
                stop = AT["w", min(PI[key] + AHEAD, len(PIECES) - 1)]
                while done[0] <= stop:
                    s = done[0]
                    kind, n = STREAM[s]
                    slot = raw[:, s % RAW, :]
                    if kind == "w":
                        dve.wait_ge(w_high_ready, n + 1)
                        tt(w_low[:, n % RING, 0:COLS[n]], slot[:, 0:COLS[n]], f32(w_high[:, n % RING, 0:COLS[n]]),
                           ALU.subtract).then_inc(raw_done, 1)
                    else:
                        dve.wait_ge(raw_in[s % RAW], 16 * (s // RAW + 1))
                        if n >= 2:
                            dve.wait_ge(mod_summed, n - 1)
                        accumulators = mod_acc(n)
                        first = chain[0]
                        for kt in range(KT):
                            acc, part = accumulators[:, kt % 2, :], slot[:, kt * SEQ:(kt + 1) * SEQ]
                            if kt < 2:
                                step = ts(acc, part, cs[:, kt:kt + 1], None, ALU.mult)
                            else:
                                dve.wait_ge(dve_chain, first + kt - 1)
                                step = stt(out=acc, in0=part, scalar=cs[:, kt:kt + 1], in1=acc, op0=ALU.mult, op1=ALU.add)
                            if kt < KT - 1:
                                step.then_inc(dve_chain, 1)
                                chain[0] += 1
                        step.then_inc(raw_done, 1)
                    done[0] += 1

            def read_mod(m):
                dve.wait_ge(mod_summed, m + 1)
                tt(modcol[:, 2 * m:2 * m + 2], mbank[:, 0:2], colrange("mod_b", 2, 2 * m), ALU.add).then_inc(mod_read, 1)

            def hidden_low_of(phase, g):
                dve.wait_ge(hidden_high, nth("hidden_high", phase, g))
                t0 = hslot(phase, g)
                src = buf_b[:, g % 2, :].rearrange("p (t s) -> p t s", t=GT)
                tt(hT_l[:, t0:t0 + GT, :], src, f32(hT_h[:, t0:t0 + GT, :]), ALU.subtract).then_inc(hidden_low, 1)

            def mean_square_or_variance(parts, b, name, rms):
                for i, part in enumerate(parts):
                    last = nc.vector.bn_stats(stats[:, b, 6 * i:6 * i + 6], part)
                link(last)
                link(nc.vector.bn_aggr(mv[:, b, :], stats[:, b, 0:6 * len(parts)]))
                if rms:
                    link(stt(out=ve[:, b:b + 1], in0=mv[:, b, 0:1], scalar=mv[:, b, 0:1], in1=mv[:, b, 1:2], op0=ALU.mult, op1=ALU.add))
                    ts(ve[:, b:b + 1], ve[:, b:b + 1], RMS_EPS, None, ALU.add).then_inc(S["var_ready"], 1)
                else:
                    ts(ve[:, b:b + 1], mv[:, b, 1:2], LN_EPS, None, ALU.add).then_inc(S["var_ready"], 1)

            def halves(t, b):
                return [t[:, b, 0:512], t[:, b, 512:1024]]

            def await_rstd(name, b):
                dve.wait_ge(S["rstd_ready"], nth("rstd_ready", name, b))

            def layer_norm(name, phase, b):
                dve.wait_ge(summed, DN[phase, GROUPS[phase] - 1, b] + 1)
                for h in range(2):
                    last = stt(out=z[:, b, h * 512:(h + 1) * 512], in0=x[:, b, h * 512:(h + 1) * 512], scalar=ALPHA,
                               in1=Y[b][h][:, :], op0=ALU.mult, op1=ALU.add)
                last.then_inc(S["y_read"], 1)
                dve.wait_ge(S["y_read"], nth("y_read", phase, b))
                mean_square_or_variance(halves(z, b), b, name, False)
                n = int(name[2])
                dve.wait_ge(gain_in, 16 * (n + 1))
                link(stt(out=z[:, b, :], in0=z[:, b, :], scalar=mv[:, b, 0:1], in1=rows[:, 0, :], op0=ALU.subtract, op1=ALU.mult))
                dve.wait_ge(shift_in, 16 * (n + 1))
                await_rstd(name, b)
                stt(out=x[:, b, :], in0=z[:, b, :], scalar=rstd[:, b:b + 1], in1=rows[:, 1, :], op0=ALU.mult, op1=ALU.add)\
                    .then_inc(S["norm_ready"], 1)

            def rms_norm(name, b):
                mean_square_or_variance(halves(x, b), b, name, True)
                await_rstd(name, b)
                ts(z[:, b, :], x[:, b, :], rstd[:, b:b + 1], None, ALU.mult).then_inc(S["norm_ready"], 1)

            def gated_residual(phase, layer, b):
                if b == 0:
                    for n in range(2):
                        await_evacuated(dve, "gate", layer, n)
                dve.wait_ge(summed, DN[phase, GROUPS[phase] - 1, b] + 1)
                for h in range(2):
                    last = tt(z[:, b, h * 512:(h + 1) * 512], Y[b][h][:, :], rows[:, 0, h * 512:(h + 1) * 512], ALU.mult)
                last.then_inc(S["y_read"], 1)
                dve.wait_ge(S["y_read"], nth("y_read", phase, b))
                link(tt(x[:, b, :], x[:, b, :], z[:, b, :], ALU.add))

            def split_transposed(name, b, gain, shift):
                for q in range(2):
                    await_product(dve, name, b, q)
                    src = bank_of(name, b, q)
                    for i in range(4):
                        kt = 4 * q + i
                        last = ts(stage[:, q, i * P:(i + 1) * P], src[:, i * P:(i + 1) * P], gain(kt), shift(kt), ALU.mult, ALU.add)
                    last.then_inc(evacuates(name, b, q), 1)
                for q in range(2):
                    dve.wait_ge(S["xT_high"], nth("xT_high", name, 2 * b + q))
                    tt(xT_l[:, 4 * q:4 * q + 4, tok(b)], stage[:, q, :].rearrange("p (t s) -> p t s", t=4),
                       f32(xT_h[:, 4 * q:4 * q + 4, tok(b)]), ALU.subtract).then_inc(S["xT_low"], 1)
                dve.wait_ge(S["xT_low"], nth("xT_low", name, 2 * b + 1))

            def low_transposed(name, b):
                for q in range(2):
                    dve.wait_ge(S["xT_high"], nth("xT_high", name, 2 * b + q))
                    tt(xT_l[:, 4 * q:4 * q + 4, tok(b)], bank_of(name, b, q)[:, :].rearrange("p (t s) -> p t s", t=4),
                       f32(xT_h[:, 4 * q:4 * q + 4, tok(b)]), ALU.subtract).then_inc(evacuates(name, b, q), 1)

            def ln_then_transpose(name, phase):
                for b in range(TB):
                    layer_norm(name, phase, b)
                    low_transposed(name, b)

            def feed_forward(phase, m0):
                for g in range(FFG):
                    split_ahead((phase, "up", g))
                    if g:
                        split_ahead((phase, "down", g - 1))
                    dve.wait_ge(relu, nth("relu", phase, g))
                    stt(out=buf_b[:, g % 2, :], in0=bank_of(phase, g)[:, :], scalar=0.0, in1=buf_a[:, g % 2, :],
                        op0=ALU.max, op1=ALU.mult).then_inc(evacuates(phase, g), 1)
                    read_mod(m0 + g)
                    hidden_low_of(phase, g)
                split_ahead((phase, "down", FFG - 1))

            def softmax(phase, heads):
                for h in heads:
                    for b in range(TB):
                        keys, c = (b + 1) * P, TB * (h % 2) + b
                        dve.wait_ge(S["scores"], nth("scores", phase, TB * h + b))
                        s = Y[b][h % 2]
                        if phase == "mla":
                            link(nc.vector.memset(s[0:64, keys - 64:keys], NEG_INF))
                        else:
                            link(tt(s[:, keys - P:keys], s[:, keys - P:keys], tri, ALU.add))
                        nc.vector.reduce_max(nmx[:, c:c + 1], s[:, 0:keys], AXX, negate=True).then_inc(S["row_max"], 1)
                for h in heads:
                    c = TB * (h % 2)
                    dve.wait_ge(S["exps"], nth("exps", phase, TB * h + TB - 1))
                    link(nc.vector.reciprocal(rinv[:, c:c + TB], rsum[:, c:c + TB]))
                    for b in range(TB):
                        p = buf_a[:, h % 2, b * SEQ:b * SEQ + (b + 1) * P]
                        ts(p, p, rinv[:, c + b:c + b + 1], None, ALU.mult).then_inc(S["probs"], 1)

            def outputs_low(phase, heads):
                for h in heads:
                    await_product(dve, phase, "O", h)
                    o, st = bank_of(phase, "O", h)[:, 0:SEQ], stage[:, h % 2, 0:SEQ]
                    if phase == "mla":
                        nc.vector.tensor_copy(st, o).then_inc(evacuates(phase, "O", h), 1)
                    else:
                        stt(out=st, in0=o, scalar=0.5, in1=o_gate(h), op0=ALU.mult, op1=ALU.mult)\
                            .then_inc(evacuates(phase, "O", h), 1)
                for h in heads:
                    th, tl, t = head_tiles(phase, h)
                    dve.wait_ge(S["o_high"], nth("o_high", phase, h))
                    tt(tl[:, t, :], stage[:, h % 2, 0:SEQ], f32(th[:, t, :]), ALU.subtract).then_inc(S["o_low"], 1)

            dve.wait_ge(cols_in_done, 16)
            lam, r2, s, d, poly, s2 = colrange("lam"), prm[:, 8, :], prm[:, 9, :], prm[:, 10, :], prm[:, 11, :], prm[:, 5, :]
            link(ts(r2, lam, -1.0, 0.0, ALU.mult, ALU.max))
            link(ts(prm[:, 7, :], lam, 0.0, None, ALU.max))
            tt(prm[:, 6, :], prm[:, 7, :], r2, ALU.add).then_inc(lam_exp_in, 1)
            ts(HBA, colrange("rg_ba"), 0.5, None, ALU.mult)
            link(ts(HBX, colrange("rg_bx"), 0.5, None, ALU.mult))
            dve.wait_ge(c_tanh, 1)
            link(stt(out=cs[:, :], in0=cth[:, :], scalar=1.0, in1=colrange("c"), op0=ALU.add, op1=ALU.mult))
            link(ts(cs[:, :], cs[:, :], 0.5, None, ALU.mult))
            dve.wait_ge(lam_exp, 1)
            e = prm[:, 7, :]
            link(ts(d, e, 2.0, None, ALU.add))
            link(nc.vector.reciprocal(d, d))
            link(tt(s, e, d, ALU.mult))
            link(tt(s2, s, s, ALU.mult))
            link(ts(poly, s2, 1.0 / 15, None, ALU.mult))
            for odd in (13, 11, 9, 7, 5, 3):
                link(stt(out=poly, in0=poly, scalar=1.0 / odd, in1=s2, op0=ALU.add, op1=ALU.mult))
            link(stt(out=poly, in0=poly, scalar=1.0, in1=s, op0=ALU.add, op1=ALU.mult))
            link(ts(r2, r2, -2.0 * RG_C / 4, None, ALU.mult))
            link(stt(out=C4, in0=poly, scalar=-RG_C, in1=r2, op0=ALU.mult, op1=ALU.add))

            for b in range(TB):
                for q in range(2):
                    dve.wait_ge(S["xT_high"], nth("xT_high", "init", 2 * b + q))
                    tt(xT_l[:, 4 * q:4 * q + 4, tok(b)], bank_of("init", b, q)[:, :].rearrange("p (t s) -> p t s", t=4),
                       f32(xT_h[:, 4 * q:4 * q + 4, tok(b)]), ALU.subtract).then_inc(evacuates("init", b, q), 1)

            ch = area_f[:, 0:GT * (SEQ + 2)].rearrange("p (t s) -> p t s", t=GT)
            conv = area_f[:, 1024:1536].rearrange("p (t s) -> p t s", t=GT)
            link(nc.vector.memset(ch[:, :, 0:2], 0.0))
            for g in range(MXG):
                split_ahead(("sc", "C", g))
                await_evacuated(dve, "sc", "C", g)
                await_product(dve, "sc", "h", g)
                tt(ch[:, :, 2:], bank_of("sc", "h", g)[:, :].rearrange("p (t s) -> p t s", t=GT),
                   kT_f[:, (g % 2) * 512:(g % 2 + 1) * 512].rearrange("p (t s) -> p t s", t=GT), ALU.mult)\
                    .then_inc(evacuates("sc", "h", g), 1)
                split_ahead(("sc", "h", g))
                await_evacuated(dve, "sc", "h", g)
                for t in range(GT):
                    last = ts(conv[:, t, :], ch[:, t, 2:2 + SEQ], col("sc_w", 2 * KT + GT * g + t), None, ALU.mult)
                link(last)
                for k in (1, 0):
                    for t in range(GT):
                        last = stt(out=conv[:, t, :], in0=ch[:, t, k:k + SEQ], scalar=col("sc_w", k * KT + GT * g + t),
                                   in1=conv[:, t, :], op0=ALU.mult, op1=ALU.add)
                    link(last)
                split_ahead(("sc", "B", g))
                await_product(dve, "sc", "B", g)
                tt(buf_b[:, g % 2, :], bank_of("sc", "B", g)[:, :], area_f[:, 1024:1536], ALU.mult).then_inc(evacuates("sc", "B", g), 1)
                hidden_low_of("sc", g)
            split_ahead(("sc", "down", MXG - 1))
            ln_then_transpose("ln0", "sc")
            feed_forward("ff0", 0)
            ln_then_transpose("ln1", "ff0")

            split_ahead(("mla", "dq", 0))
            cqn = flat(buf_a)[:, 0:TB * Q_LORA].rearrange("p (b n) -> p b n", b=TB)
            ckvn = buf_b[:, 0, :].rearrange("p (b n) -> p b n", b=TB)
            for b in range(TB):
                for i, (normed, width) in enumerate(((cqn, Q_LORA), (ckvn, KV_LORA))):
                    dve.wait_ge(latent, 2 * b + i + 1)
                    src = Y[b][i][:, 0:width]
                    mean_square_or_variance([src], 2 * b + i, "latent", True)
                    await_rstd("latent", 2 * b + i)
                    ts(normed[:, b, :], src, rstd[:, 2 * b + i:2 * b + i + 1], None, ALU.mult).then_inc(lora_ready, 1)
            split_ahead(("mla", "dkv", 0))

            def rope(n, *key):
                await_product(dve, *key)
                src = bank_of(*key)
                scale = float(NOPE + ROPE) ** -0.5 if n < 4 else 1.0
                stt(out=area[:, 5, :], in0=src[:, 0:SEQ], scalar=scale, in1=cosT, op0=ALU.mult, op1=ALU.mult)
                stt(out=area[:, 6, :], in0=src[:, SEQ:], scalar=scale, in1=sinT, op0=ALU.mult, op1=ALU.mult).then_inc(evacuates(*key), 1)
                await_evacuated(dve, *key)
                tt(area[:, n, :], area[:, 5, :], area[:, 6, :], ALU.add).then_inc(rope_ready, 1)

            rope(4, "mla", "kpe")
            for b in range(TB):
                await_product(dve, "mla", "tq", b)
                for kt in range(QT):
                    last = ts(stage[:, b, kt * P:(kt + 1) * P], bank_of("mla", "tq", b)[:, kt * P:(kt + 1) * P], col("g_q", kt), None, ALU.mult)
                last.then_inc(evacuates("mla", "tq", b), 1)
            for b in range(TB):
                dve.wait_ge(lora_high, b + 1)
                tt(hT_l[:, 0:QT, tok(b)], stage[:, b, 0:QT * P].rearrange("p (t s) -> p t s", t=QT),
                   f32(hT_h[:, 0:QT, tok(b)]), ALU.subtract).then_inc(lora_low, 1)
            dve.wait_ge(lora_low, 1)
            await_product(dve, "mla", "tkv")
            for kt in range(CT):
                last = ts(stage[:, 0, kt * SEQ:(kt + 1) * SEQ], bank_of("mla", "tkv")[:, kt * SEQ:(kt + 1) * SEQ], col("g_kv", kt), None, ALU.mult)
            last.then_inc(evacuates("mla", "tkv"), 1)
            dve.wait_ge(lora_high, 3)
            tt(hT_l[:, QT:QT + CT, :], stage[:, 0, :].rearrange("p (t s) -> p t s", t=CT),
               f32(hT_h[:, QT:QT + CT, :]), ALU.subtract).then_inc(lora_low, 1)
            for kind in ("kpe", "uk", "uv"):
                split_ahead(("mla", kind, 0))
            for g in range(MXG + 1):
                heads = (GT * g - 2, GT * g - 1)
                if g:
                    softmax("mla", heads)
                if g < MXG:
                    dve.wait_ge(rope_ready, g + 1)
                    rope(g, "mla", "qp", g)
                    split_ahead(("mla", "q", g))
                if g:
                    outputs_low("mla", heads)
            for g in range(MXG):
                split_ahead(("mla", "down", g))
            ln_then_transpose("ln2", "mla")
            feed_forward("ff1", FFG)

            dve.wait_ge(mod_read, NMOD)
            for dst, scale, gain in ((A0, "scale0", "norm_g0"), (A1, "scale1", "norm_g1"), (AK, "kv_scale", "kv_g")):
                last = stt(out=dst, in0=mrange(scale), scalar=1.0, in1=colrange(gain), op0=ALU.add, op1=ALU.mult)
            link(last)
            for b in range(TB):
                layer_norm("ln3", "ff1", b)
                dve.wait_ge(S["norm_ready"], nth("norm_ready", "ln3", b))
                rms_norm("rs1", b)
                split_transposed("rs1", b, lambda kt: A0[:, kt:kt + 1], lambda kt: mcol("shift0", kt))

            uT = flat(buf_a)[:, 0:GT * (SEQ + 3)].rearrange("p (t s) -> p t s", t=GT)
            nc.vector.memset(uT[:, :, 0:3], 0.0).then_inc(conv_ready, 1)
            hs = rows[:, 1, 512:1024]
            for g in range(MXG + 1):
                if g < MXG:
                    uc = kT[:, 2 * (g % 2):2 * (g % 2) + 2, :]
                    sg = kT_f[:, 1024 + (g % 2) * 512:1024 + (g % 2 + 1) * 512]
                    split_ahead(("rg", "u", g))
                    await_evacuated(dve, "rg", "u", g)
                    for t in range(GT):
                        kt = GT * g + t
                        last = ts(uc[:, t, :], uT[:, t, 3:3 + SEQ], col("rg_w", 3 * KT + kt), col("rg_cb", kt), ALU.mult, ALU.add)
                    link(last)
                    for k in (2, 1, 0):
                        for t in range(GT):
                            last = stt(out=uc[:, t, :], in0=uT[:, t, k:k + SEQ], scalar=col("rg_w", k * KT + GT * g + t),
                                       in1=uc[:, t, :], op0=ALU.mult, op1=ALU.add)
                        if k:
                            link(last)
                    last.then_inc(conv_ready, 1)
                    dve.wait_ge(conv_ready, g + 2)
                    dve.wait_ge(uc_high, g + 1)
                    tt(hT_l[:, 4:6, :], uc, f32(hT_h[:, 4:6, :]), ALU.subtract).then_inc(uc_low, 1)
                    split_ahead(("rg", "g", g))
                    dve.wait_ge(gate_tanh, g + 1)
                    stt(out=sg, in0=thg_of(rows), scalar=1.0, in1=bank_of("rg", "g", g)[:, :], op0=ALU.add, op1=ALU.mult)\
                        .then_inc(evacuates("rg", "g", g), 1)
                if g:
                    i = g - 1
                    uc = kT_f[:, (i % 2) * 512:(i % 2 + 1) * 512]
                    sg = kT_f[:, 1024 + (i % 2) * 512:1024 + (i % 2 + 1) * 512]
                    th_x, th_l, ratio = area_f[:, 512:1024], area_f[:, 1024:1536], stage[:, 1, :]
                    split_ahead(("rg", "ax", i))
                    dve.wait_ge(decay_ready, i + 1)
                    dve.wait_ge(square_ready, i + 1)
                    stt(out=ratio, in0=area_f[:, 1536:2048], scalar=1.0, in1=th_l, op0=ALU.add, op1=ALU.mult).then_inc(ratio_ready, 1)
                    await_evacuated(dve, "rg", "x", i)
                    link(stt(out=th_x, in0=th_x, scalar=1.0, in1=uc, op0=ALU.add, op1=ALU.mult))
                    dve.wait_ge(root_ready, i + 1)
                    link(tt(th_x, th_x, th_l, ALU.mult))
                    for t in range(GT):
                        last = nc.vector.tensor_tensor_scan(hs[:, t * SEQ:(t + 1) * SEQ], stage[:, 0, t * SEQ:(t + 1) * SEQ],
                                                            th_x[:, t * SEQ:(t + 1) * SEQ], 0.0, ALU.mult, ALU.add)
                    link(last)
                    stt(out=buf_b[:, i % 2, :], in0=hs, scalar=0.5, in1=sg, op0=ALU.mult, op1=ALU.mult).then_inc(rg_hidden, 1)
                    hidden_low_of("rg", i)
            for g in range(MXG):
                split_ahead(("rg", "down", g))
            for b in range(TB):
                gated_residual("rg", 0, b)
                rms_norm("rs2", b)
                split_transposed("rs2kv", b, lambda kt: AK[:, kt:kt + 1], lambda kt: mcol("kv_shift", kt))

            for kind in "kv":
                for g in range(MXG):
                    split_ahead(("mo", kind, g))
            for b in range(TB):
                split_transposed("rs2", b, lambda kt: A1[:, kt:kt + 1], lambda kt: mcol("shift1", kt))
            for g in range(MXG + 1):
                heads = (GT * g - 2, GT * g - 1)
                if g:
                    softmax("mo", heads)
                if g < MXG:
                    split_ahead(("mo", "q", g))
                    split_ahead(("mo", "g", g))
                    dve.wait_ge(gate_tanh, MXG + g + 1)
                    t0 = 2 * GT + GT * (g % 2)
                    stt(out=q_all[:, t0:t0 + GT, :], in0=stage[:, :, SEQ:], scalar=1.0,
                        in1=bank_of("mo", "g", g)[:, :].rearrange("p (t s) -> p t s", t=2),
                        op0=ALU.add, op1=ALU.mult).then_inc(evacuates("mo", "g", g), 1)
                if g:
                    outputs_low("mo", heads)
            split_ahead(("mo", "down", 0))
            for b in range(TB):
                gated_residual("mo", 1, b)
                rms_norm("rs3", b)
                dve.wait_ge(S["norm_ready"], nth("norm_ready", "rs3", b))
                dve.wait_ge(shift_in, 16 * 5)
                tt(z[:, b, :], z[:, b, :], rows[:, 1, :], ALU.mult).then_inc(out_ready, 1)
            assert done[0] == len(STREAM)


def thg_of(rows):
    return rows[:, 1, 0:512]


def tiles(w, kts, width=P):
    k, n = w.shape
    return w.reshape(kts, P, n // width, width).transpose(1, 2, 0, 3).reshape(P, -1)


def k_major(w, kts):
    return w.reshape(kts, P, w.shape[1]).transpose(1, 0, 2).reshape(P, -1)


def piece_of(i, phase, kind, g):
    sl = slice(g * GT * P, (g + 1) * GT * P)
    if kind == "down":
        w = {"sc": i["sc_w_out"][0], "ff0": i["ff_w2"][0], "mla": i["mla_w_o"][0], "ff1": i["ff_w2"][1],
             "rg": i["rg_w_out_2"][0], "mo": i["att_w_out_2"][0]}[phase]
        return k_major(w[sl, :], GT)
    if phase == "sc":
        return tiles(i["sc_w_in"][0][:, "BCh".index(kind) * D:][:, sl], KT)
    if kind == "up":
        return tiles(i["ff_w1"][int(phase[2])][:, sl], KT)
    if phase == "mla":
        if kind == "dq":
            return k_major(i["mla_w_dq"][0][g * 4 * P:(g + 1) * 4 * P, :], KT // 2)
        dkv = i["mla_w_dkv"][0]
        if kind == "dkv":
            return k_major(dkv[:, 0:KV_LORA], KT)
        if kind == "kpe":
            a, b = dkv[:, KV_LORA:KV_LORA + ROPE // 2], dkv[:, KV_LORA + ROPE // 2:]
            return tiles(np.concatenate([a, b, a, b, b, a, b, a], axis=1), KT)
        if kind == "uk":
            return tiles(i["mla_w_uk"][0].reshape(KV_LORA, HEADS * P), CT)
        if kind == "uv":
            return k_major(i["mla_w_uv"][0].reshape(KV_LORA, HEADS * P), CT)
        uq = i["mla_w_uq"][0].reshape(Q_LORA, HEADS, NOPE + ROPE)
        heads = (GT * g, GT * g + 1)
        (a, b), (c, d) = [(uq[:, h, NOPE:NOPE + ROPE // 2], uq[:, h, NOPE + ROPE // 2:]) for h in heads]
        return tiles(np.concatenate([uq[:, h, 0:NOPE] for h in heads] + [a, b, c, d, b, a, d, c], axis=1), QT)
    if kind == "ax":
        return np.concatenate([tiles(i["rg_w_a_2"][0][g], GT), tiles(i["rg_w_x_2"][0][g], GT)], axis=1)
    w = {"rg": i["rg_w_in_2"][0], "mo": i["att_w_in_2"][0] if kind in "qg" else i["w_kv_2"]}[phase]
    w = w[:, ("ug" if phase == "rg" else "qg" if kind in "qg" else "kv").index(kind) * D:][:, sl]
    return k_major(w, KT) if kind == "v" else tiles(w, KT)


def pack_weights(i):
    mod = np.concatenate([i["mod_w_2"][0], i["mod_w_2"][1], i["kv_mod_w_2"]], axis=1)
    parts = []
    for kind, n in STREAM:
        if kind == "mod":
            a = k_major(mod[:, n * 2 * P:(n + 1) * 2 * P], KT)
        else:
            a = piece_of(i, *PIECES[n][0])
            assert a.shape == (P, COLS[n]), (PIECES[n], a.shape)
        parts.append(a.reshape(-1))
    return np.concatenate(parts)


def pack_cols(i):
    def c(v):
        return v.reshape(-1, P).T

    of = {"c": c(i["c_2"]), "mod_b": np.concatenate([c(i["mod_b_2"][0]), c(i["mod_b_2"][1]), c(i["kv_mod_b_2"])], axis=1),
          "norm_g0": c(i["norm_g_2"][0]), "norm_g1": c(i["norm_g_2"][1]), "kv_g": c(i["kv_norm_g_2"]),
          "ln0_g": c(i["ln_mix_g"][0]), "ln0_b": c(i["ln_mix_b"][0]), "ln1_g": c(i["ln_ff_g"][0]), "ln1_b": c(i["ln_ff_b"][0]),
          "ln2_g": c(i["ln_mix_g"][1]), "ln2_b": c(i["ln_mix_b"][1]),
          "sc_w": c(i["sc_conv_w"][0]), "rg_w": c(i["rg_conv_w_2"][0]), "rg_cb": c(i["rg_conv_b_2"]),
          "rg_ba": c(i["rg_b_a_2"]), "rg_bx": c(i["rg_b_x_2"]), "lam": c(i["rg_lambda_2"]),
          "g_q": c(i["mla_g_q"]), "g_kv": c(i["mla_g_kv"])}
    return np.ascontiguousarray(np.concatenate([of[name] for name in COL_WIDTHS], axis=1))


def constants():
    r = np.arange(P)
    tri = np.where(r[None, :] > r[:, None], np.float32(NEG_INF), np.float32(0))
    freq = np.float32(10000.0) ** (-np.arange(0, ROPE, 2, dtype=np.float32) / np.float32(ROPE))
    angle = (np.arange(SEQ, dtype=np.float32)[:, None] * freq[None, :]).T
    cos, sin = np.cos(angle)[r % (ROPE // 2)], np.sin(angle)[r % (ROPE // 2)]
    sin = np.where((r % ROPE < ROPE // 2)[:, None], -sin, sin)
    return np.concatenate([np.eye(P), tri, cos, sin], axis=1).astype(np.float32)


def kernel(**inputs):
    import concourse.bacc as bacc
    from concourse.bass_utils import run_bass_kernel_spmd

    i = {name: np.asarray(a) for name, a in inputs.items()}
    rows = np.stack([i["ln_mix_g"][0], i["ln_mix_b"][0], i["ln_ff_g"][0], i["ln_ff_b"][0],
                     i["ln_mix_g"][1], i["ln_mix_b"][1], i["ln_ff_g"][1], i["ln_ff_b"][1], i["final_norm_g_2"]])
    arrays = {"weights": pack_weights(i), "x_in": np.ascontiguousarray(i["x"][0]), "cols_in": pack_cols(i),
              "consts_in": constants(), "rows_in": rows}
    nc = bacc.Bacc("TRN2", target_bir_lowering=False, num_devices=1)
    args = [nc.dram_tensor(name, a.shape, F32, kind="ExternalInput").ap() for name, a in arrays.items()]
    out = nc.dram_tensor("out", (SEQ, D), F32, kind="ExternalOutput").ap()
    build(nc, *args, out)
    r = run_bass_kernel_spmd(nc, [arrays], core_ids=[0])
    return r.results[0]["out"].reshape(1, SEQ, D)
```

```python
from contextlib import ExitStack

import concourse.bass as bass
import numpy as np
from concourse import mybir

F32 = mybir.dt.float32
F32R = mybir.dt.float32r
ALU = mybir.AluOpType
ACT = mybir.ActivationFunctionType
AXX = mybir.AxisListType.X

P = 128
SEQ, D, D_FF = 256, 1024, 4096
TB = SEQ // P
KT = D // P
HEADS = 8
NOPE, ROPE = 128, 64
Q_LORA, KV_LORA = 384, 256
QT, CT = Q_LORA // P, KV_LORA // P
RG_C = 8.0
ALPHA = 4.0 ** 0.25
LN_EPS, RMS_EPS = 1e-5, 1e-6
NEG_INF = -1e30
GT = 2
FFG = D_FF // (GT * P)
MXG = D // (GT * P)
SCMODS = 2
NMOD = 2 * FFG

PIECE = 2048
RAW = 3
RING = 6
AHEAD = 4
RG_AHEAD = 5
PBANKS = 3
HRING = 3


GROUPS = {"sc": MXG, "ff0": FFG, "mla": MXG, "ff1": FFG, "rg": MXG, "mo": MXG}
TAIL = {"sc": 3, "ff0": 3, "mla": MXG, "ff1": 3, "rg": 1, "mo": MXG}


def piece_table():
    t = []

    def add(phase, kind, n, cols=PIECE):
        t.append(((phase, kind, n), cols))

    for g in range(MXG):
        for kind in "ChB":
            add("sc", kind, g)
        if 0 < g <= MXG - TAIL["sc"]:
            add("sc", "down", g - 1)
    for g in range(MXG - TAIL["sc"], MXG):
        add("sc", "down", g)

    def ff(phase):
        for g in range(FFG):
            add(phase, "up", g)
            if 0 < g <= FFG - TAIL[phase]:
                add(phase, "down", g - 1)
        for g in range(FFG - TAIL[phase], FFG):
            add(phase, "down", g)

    ff("ff0")
    add("mla", "dkv", 0)
    for n in range(2):
        add("mla", "dq", n, KT // 2 * Q_LORA)
    add("mla", "kpe", 0)
    add("mla", "uk", 0)
    add("mla", "uv", 0)
    for g in range(MXG):
        add("mla", "q", g, 2 * GT * QT * P)
    for g in range(MXG):
        add("mla", "down", g)
    ff("ff1")
    for g in range(MXG + 1):
        if g < MXG:
            add("rg", "u", g)
        if g:
            add("rg", "ax", g - 1, 2 * GT * 2 * P)
            add("rg", "g", g - 1)
        if g == MXG - 1:
            add("rg", "down", 0)
    for g in range(1, MXG):
        add("rg", "down", g)
    for kind in ("v", "k", "qg"):
        for g in range(MXG):
            for k in kind:
                add("mo", k, g)
    for g in range(MXG):
        add("mo", "down", g)
    return t


PIECES = piece_table()
COLS = [c for _, c in PIECES]
PI = {key: n for n, (key, _) in enumerate(PIECES)}


def carries_mod(phase, kind, g):
    if phase == "sc":
        return kind == "B" and g in (1, 2)
    return phase in ("ff0", "ff1") and (kind == "up" and g >= 2 or kind == "down" and g == FFG - 1)


def stream_table():
    t, m = [], 0
    for n, (key, _) in enumerate(PIECES):
        t.append(("w", n))
        if carries_mod(*key):
            t.append(("mod", m))
            m += 1
    return t


STREAM = stream_table()
AT = {item: n for n, item in enumerate(STREAM)}
WIDTH = [COLS[n] if kind == "w" else PIECE for kind, n in STREAM]


def unit_table():
    t = []

    def norm(name):
        t.extend((name, b, q) for b in range(TB) for q in range(2))

    def attention(phase, projections):
        for g in range(MXG + 1):
            if g < MXG:
                t.extend((phase, kind, g) for kind in projections)
            if phase == "mo" and g == MXG:
                t.extend([("gate", 1, 0), ("gate", 1, 1)])
            if g:
                t.extend((phase, kind, h) for kind in ("PT", "O") for h in (GT * g - 2, GT * g - 1))

    norm("init")
    for g in range(MXG):
        t.extend(("sc", kind, g) for kind in "ChB")
    norm("ln0")
    t.extend(("ff0", g) for g in range(FFG))
    norm("ln1")
    t.append(("mla", "kpe"))
    t.append(("mla", "tkv"))
    t.extend(("mla", "k", n) for n in range(4))
    t.extend([("mla", "tq", 0), ("mla", "tq", 1)])
    t.extend(("mla", "v", b, n) for b in range(TB) for n in range(2))
    attention("mla", ("qn", "qp"))
    norm("ln2")
    t.extend(("ff1", g) for g in range(FFG))
    norm("rs1")
    for g in range(MXG + 1):
        if g < MXG:
            t.append(("rg", "u", g))
        if g == 0:
            t.extend([("gate", 0, 0), ("gate", 0, 1)])
        else:
            t.extend(("rg", kind, g - 1) for kind in "axg")
    t.extend([("rs2kv", 0, 0), ("rs2kv", 0, 1), ("mo", "v", 0, 0), ("rs2kv", 1, 0), ("rs2kv", 1, 1)])
    t.extend(("mo", "v", b, n) for b, n in ((0, 1), (1, 0), (1, 1)))
    t.extend(("mo", "k", g) for g in range(MXG))
    norm("rs2")
    attention("mo", "qg")
    return t


UNITS = unit_table()
UN = {key: n for n, key in enumerate(UNITS)}

def down_table():
    t = []
    for phase, groups in GROUPS.items():
        t.extend((phase, g, b) for g in range(groups - TAIL[phase]) for b in range(TB))
        t.extend((phase, g, b) for b in range(TB) for g in range(groups - TAIL[phase], groups))
    return t


DN = {key: n for n, key in enumerate(down_table())}


def last_unit(phase, kind, n):
    if kind == "up":
        return (phase, n)
    if phase == "mla" and kind == "q":
        return ("mla", "qp", n)
    return {"kpe": ("mla", "kpe"), "uk": ("mla", "k", 3), "uv": ("mla", "v", 1, 1),
            "ax": ("rg", "x", n), "v": ("mo", "v", TB - 1, n // 2)}.get(kind, (phase, kind, n))


LAYER_NORMS = {"ln0": TB, "ln1": TB, "latent": 2, "ln2": TB, "ln3": TB}
SQUARES = {"rs1": TB, "rs2": TB, "rs3": TB}
ROOTS = {"ln0": TB, "ln1": TB, "latent": 2, "ln2": TB, "ln3": 2 * TB, "rs2": TB, "rs3": TB}
HIDDEN = {"sc": MXG, "ff0": FFG, "ff1": FFG, "rg": MXG}
SIGNALS = {
    "relu": {"ff0": FFG, "ff1": FFG},
    "hidden_high": HIDDEN,
    "hidden_low": HIDDEN,
    "y_read": {p: TB for p in GROUPS},
    "var_ready": LAYER_NORMS,
    "squares": SQUARES,
    "rstd_ready": ROOTS,
    "x_ready": {"ln0": TB, "ln1": TB, "ln2": TB, "ln3": TB, "rg": TB, "mo": TB},
    "z_ready": {"rs1": TB, "rs2": TB},
    "xT_high": {p: 4 for p in ("init", "ln0", "ln1", "ln2", "rs1", "rs2kv", "rs2")},
    "xT_low": {p: 4 for p in ("rs1", "rs2kv", "rs2")},
    "scores": {"mla": TB * HEADS, "mo": TB * HEADS},
    "row_max": {"mla": TB * HEADS, "mo": TB * HEADS},
    "exps": {"mla": TB * HEADS, "mo": TB * HEADS},
    "probs": {"mla": TB * HEADS, "mo": TB * HEADS},
    "o_high": {"mla": HEADS, "mo": HEADS},
    "o_low": {"mla": HEADS, "mo": HEADS},
}


def nth(signal, phase, i=0):
    count = 0
    if SIGNALS[signal].get("ln3") == 2 * TB:
        phase, i = {"ln3": ("ln3", 2 * i), "rs1": ("ln3", 2 * i + 1)}.get(phase, (phase, i))
    for p, n in SIGNALS[signal].items():
        if p == phase:
            return count + i + 1
        count += n
    raise KeyError((signal, phase))


COL_WIDTHS = {"c": KT, "mod_b": 2 * NMOD, "norm_g0": KT, "norm_g1": KT, "kv_g": KT,
              "ln0_g": KT, "ln0_b": KT, "ln1_g": KT, "ln1_b": KT, "ln2_g": KT, "ln2_b": KT,
              "sc_w": 3 * KT, "rg_w": 4 * KT, "rg_cb": KT, "rg_ba": KT, "rg_bx": KT, "lam": KT,
              "g_q": QT, "g_kv": CT}
COL = {}
for _n, _w in COL_WIDTHS.items():
    COL[_n] = sum(COL_WIDTHS[k] for k in COL)
NCOL = sum(COL_WIDTHS.values())
MOD = {name: KT * n for n, name in enumerate(["shift0", "scale0", "gate0", "shift1", "scale1", "gate1",
                                              "kv_shift", "kv_scale"])}


def build(nc, weights, x_in, cols_in, consts_in, rows_in, out):
    with ExitStack() as ctx:
        def sb(name, shape, dt=F32):
            return ctx.enter_context(nc.sbuf_tensor(name, shape, dt))

        raw = sb("raw", [P, RAW, PIECE])
        w_high = sb("w_high", [P, RING, PIECE], F32R)
        w_low = sb("w_low", [P, RING, PIECE], F32R)
        x = sb("x", [P, TB, D])
        z = sb("z", [P, TB, D])
        xT_h = sb("xT_h", [P, KT, SEQ], F32R)
        xT_l = sb("xT_l", [P, KT, SEQ], F32R)
        stage = sb("stage", [P, 2, 512])
        rows = sb("rows", [P, 2, D])
        consts = sb("consts", [P, 2 * P + 2 * SEQ])
        ones = sb("ones", [P, P])
        cols = sb("cols", [P, NCOL])
        modcol = sb("modcol", [P, 2 * NMOD])
        macc = sb("macc", [P, 2, SEQ])
        buf_a = sb("buf_a", [P, 2, 512])
        buf_b = sb("buf_b", [P, 2, 512])
        hT_h = sb("hT_h", [P, HRING * GT, SEQ], F32R)
        hT_l = sb("hT_l", [P, HRING * GT, SEQ], F32R)
        kT = sb("kT", [P, KT, SEQ])
        area = sb("area", [P, KT, SEQ])
        small = sb("small", [P, 85])

        ident, tri = consts[:, 0:P], consts[:, P:2 * P]
        cosT, sinT = consts[:, 2 * P:2 * P + SEQ], consts[:, 2 * P + SEQ:]
        flat = lambda t: t[:, :, :].rearrange("p a b -> p (a b)")
        kT_f, area_f = flat(kT), flat(area)
        stats = small[:, 0:48].rearrange("p (b n) -> p b n", b=2 * TB)
        mv = small[:, 48:56].rearrange("p (b n) -> p b n", b=2 * TB)
        ve = small[:, 56:60]
        rstd = small[:, 60:64]
        minus_half = small[:, 79:81]
        msq = small[:, 81:85]
        ssum = small[:, 77:79]
        nmx, rsum, rinv = (small[:, 65 + 4 * n:69 + 4 * n] for n in range(3))
        cs = sb("cs", [P, KT])
        cth = sb("cth", [P, KT])
        prm = sb("prm", [P, 12, KT])
        A0, A1, AK, HBA, HBX, C4 = (prm[:, n, :] for n in range(6))

        def col(name, n=0):
            return cols[:, COL[name] + n:COL[name] + n + 1]

        def colrange(name, n=KT, start=0):
            return cols[:, COL[name] + start:COL[name] + start + n]

        def mcol(name, n):
            return modcol[:, MOD[name] + n:MOD[name] + n + 1]

        def mrange(name):
            return modcol[:, MOD[name]:MOD[name] + KT]

        Y = [[ctx.enter_context(nc.psum_tensor(f"Y{b}{h}", [P, 512], F32)) for h in range(2)] for b in range(TB)]
        bank = [ctx.enter_context(nc.psum_tensor(f"bank{n}", [P, 512], F32)) for n in range(PBANKS)]
        mbank = ctx.enter_context(nc.psum_tensor("mbank", [P, 512], F32))

        modulation = {"rs1": (lambda kt: A0[:, kt:kt + 1], lambda kt: mcol("shift0", kt)),
                      "rs2kv": (lambda kt: AK[:, kt:kt + 1], lambda kt: mcol("kv_shift", kt)),
                      "rs2": (lambda kt: A1[:, kt:kt + 1], lambda kt: mcol("shift1", kt))}

        def mod_acc(m):
            return macc if m % 2 == 0 else stage[:, 1, :].rearrange("p (k s) -> p k s", k=2)

        def tok(b):
            return slice(b * P, (b + 1) * P)

        def sem(name):
            return ctx.enter_context(nc.semaphore(name))

        raw_in = [sem(f"raw_in{n}") for n in range(RAW)]
        half_high, half_low = sem("half_high"), sem("half_low")
        w_high_ready = sem("w_high_ready")
        raw_done = sem("raw_done")
        product = sem("product")
        summed = sem("summed")
        evacuated = [sem(f"evacuated{n}") for n in range(PBANKS)]
        latent = sem("latent")
        mod_added, mod_summed, mod_read = sem("mod_added"), sem("mod_summed"), sem("mod_read")
        S = {name: sem(name) for name in SIGNALS}
        relu, hidden_high, hidden_low = S["relu"], S["hidden_high"], S["hidden_low"]
        x_in_done = [sem(f"x_in_done{b}") for b in range(TB)]
        ident_in_done, consts_in_done, cols_in_done = sem("ident_in_done"), sem("consts_in_done"), sem("cols_in_done")
        gain_in, shift_in = sem("gain_in"), sem("shift_in")
        ones_ready, c_tanh, lam_exp_in, lam_exp = sem("ones_ready"), sem("c_tanh"), sem("lam_exp_in"), sem("lam_exp")
        prm_ready, diag_ready = sem("prm_ready"), sem("diag_ready")
        lora_ready, lora_high, lora_low, rope_ready = sem("lora_ready"), sem("lora_high"), sem("lora_low"), sem("rope_ready")
        conv_ready, uc_high, uc_low = sem("conv_ready"), sem("uc_high"), sem("uc_low")
        gate_tanh, decay_ready, ratio_ready, root_ready = sem("gate_tanh"), sem("decay_ready"), sem("ratio_ready"), sem("root_ready")
        square_ready, rg_hidden = sem("square_ready"), sem("rg_hidden")
        gated_ready, scan_ready = sem("gated_ready"), sem("scan_ready")
        dve_chain, pool_chain = sem("dve_chain"), sem("pool_chain")
        out_ready, out_done = sem("out_ready"), sem("out_done")

        def bank_of(*key):
            return bank[UN[key] % PBANKS]

        def await_product(eng, *key):
            eng.wait_ge(product, UN[key] + 1)

        def await_evacuated(eng, *key):
            eng.wait_ge(evacuated[UN[key] % PBANKS], UN[key] // PBANKS + 1)

        def evacuates(*key):
            return evacuated[UN[key] % PBANKS]

        def await_piece_used(eng, n):
            phase, kind, i = PIECES[n][0]
            if kind == "down":
                eng.wait_ge(summed, DN[phase, i, TB - 1] + 1)
            elif kind in ("dq", "dkv"):
                eng.wait_ge(latent, TB if kind == "dkv" else 2 * TB)
            else:
                eng.wait_ge(product, UN[last_unit(phase, kind, i)] + 1)

        def hslot(phase, g):
            if phase == "rg":
                return GT * (g % 2) if g < MXG - 1 else 2 * GT
            return GT * (g % HRING)

        def head_tiles(phase, h):
            if phase == "mo" and h < GT * HRING:
                return hT_h, hT_l, h
            return xT_h, xT_l, h % (GT * HRING) if phase == "mo" else h

        area_v = area_f.rearrange("p (b n) -> p b n", b=TB)
        q_all = flat(rows).rearrange("p (h s) -> p h s", s=SEQ)

        def q_tile(phase, h):
            return q_all[:, h if phase == "mla" else h % (2 * GT), :]

        def o_gate(h):
            return q_all[:, 2 * GT + h % (2 * GT), :]

        block = ctx.enter_context(nc.Block())

        @block.sync
        def _(sp):
            def load_row(slot, which, semaphore):
                sp.dma_start(rows[:, slot, :], rows_in[which, :].partition_broadcast(P)).then_inc(semaphore, 16)

            sp.dma_start(ident, consts_in[:, 0:P]).then_inc(ident_in_done, 16)
            for b in range(TB):
                sp.dma_start(x[:, b, :], x_in[b * P:(b + 1) * P, :]).then_inc(x_in_done[b], 16)
            start = 0
            for s, (kind, n) in enumerate(STREAM):
                if s >= RAW:
                    sp.wait_ge(raw_done, s - RAW + 1)
                src = weights[start:start + P * WIDTH[s]].rearrange("(p n) -> p n", p=P)
                sp.dma_start(raw[:, s % RAW, 0:WIDTH[s]], src).then_inc(raw_in[s % RAW], 16)
                start += P * WIDTH[s]
                if s == 0:
                    sp.dma_start(cols[:, :], cols_in).then_inc(cols_in_done, 16)
                if s == RAW:
                    sp.dma_start(consts[:, P:], consts_in[:, P:]).then_inc(consts_in_done, 16)
                key = PIECES[n][0] if kind == "w" else None
                which = {("sc", "down", 0): 0, ("ff0", "up", 8): 1, ("ff1", "up", 0): 2, ("ff1", "up", 8): 3}.get(key)
                if which is not None:
                    if which in (1, 3):
                        sp.wait_ge(S["x_ready"], nth("x_ready", f"ln{which - 1}", TB - 1))
                    if which == 2:
                        sp.wait_ge(S["scores"], nth("scores", "mla", TB * HEADS - 1))
                    load_row(0, 2 * which, gain_in)
                    load_row(1, 2 * which + 1, shift_in)
            await_evacuated(sp, "mo", "O", HEADS - 1)
            load_row(1, 8, shift_in)
            for b in range(TB):
                sp.wait_ge(out_ready, b + 1)
                sp.dma_start(out[b * P:(b + 1) * P, :], x[:, b, :]).then_inc(out_done, 16)
            sp.wait_ge(out_done, 16 * TB)

        @block.tensor
        def _(pe):
            mm = nc.tensor.matmul
            issued = [0, 0]

            def open_unit(*key):
                u = UN[key]
                assert u == issued[0], (key, UNITS[issued[0]])
                issued[0] += 1
                if u >= PBANKS:
                    pe.wait_ge(evacuated[u % PBANKS], u // PBANKS)
                return bank[u % PBANKS]

            def await_piece(n):
                pe.wait_ge(raw_done, AT["w", n] + 1)

            def await_xT(phase, b, q):
                if phase[:2] == "rs":
                    pe.wait_ge(S["xT_low"], nth("xT_low", phase, 2 * b + q))
                else:
                    await_evacuated(pe, phase, b, q)

            def up_tile(dst, n, tile, kts, xh, xl, fresh=None):
                for kt in range(kts):
                    if fresh and kt % 4 == 0:
                        for b in range(TB):
                            await_xT(fresh, b, kt // 4)
                    c = (tile * kts + kt) * P
                    high, low = w_high[:, n % RING, c:c + P], w_low[:, n % RING, c:c + P]
                    mm(dst, high, xh[:, kt, :], start=kt == 0, stop=False)
                    mm(dst, high, xl[:, kt, :], start=False, stop=False)
                    last = mm(dst, low, xh[:, kt, :], start=False, stop=kt == kts - 1)
                return last

            def up(n, key, tile0=0, kts=KT, xh=xT_h, xl=xT_l, fresh=None):
                dst = open_unit(*key)
                if n:
                    await_piece(n)
                else:
                    pe.wait_ge(half_low, 1)
                up_tile(dst[:, 0:SEQ], n, tile0, kts, xh, xl, fresh)
                if n == 0:
                    await_piece(n)
                up_tile(dst[:, SEQ:], n, tile0 + 1, kts, xh, xl).then_inc(product, 1)

            def token_major(dst, n, kts, width, c0, stride, b, xh, xl, first, final, fresh=None):
                for kt in range(kts):
                    if fresh and kt % 4 == 0:
                        await_xT(fresh, b, kt // 4)
                    c = kt * stride + c0
                    high, low = w_high[:, n % RING, c:c + width], w_low[:, n % RING, c:c + width]
                    mm(dst, xh[:, kt, tok(b)], high, start=first and kt == 0, stop=False)
                    mm(dst, xh[:, kt, tok(b)], low, start=False, stop=False)
                    last = mm(dst, xl[:, kt, tok(b)], high, start=False, stop=final and kt == kts - 1)
                return last

            def across(n, key, kts, width, c0=0, stride=None, xh=xT_h, xl=xT_l, blocks=range(TB)):
                dst = open_unit(*key)
                await_piece(n)
                for i, b in enumerate(blocks):
                    last = token_major(dst[:, i * width:(i + 1) * width], n, kts, width, c0, stride or width, b, xh, xl, True, True)
                last.then_inc(product, 1)

            def down(phase, g, b, th=hT_h, tl=hT_l):
                assert DN[phase, g, b] == issued[1]
                issued[1] += 1
                n = PI[phase, "down", g]
                if th is hT_h:
                    t0 = hslot(phase, g)
                    pe.wait_ge(hidden_low, nth("hidden_low", phase, g))
                else:
                    pe.wait_ge(S["o_low"], nth("o_low", phase, GT * g + GT - 1))
                    th, tl, t0 = head_tiles(phase, GT * g)
                if g == 0:
                    phases = list(GROUPS)
                    if phase != phases[0]:
                        pe.wait_ge(S["y_read"], nth("y_read", phases[phases.index(phase) - 1], b))
                await_piece(n)
                for t in range(GT):
                    first, final = g == 0 and t == 0, g == GROUPS[phase] - 1 and t == GT - 1
                    high = [w_high[:, n % RING, t * D + h * 512:t * D + (h + 1) * 512] for h in range(2)]
                    low = [w_low[:, n % RING, t * D + h * 512:t * D + (h + 1) * 512] for h in range(2)]
                    for h in range(2):
                        mm(Y[b][h][:, :], th[:, t0 + t, tok(b)], high[h], start=first, stop=False)
                        mm(Y[b][h][:, :], th[:, t0 + t, tok(b)], low[h], start=False, stop=False)
                    for h in range(2):
                        last = mm(Y[b][h][:, :], tl[:, t0 + t, tok(b)], high[h], start=False, stop=final)
                last.then_inc(summed, 1)

            def tail(phase, th=hT_h, tl=hT_l, early=None, m=None):
                for b in range(TB):
                    for g in range(GROUPS[phase] - TAIL[phase], GROUPS[phase]):
                        if early and b and g == GROUPS[phase] - 1:
                            early()
                        down(phase, g, b, th, tl)
                    if m is not None and b == 0:
                        mod_sums(m)

            def transposes(name, src, signal=None, blocks=range(TB)):
                for b in blocks:
                    if signal:
                        pe.wait_ge(S[signal], nth(signal, name, b))
                    for q in range(2):
                        dst = open_unit(name, b, q)
                        for i in range(4):
                            kt = 4 * q + i
                            last = nc.tensor.transpose(dst[:, i * P:(i + 1) * P], src[:, b, kt * P:(kt + 1) * P], ident)
                        last.then_inc(product, 1)

            def mod_sums(m):
                pe.wait_ge(mod_added, m + 1)
                if m:
                    pe.wait_ge(mod_read, m)
                for i in range(2):
                    last = mm(mbank[:, i:i + 1], mod_acc(m)[:, 0, i * P:(i + 1) * P], ones[:, 0:1], start=True, stop=True)
                last.then_inc(mod_summed, 1)

            def feed_forward(phase, m0, fresh, early=None):
                for g in range(FFG):
                    if g >= 2:
                        mod_sums(m0 + g - 2)
                    up(PI[phase, "up", g], (phase, g), fresh=None if g else fresh)
                    if 0 < g <= FFG - TAIL[phase]:
                        for b in range(TB):
                            down(phase, g - 1, b)
                tail(phase, m=m0 + FFG - 2, early=early)

            def gate_rows(layer):
                for n in range(2):
                    dst = open_unit("gate", layer, n)
                    pe.wait_ge(diag_ready, 2 * layer + n + 1)
                    diag = area_f if layer == 0 else z[:, 0, :]
                    mm(dst[:, :], ones[:, :], diag[:, n * 512:(n + 1) * 512], start=True, stop=True).then_inc(product, 1)

            def scores(phase, h):
                q = q_tile(phase, h)
                for b in range(TB):
                    keys = (b + 1) * P
                    dst, mla = Y[b][h % 2], phase == "mla"
                    last = mm(dst[:, 0:keys], q[:, tok(b)], kT[:, h, 0:keys], start=True, stop=not mla)
                    if mla:
                        r = slice(ROPE * (h % 2), ROPE * (h % 2 + 1))
                        last = mm(dst[:, 0:keys], area[r, h // 2, tok(b)], area[r, 4, 0:keys], start=False, stop=True)
                    last.then_inc(S["scores"], 1)

            def values(phase, heads):
                v = z if phase == "mla" else area_v
                for h in heads:
                    dst = open_unit(phase, "PT", h)
                    pe.wait_ge(S["probs"], nth("probs", phase, TB * h + 1))
                    p = buf_a[:, h % 2, :]
                    for i, (b, kb) in enumerate([(0, 0), (1, 0), (1, 1)]):
                        last = nc.tensor.transpose(dst[:, i * P:(i + 1) * P],
                                                   p[:, b * SEQ + kb * P:b * SEQ + (kb + 1) * P], ident)
                    last.then_inc(product, 1)
                for h in heads:
                    dst = open_unit(phase, "O", h)
                    await_evacuated(pe, phase, "PT", h)
                    pT = buf_b[:, h % 2, :]
                    mm(dst[:, 0:SEQ], v[:, 0, h * P:(h + 1) * P], pT[:, 0:SEQ], start=True, stop=False)
                    mm(dst[:, P:SEQ], v[:, 1, h * P:(h + 1) * P], pT[:, SEQ:SEQ + P], start=False, stop=True).then_inc(product, 1)

            def attention(phase, project, await_q, last=lambda: None):
                for g in range(MXG + 1):
                    if g:
                        await_q(g - 1)
                        for h in (GT * g - 2, GT * g - 1):
                            scores(phase, h)
                    if g < MXG:
                        project(g)
                    else:
                        last()
                    if g:
                        values(phase, (GT * g - 2, GT * g - 1))

            pe.wait_ge(ident_in_done, 16)
            for b in range(TB):
                pe.wait_ge(x_in_done[b], 16)
                transposes("init", x, blocks=[b])
            for g in range(MXG):
                if g == MXG - 1:
                    pe.wait_ge(ones_ready, 1)
                    mod_sums(0)
                for kind in "ChB":
                    up(PI["sc", kind, g], ("sc", kind, g), fresh="init" if (kind, g) == ("C", 0) else None)
                if 0 < g <= MXG - TAIL["sc"]:
                    for b in range(TB):
                        down("sc", g - 1, b)
            tail("sc", early=lambda: transposes("ln0", x, "x_ready", [0]), m=SCMODS - 1)
            transposes("ln0", x, "x_ready", [1])
            feed_forward("ff0", SCMODS, "ln0", lambda: transposes("ln1", x, "x_ready", [0]))

            for b in range(TB):
                if b:
                    transposes("ln1", x, "x_ready", [b])
                pe.wait_ge(S["y_read"], nth("y_read", "ff0", b))
                i = PI["mla", "dkv", 0]
                await_piece(i)
                token_major(Y[b][1][:, 0:KV_LORA], i, KT, KV_LORA, 0, KV_LORA, b, xT_h, xT_l, True, True, "ln1").then_inc(latent, 1)
            for b in range(TB):
                for n in range(2):
                    i = PI["mla", "dq", n]
                    await_piece(i)
                    last = token_major(Y[b][0][:, 0:Q_LORA], i, KT // 2, Q_LORA, 0, Q_LORA, b, xT_h[:, 4 * n:4 * n + 4, :],
                                       xT_l[:, 4 * n:4 * n + 4, :], n == 0, n == 1)
                last.then_inc(latent, 1)
            up(PI["mla", "kpe", 0], ("mla", "kpe"))
            cqn = flat(buf_a)[:, 0:TB * Q_LORA].rearrange("p (b n) -> p b n", b=TB)
            ckvn = buf_b[:, 0, :].rearrange("p (b n) -> p b n", b=TB)
            dst = open_unit("mla", "tkv")
            pe.wait_ge(lora_ready, 1)
            for kt in range(CT):
                for b in range(TB):
                    last = nc.tensor.transpose(dst[:, (kt * TB + b) * P:(kt * TB + b + 1) * P],
                                               ckvn[:, b, kt * P:(kt + 1) * P], ident)
            last.then_inc(product, 1)
            pe.wait_ge(lora_low, 1)
            ckv = (hT_h[:, QT:QT + CT, :], hT_l[:, QT:QT + CT, :])
            for n in range(4):
                up(PI["mla", "uk", 0], ("mla", "k", n), 2 * n, CT, *ckv)
            for b in range(TB):
                dst = open_unit("mla", "tq", b)
                pe.wait_ge(lora_ready, 2)
                for kt in range(QT):
                    last = nc.tensor.transpose(dst[:, kt * P:(kt + 1) * P], cqn[:, b, kt * P:(kt + 1) * P], ident)
                last.then_inc(product, 1)
            for b in range(TB):
                for n in range(2):
                    across(PI["mla", "uv", 0], ("mla", "v", b, n), CT, 512, n * 512, D, *ckv, blocks=[b])

            pe.wait_ge(lora_low, 3)

            def project(g):
                for i, kind in enumerate(("qn", "qp")):
                    up(PI["mla", "q", g], ("mla", kind, g), GT * i, QT, hT_h, hT_l)

            def await_q(g):
                await_evacuated(pe, "mla", "qn", g)
                pe.wait_ge(rope_ready, g + 2)
                if g == 0:
                    for b, n in ((0, 1), (1, 0), (1, 1)):
                        await_evacuated(pe, "mla", "v", b, n)

            attention("mla", project, await_q)
            tail("mla", xT_h, xT_l, lambda: transposes("ln2", x, "x_ready", [0]))
            transposes("ln2", x, "x_ready", [1])
            feed_forward("ff1", SCMODS + FFG - 1, "ln2")

            transposes("rs1", z, "z_ready")
            for g in range(MXG + 1):
                if g < MXG:
                    up(PI["rg", "u", g], ("rg", "u", g), fresh=None if g else "rs1")
                if g == 0:
                    gate_rows(0)
                else:
                    pe.wait_ge(uc_low, g)
                    for i, kind in enumerate("ax"):
                        up(PI["rg", "ax", g - 1], ("rg", kind, g - 1), GT * i, GT, hT_h[:, 4:6, :], hT_l[:, 4:6, :])
                    up(PI["rg", "g", g - 1], ("rg", "g", g - 1))
                for n in {MXG - 1: (0,), MXG: range(1, MXG - 1)}.get(g, ()):
                    for b in range(TB):
                        down("rg", n, b)

            def rs2kv_transposes(b):
                pe.wait_ge(S["z_ready"], nth("z_ready", "rs2", b))
                transposes("rs2kv", z, blocks=[b])

            def moba_values(b, n):
                dst = open_unit("mo", "v", b, n)
                for i in range(2):
                    await_piece(PI["mo", "v", 2 * n + i])
                    last = token_major(dst[:, i * SEQ:(i + 1) * SEQ], PI["mo", "v", 2 * n + i], KT, 2 * P, 0, 2 * P, b,
                                       xT_h, xT_l, True, True, "rs2kv" if n == i == 0 else None)
                last.then_inc(product, 1)

            tail("rg")
            rs2kv_transposes(0)
            moba_values(0, 0)
            rs2kv_transposes(1)
            moba_values(0, 1)
            for n in range(2):
                moba_values(1, n)
            for g in range(MXG):
                up(PI["mo", "k", g], ("mo", "k", g))
            transposes("rs2", z)

            def project_moba(g):
                for kind in "qg":
                    up(PI["mo", kind, g], ("mo", kind, g), fresh="rs2" if (kind, g) == ("q", 0) else None)

            def await_q_moba(g):
                await_evacuated(pe, "mo", "q", g)
                if g == 0:
                    for b, n in ((0, 1), (1, 0), (1, 1)):
                        await_evacuated(pe, "mo", "v", b, n)

            attention("mo", project_moba, await_q_moba, lambda: gate_rows(1))
            tail("mo", xT_h, xT_l)
            assert issued == [len(UNITS), len(DN)]

        @block.gpsimd
        def _(pool):
            chain = [0]

            def link(instruction):
                chain[0] += 1
                instruction.then_inc(pool_chain, 1)
                pool.wait_ge(pool_chain, chain[0])

            nc.gpsimd.memset(ones[:, :], 1.0).then_inc(ones_ready, 1)
            link(nc.gpsimd.memset(minus_half, -0.5))

            def roots(*names, blocks=TB):
                for b, name in [(b, name) for b in range(blocks) for name in names]:
                    if name in SQUARES:
                        pool.wait_ge(S["squares"], nth("squares", name, b))
                        root(slice(b, b + 1), ssum[:, b:b + 1], RMS_EPS, 1.0 / D)
                    else:
                        pool.wait_ge(S["var_ready"], nth("var_ready", name, b))
                        root(slice(b, b + 1), mv[:, b, 1:2], LN_EPS)

            def root(n, src, epsilon, scale=1.0):
                link(nc.gpsimd.tensor_scalar(ve[:, n], src, scale, epsilon, ALU.mult, ALU.add))
                nc.gpsimd.tensor_tensor(rstd[:, n], ve[:, n], minus_half[:, 0:n.stop - n.start], ALU.pow)\
                    .then_inc(S["rstd_ready"], 1)

            def add_accumulators(pieces):
                for m in pieces:
                    pool.wait_ge(raw_done, AT["mod", m] + 1)
                    acc = mod_acc(m)
                    nc.gpsimd.tensor_tensor(acc[:, 0, :], acc[:, 0, :], acc[:, 1, :], ALU.add).then_inc(mod_added, 1)

            def diagonals(layer):
                dst = area_f if layer == 0 else z[:, 0, :]
                for n in range(2):
                    for i in range(4):
                        t = 4 * n + i
                        last = nc.gpsimd.tensor_scalar(dst[:, t * P:(t + 1) * P], ident, mcol(f"gate{layer}", t), None, ALU.mult)
                    last.then_inc(diag_ready, 1)

            pool.wait_ge(ident_in_done, 16)
            add_accumulators(range(SCMODS))
            roots("ln0")
            add_accumulators(range(SCMODS, SCMODS + FFG - 1))
            roots("ln1")
            for n in range(2):
                pool.wait_ge(S["var_ready"], nth("var_ready", "latent", n))
                root(slice(TB * n, TB * (n + 1)), msq[:, TB * n:TB * (n + 1)], RMS_EPS)
            roots("ln2")
            add_accumulators(range(SCMODS + FFG - 1, NMOD))
            roots("ln3", "rs1")
            pool.wait_ge(mod_read, NMOD)
            diagonals(0)
            roots("rs2")
            for b in range(TB):
                for q in range(2):
                    await_product(pool, "rs2", b, q)
            diagonals(1)
            roots("rs3")

        @block.scalar
        def _(act):
            done = [0]

            def split_ahead(key, ahead=AHEAD):
                while done[0] < len(PIECES) and done[0] <= PI[key] + ahead:
                    n = done[0]
                    s = AT["w", n]
                    act.wait_ge(raw_in[s % RAW], 16 * (s // RAW + 1))
                    if n >= RING:
                        await_piece_used(act, n - RING)
                    start = 0
                    if n == 0:
                        start = PIECE // 2
                        nc.scalar.copy(w_high[:, 0, 0:start], raw[:, 0, 0:start]).then_inc(half_high, 1)
                    nc.scalar.copy(w_high[:, n % RING, start:COLS[n]], raw[:, s % RAW, start:COLS[n]]).then_inc(w_high_ready, 1)
                    done[0] += 1

            def hidden_high_of(phase, g):
                back = 2 if phase == "rg" else HRING
                if (phase, g) == ("rg", MXG - 1):
                    await_product(act, "rg", "x", g)
                elif g >= back:
                    act.wait_ge(summed, DN[phase, g - back, TB - 1] + 1)
                t0 = hslot(phase, g)
                src = buf_b[:, g % 2, :].rearrange("p (t s) -> p t s", t=GT)
                nc.scalar.copy(hT_h[:, t0:t0 + GT, :], src).then_inc(hidden_high, 1)

            def norm_transposed(name, blocks=range(TB)):
                for b in blocks:
                    for q in range(2):
                        await_product(act, name, b, q)
                        src = bank_of(name, b, q)[:, :].rearrange("p (t s) -> p t s", t=4)
                        nc.scalar.copy(xT_h[:, 4 * q:4 * q + 4, tok(b)], src).then_inc(S["xT_high"], 1)

            def rms_norm(name, source, b):
                act.wait_ge(S["x_ready"], nth("x_ready", source, b))
                squared = rows[:, 0, :] if (name, b) == ("rs3", 0) else z[:, b, :]
                nc.scalar.activation(squared, x[:, b, :], ACT.Square, accum_out=ssum[:, b:b + 1]).then_inc(S["squares"], 1)
                if name != "rs3":
                    act.wait_ge(S["rstd_ready"], nth("rstd_ready", name, b))
                    nc.scalar.mul(z[:, b, :], x[:, b, :], rstd[:, b:b + 1]).then_inc(S["z_ready"], 1)

            def scaled_transposed(name, b, gain, shift, between=lambda: None):
                await_product(act, name, b, 0)
                before = nth("xT_low", name, 2 * b) - 2
                if before > 0:
                    act.wait_ge(S["xT_low"], before)
                for i in range(4):
                    last = nc.scalar.activation(stage[:, 0, i * P:(i + 1) * P], bank_of(name, b, 0)[:, i * P:(i + 1) * P],
                                                ACT.Identity, scale=gain(i), bias=shift(i))
                last.then_inc(evacuates(name, b, 0), 1)
                for q in range(2):
                    await_evacuated(act, name, b, q)
                    nc.scalar.copy(xT_h[:, 4 * q:4 * q + 4, tok(b)], stage[:, q, :].rearrange("p (t s) -> p t s", t=4))\
                        .then_inc(S["xT_high"], 1)
                    if q == 0:
                        between()

            def feed_forward(phase):
                for g in range(FFG):
                    split_ahead((phase, "up", g), AHEAD if g else AHEAD - 1)
                    await_product(act, phase, g)
                    if g >= 2:
                        await_evacuated(act, phase, g - 2)
                    nc.scalar.activation(buf_a[:, g % 2, :], bank_of(phase, g)[:, :], ACT.Relu).then_inc(relu, 1)
                    await_evacuated(act, phase, g)
                    hidden_high_of(phase, g)

            def exponentials(phase, h):
                for b in range(TB):
                    keys, c = (b + 1) * P, TB * (h % 2) + b
                    act.wait_ge(S["row_max"], nth("row_max", phase, TB * h + b))
                    if h >= 2:
                        await_product(act, phase, "PT", h - 2)
                    nc.scalar.activation(buf_a[:, h % 2, b * SEQ:b * SEQ + keys], Y[b][h % 2][:, 0:keys], ACT.Exp,
                                         bias=nmx[:, c:c + 1], accum_out=rsum[:, c:c + 1]).then_inc(S["exps"], 1)

            def outputs_high(phase, heads):
                for h in heads:
                    await_product(act, phase, "PT", h)
                    if h >= 2:
                        await_product(act, phase, "O", h - 2)
                    nc.scalar.copy(buf_b[:, h % 2, 0:3 * P], bank_of(phase, "PT", h)[:, 0:3 * P])\
                        .then_inc(evacuates(phase, "PT", h), 1)
                for h in heads:
                    await_evacuated(act, phase, "O", h)
                    th, _, t = head_tiles(phase, h)
                    nc.scalar.copy(th[:, t, :], stage[:, h % 2, 0:SEQ]).then_inc(S["o_high"], 1)

            for b in range(TB):
                for q in range(2):
                    await_product(act, "init", b, q)
                    src = bank_of("init", b, q)[:, :].rearrange("p (t s) -> p t s", t=4)
                    nc.scalar.copy(xT_h[:, 4 * q:4 * q + 4, tok(b)], src).then_inc(S["xT_high"], 1)
            split_ahead(("sc", "C", 0), 0)
            act.wait_ge(cols_in_done, 16)
            nc.scalar.activation(cth[:, :], colrange("c"), ACT.Tanh, scale=0.5).then_inc(c_tanh, 1)
            act.wait_ge(lam_exp_in, 1)
            nc.scalar.activation(prm[:, 7, :], prm[:, 6, :], ACT.Exp, scale=-1.0).then_inc(lam_exp, 1)
            for g in range(MXG):
                split_ahead(("sc", "C", g))
                await_product(act, "sc", "C", g)
                if g >= 2:
                    await_evacuated(act, "sc", "h", g - 2)
                nc.scalar.copy(kT_f[:, (g % 2) * 512:(g % 2 + 1) * 512], bank_of("sc", "C", g)[:, :])\
                    .then_inc(evacuates("sc", "C", g), 1)
                split_ahead(("sc", "h", g))
                split_ahead(("sc", "B", g))
                await_evacuated(act, "sc", "B", g)
                hidden_high_of("sc", g)
            split_ahead(("sc", "down", MXG - 1), 3)
            norm_transposed("ln0")
            feed_forward("ff0")
            split_ahead(("ff0", "down", FFG - 1), 2)
            norm_transposed("ln1")

            split_ahead(("mla", "dq", 1))
            await_evacuated(act, "mla", "tkv")
            nc.scalar.copy(hT_h[:, QT:QT + CT, :], stage[:, 0, :].rearrange("p (t s) -> p t s", t=CT)).then_inc(lora_high, 1)
            split_ahead(("mla", "kpe", 0))
            for n in range(4):
                await_product(act, "mla", "k", n)
                nc.scalar.copy(kT[:, 2 * n:2 * n + 2, :], bank_of("mla", "k", n)[:, :].rearrange("p (t s) -> p t s", t=2))\
                    .then_inc(evacuates("mla", "k", n), 1)
            split_ahead(("mla", "uk", 0))
            for b in range(TB):
                await_evacuated(act, "mla", "tq", b)
                src = stage[:, b, 0:QT * P].rearrange("p (t s) -> p t s", t=QT)
                nc.scalar.copy(hT_h[:, 0:QT, tok(b)], src).then_inc(lora_high, 1)
            for b in range(TB):
                for n in range(2):
                    await_product(act, "mla", "v", b, n)
                    nc.scalar.copy(z[:, b, n * 512:(n + 1) * 512], bank_of("mla", "v", b, n)[:, :])\
                        .then_inc(evacuates("mla", "v", b, n), 1)
            split_ahead(("mla", "uv", 0))
            for g in range(MXG + 1):
                heads = (GT * g - 2, GT * g - 1)
                if g:
                    for h in heads:
                        exponentials("mla", h)
                if g < MXG:
                    await_product(act, "mla", "qn", g)
                    nc.scalar.mul(q_all[:, GT * g:GT * (g + 1), :], bank_of("mla", "qn", g)[:, :].rearrange("p (t s) -> p t s", t=2),
                                  float(NOPE + ROPE) ** -0.5).then_inc(evacuates("mla", "qn", g), 1)
                    split_ahead(("mla", "q", g))
                if g:
                    outputs_high("mla", heads)
            split_ahead(("mla", "down", MXG - 1), 2)
            norm_transposed("ln2")
            feed_forward("ff1")
            split_ahead(("ff1", "down", FFG - 1), 2)
            rms_norm("rs1", "ln3", 0)
            act.wait_ge(prm_ready, 1)
            for b in range(TB):
                scaled_transposed("rs1", b, *modulation["rs1"], *[lambda: rms_norm("rs1", "ln3", 1)] * (b == 0))
            uT = flat(buf_a)[:, 0:GT * (SEQ + 3)].rearrange("p (t s) -> p t s", t=GT)
            thg = rows[:, 1, 0:512]
            split_ahead(("rg", "u", 0), 2)
            for g in range(MXG + 1):
                i = g - 1
                if g < MXG:
                    await_product(act, "rg", "u", g)
                    act.wait_ge(conv_ready, g + 1)
                    nc.scalar.copy(uT[:, :, 3:], bank_of("rg", "u", g)[:, :].rearrange("p (t s) -> p t s", t=GT))\
                        .then_inc(evacuates("rg", "u", g), 1)
                    split_ahead(("rg", "u", g), RG_AHEAD)
                    act.wait_ge(conv_ready, g + 2)
                    if g:
                        await_product(act, "rg", "x", g - 1)
                    nc.scalar.copy(hT_h[:, 4:6, :], kT[:, 2 * (g % 2):2 * (g % 2) + 2, :]).then_inc(uc_high, 1)
                if g == 0:
                    act.wait_ge(S["x_ready"], nth("x_ready", "ln3", TB - 1))
                    for n in range(2):
                        await_product(act, "gate", 0, n)
                        nc.scalar.copy(rows[:, 0, n * 512:(n + 1) * 512], bank_of("gate", 0, n)[:, :]).then_inc(evacuates("gate", 0, n), 1)
                else:
                    if g == MXG:
                        split_ahead(("rg", "ax", i))
                    if i:
                        act.wait_ge(rg_hidden, i)

                    def gate_tanhs(n, kind, half_bias):
                        await_product(act, "rg", kind, i)
                        for t in range(GT):
                            kt = GT * i + t
                            last = nc.scalar.activation(area_f[:, n * 512 + t * SEQ:n * 512 + (t + 1) * SEQ],
                                                        bank_of("rg", kind, i)[:, t * SEQ:(t + 1) * SEQ], ACT.Tanh,
                                                        scale=0.5, bias=half_bias[:, kt:kt + 1])
                        last.then_inc(evacuates("rg", kind, i), 1)

                    gate_tanhs(0, "a", HBA)
                    await_evacuated(act, "rg", "a", i)
                    for t in range(GT):
                        kt = GT * i + t
                        c4, src = C4[:, kt:kt + 1], area_f[:, t * SEQ:(t + 1) * SEQ]
                        nc.scalar.activation(stage[:, 0, t * SEQ:(t + 1) * SEQ], src, ACT.Exp, scale=c4, bias=c4)
                        last = nc.scalar.activation(area_f[:, 1024 + t * SEQ:1024 + (t + 1) * SEQ], src, ACT.Tanh, scale=c4, bias=c4)
                    last.then_inc(decay_ready, 1)
                    act.wait_ge(decay_ready, i + 1)
                    nc.scalar.activation(area_f[:, 1536:2048], stage[:, 0, :], ACT.Square).then_inc(square_ready, 1)
                    gate_tanhs(1, "x", HBX)
                    act.wait_ge(ratio_ready, i + 1)
                    nc.scalar.activation(area_f[:, 1024:1536], stage[:, 1, :], ACT.Sqrt, scale=-0.25).then_inc(root_ready, 1)
                    await_product(act, "rg", "g", i)
                    if i:
                        await_evacuated(act, "rg", "g", i - 1)
                    nc.scalar.activation(thg, bank_of("rg", "g", i)[:, :], ACT.Tanh, scale=0.5).then_inc(gate_tanh, 1)
                    act.wait_ge(rg_hidden, i + 1)
                    hidden_high_of("rg", i)
                    split_ahead(("rg", "g", i), RG_AHEAD)
            split_ahead(("rg", "down", MXG - 1), 3)

            rms_norm("rs2", "rg", 0)
            split_ahead(("rg", "down", MXG - 1), 4)
            for b in range(TB):
                scaled_transposed("rs2kv", b, *modulation["rs2kv"])
                if b == 0:
                    rms_norm("rs2", "rg", 1)
            for b in range(TB):
                for n in range(2):
                    if b:
                        split_ahead(("mo", "v", 2 * n + 1))
                    await_product(act, "mo", "v", b, n)
                    nc.scalar.copy(area_v[:, b, n * 512:(n + 1) * 512], bank_of("mo", "v", b, n)[:, :])\
                        .then_inc(evacuates("mo", "v", b, n), 1)
            for g in range(MXG):
                split_ahead(("mo", "k", g))
                await_product(act, "mo", "k", g)
                nc.scalar.copy(kT[:, 2 * g:2 * g + 2, :], bank_of("mo", "k", g)[:, :].rearrange("p (t s) -> p t s", t=2))\
                    .then_inc(evacuates("mo", "k", g), 1)
            for b in range(TB):
                scaled_transposed("rs2", b, *modulation["rs2"])
            for g in range(MXG + 1):
                heads = (GT * g - 2, GT * g - 1)
                if g:
                    for h in heads:
                        exponentials("mo", h)
                if g < MXG:
                    split_ahead(("mo", "q", g))
                    await_product(act, "mo", "q", g)
                    if g == 0:
                        act.wait_ge(S["y_read"], nth("y_read", "rg", TB - 1))
                    t0 = GT * (g % 2)
                    nc.scalar.mul(q_all[:, t0:t0 + GT, :], bank_of("mo", "q", g)[:, :].rearrange("p (t s) -> p t s", t=2),
                                  float(P) ** -0.5).then_inc(evacuates("mo", "q", g), 1)
                    split_ahead(("mo", "g", g))
                    await_product(act, "mo", "g", g)
                    if g:
                        await_evacuated(act, "mo", "g", g - 1)
                    nc.scalar.activation(stage[:, :, SEQ:], bank_of("mo", "g", g)[:, :].rearrange("p (t s) -> p t s", t=2),
                                         ACT.Tanh, scale=0.5).then_inc(gate_tanh, 1)
                else:
                    for n in range(2):
                        await_product(act, "gate", 1, n)
                        nc.scalar.copy(z[:, 1, n * 512:(n + 1) * 512], bank_of("gate", 1, n)[:, :]).then_inc(evacuates("gate", 1, n), 1)
                if g:
                    outputs_high("mo", heads)
            split_ahead(("mo", "down", 0))
            for b in range(TB):
                rms_norm("rs3", "mo", b)
            assert done[0] == len(PIECES)

        @block.vector
        def _(dve):
            chain = [0]
            done = [0]
            tt, ts, stt = nc.vector.tensor_tensor, nc.vector.tensor_scalar, nc.vector.scalar_tensor_tensor

            def link(instruction):
                chain[0] += 1
                instruction.then_inc(dve_chain, 1)
                dve.wait_ge(dve_chain, chain[0])

            def f32(ap):
                return ap.bitcast(F32)

            def split_ahead(key, ahead=AHEAD):
                stop = AT["w", min(PI[key] + ahead, len(PIECES) - 1)]
                while done[0] <= stop:
                    s = done[0]
                    kind, n = STREAM[s]
                    slot = raw[:, s % RAW, :]
                    if kind == "w":
                        start = 0
                        if n == 0:
                            start = PIECE // 2
                            dve.wait_ge(half_high, 1)
                            tt(w_low[:, 0, 0:start], slot[:, 0:start], f32(w_high[:, 0, 0:start]), ALU.subtract).then_inc(half_low, 1)
                        dve.wait_ge(w_high_ready, n + 1)
                        tt(w_low[:, n % RING, start:COLS[n]], slot[:, start:COLS[n]], f32(w_high[:, n % RING, start:COLS[n]]),
                           ALU.subtract).then_inc(raw_done, 1)
                    else:
                        dve.wait_ge(raw_in[s % RAW], 16 * (s // RAW + 1))
                        if n >= 2:
                            dve.wait_ge(mod_summed, n - 1)
                        accumulators = mod_acc(n)
                        first = chain[0]
                        for kt in range(KT):
                            acc, part = accumulators[:, kt % 2, :], slot[:, kt * SEQ:(kt + 1) * SEQ]
                            if kt < 2:
                                step = ts(acc, part, cs[:, kt:kt + 1], None, ALU.mult)
                            else:
                                dve.wait_ge(dve_chain, first + kt - 1)
                                step = stt(out=acc, in0=part, scalar=cs[:, kt:kt + 1], in1=acc, op0=ALU.mult, op1=ALU.add)
                            if kt < KT - 1:
                                step.then_inc(dve_chain, 1)
                                chain[0] += 1
                        step.then_inc(raw_done, 1)
                    done[0] += 1

            def read_mod(m):
                dve.wait_ge(mod_summed, m + 1)
                tt(modcol[:, 2 * m:2 * m + 2], mbank[:, 0:2], colrange("mod_b", 2, 2 * m), ALU.add).then_inc(mod_read, 1)

            def hidden_low_of(phase, g):
                dve.wait_ge(hidden_high, nth("hidden_high", phase, g))
                t0 = hslot(phase, g)
                src = buf_b[:, g % 2, :].rearrange("p (t s) -> p t s", t=GT)
                tt(hT_l[:, t0:t0 + GT, :], src, f32(hT_h[:, t0:t0 + GT, :]), ALU.subtract).then_inc(hidden_low, 1)

            def variance(parts, b):
                for i, part in enumerate(parts):
                    last = nc.vector.bn_stats(stats[:, b, 6 * i:6 * i + 6], part)
                link(last)
                return nc.vector.bn_aggr(mv[:, b, :], stats[:, b, 0:6 * len(parts)])

            def halves(t, b):
                return [t[:, b, 0:512], t[:, b, 512:1024]]

            def await_rstd(name, b):
                dve.wait_ge(S["rstd_ready"], nth("rstd_ready", name, b))

            def layer_norm_sums(name, phase, b):
                dve.wait_ge(summed, DN[phase, GROUPS[phase] - 1, b] + 1)
                for h in range(2):
                    last = stt(out=z[:, b, h * 512:(h + 1) * 512], in0=x[:, b, h * 512:(h + 1) * 512], scalar=ALPHA,
                               in1=Y[b][h][:, :], op0=ALU.mult, op1=ALU.add)
                last.then_inc(S["y_read"], 1)
                dve.wait_ge(S["y_read"], nth("y_read", phase, b))
                variance(halves(z, b), b).then_inc(S["var_ready"], 1)
                dve.wait_ge(S["var_ready"], nth("var_ready", name, b))

            def layer_norm_apply(name, b):
                n = int(name[2])
                dve.wait_ge(gain_in, 16 * (n + 1))
                link(stt(out=z[:, b, :], in0=z[:, b, :], scalar=mv[:, b, 0:1], in1=rows[:, 0, :], op0=ALU.subtract, op1=ALU.mult))
                dve.wait_ge(shift_in, 16 * (n + 1))
                await_rstd(name, b)
                stt(out=x[:, b, :], in0=z[:, b, :], scalar=rstd[:, b:b + 1], in1=rows[:, 1, :], op0=ALU.mult, op1=ALU.add)\
                    .then_inc(S["x_ready"], 1)

            def gated_residual(phase, layer, b):
                if b == 0:
                    for n in range(2):
                        await_evacuated(dve, "gate", layer, n)
                dve.wait_ge(summed, DN[phase, GROUPS[phase] - 1, b] + 1)
                gate, product_of = (rows[:, 0, :], z[:, b, :]) if layer == 0 else (z[:, 1, :], z[:, 0, :])
                for h in range(2):
                    last = tt(product_of[:, h * 512:(h + 1) * 512], Y[b][h][:, :], gate[:, h * 512:(h + 1) * 512], ALU.mult)
                last.then_inc(S["y_read"], 1)
                dve.wait_ge(S["y_read"], nth("y_read", phase, b))
                tt(x[:, b, :], x[:, b, :], product_of, ALU.add).then_inc(S["x_ready"], 1)
                dve.wait_ge(S["x_ready"], nth("x_ready", phase, b))

            def split_transposed(name, b, gain, shift):
                await_product(dve, name, b, 1)
                for i in range(4):
                    last = ts(stage[:, 1, i * P:(i + 1) * P], bank_of(name, b, 1)[:, i * P:(i + 1) * P], gain(4 + i), shift(4 + i),
                              ALU.mult, ALU.add)
                last.then_inc(evacuates(name, b, 1), 1)
                for q in range(2):
                    dve.wait_ge(S["xT_high"], nth("xT_high", name, 2 * b + q))
                    tt(xT_l[:, 4 * q:4 * q + 4, tok(b)], stage[:, q, :].rearrange("p (t s) -> p t s", t=4),
                       f32(xT_h[:, 4 * q:4 * q + 4, tok(b)]), ALU.subtract).then_inc(S["xT_low"], 1)
                dve.wait_ge(S["xT_low"], nth("xT_low", name, 2 * b + 1))

            def low_transposed(name, b):
                for q in range(2):
                    dve.wait_ge(S["xT_high"], nth("xT_high", name, 2 * b + q))
                    tt(xT_l[:, 4 * q:4 * q + 4, tok(b)], bank_of(name, b, q)[:, :].rearrange("p (t s) -> p t s", t=4),
                       f32(xT_h[:, 4 * q:4 * q + 4, tok(b)]), ALU.subtract).then_inc(evacuates(name, b, q), 1)

            def modulation_parameters():
                dve.wait_ge(mod_read, NMOD)
                for dst, scale, gain in ((A0, "scale0", "norm_g0"), (A1, "scale1", "norm_g1"), (AK, "kv_scale", "kv_g")):
                    last = stt(out=dst, in0=mrange(scale), scalar=1.0, in1=colrange(gain), op0=ALU.add, op1=ALU.mult)
                last.then_inc(prm_ready, 1)
                dve.wait_ge(prm_ready, 1)

            def layer_norms(name, phase, ahead, m=None, lows=True):
                last_piece = (phase, "down", GROUPS[phase] - 1)
                split_ahead(last_piece, 0)
                layer_norm_sums(name, phase, 0)
                layer_norm_apply(name, 0)
                if m is not None:
                    read_mod(m)
                if m == NMOD - 1:
                    modulation_parameters()
                split_ahead(last_piece, ahead)
                if lows:
                    low_transposed(name, 0)
                layer_norm_sums(name, phase, 1)
                layer_norm_apply(name, 1)
                if lows:
                    low_transposed(name, 1)

            def feed_forward(phase, m0):
                for g in range(FFG):
                    split_ahead((phase, "up", g), AHEAD if g else AHEAD - 1)
                    if g >= 2:
                        read_mod(m0 + g - 2)
                    dve.wait_ge(relu, nth("relu", phase, g))
                    stt(out=buf_b[:, g % 2, :], in0=bank_of(phase, g)[:, :], scalar=0.0, in1=buf_a[:, g % 2, :],
                        op0=ALU.max, op1=ALU.mult).then_inc(evacuates(phase, g), 1)
                    hidden_low_of(phase, g)

            def softmax(phase, heads):
                for h in heads:
                    for b in range(TB):
                        keys, c = (b + 1) * P, TB * (h % 2) + b
                        dve.wait_ge(S["scores"], nth("scores", phase, TB * h + b))
                        s = Y[b][h % 2]
                        if phase == "mla":
                            link(nc.vector.memset(s[0:64, keys - 64:keys], NEG_INF))
                        else:
                            link(tt(s[:, keys - P:keys], s[:, keys - P:keys], tri, ALU.add))
                        nc.vector.reduce_max(nmx[:, c:c + 1], s[:, 0:keys], AXX, negate=True).then_inc(S["row_max"], 1)
                for h in heads:
                    c = TB * (h % 2)
                    dve.wait_ge(S["exps"], nth("exps", phase, TB * h + TB - 1))
                    link(nc.vector.reciprocal(rinv[:, c:c + TB], rsum[:, c:c + TB]))
                    for b in range(TB):
                        p = buf_a[:, h % 2, b * SEQ:b * SEQ + (b + 1) * P]
                        ts(p, p, rinv[:, c + b:c + b + 1], None, ALU.mult).then_inc(S["probs"], 1)

            def outputs_low(phase, heads):
                for h in heads:
                    await_product(dve, phase, "O", h)
                    o, st = bank_of(phase, "O", h)[:, 0:SEQ], stage[:, h % 2, 0:SEQ]
                    if phase == "mla":
                        nc.vector.tensor_copy(st, o).then_inc(evacuates(phase, "O", h), 1)
                    else:
                        stt(out=st, in0=o, scalar=0.5, in1=o_gate(h), op0=ALU.mult, op1=ALU.mult)\
                            .then_inc(evacuates(phase, "O", h), 1)
                for h in heads:
                    th, tl, t = head_tiles(phase, h)
                    dve.wait_ge(S["o_high"], nth("o_high", phase, h))
                    tt(tl[:, t, :], stage[:, h % 2, 0:SEQ], f32(th[:, t, :]), ALU.subtract).then_inc(S["o_low"], 1)

            for b in range(TB):
                for q in range(2):
                    dve.wait_ge(S["xT_high"], nth("xT_high", "init", 2 * b + q))
                    tt(xT_l[:, 4 * q:4 * q + 4, tok(b)], bank_of("init", b, q)[:, :].rearrange("p (t s) -> p t s", t=4),
                       f32(xT_h[:, 4 * q:4 * q + 4, tok(b)]), ALU.subtract).then_inc(evacuates("init", b, q), 1)

            split_ahead(("sc", "C", 0), 0)
            dve.wait_ge(cols_in_done, 16)
            lam, r2, s, d, poly, s2 = colrange("lam"), prm[:, 8, :], prm[:, 9, :], prm[:, 10, :], prm[:, 11, :], prm[:, 5, :]
            link(ts(r2, lam, -1.0, 0.0, ALU.mult, ALU.max))
            link(ts(prm[:, 7, :], lam, 0.0, None, ALU.max))
            tt(prm[:, 6, :], prm[:, 7, :], r2, ALU.add).then_inc(lam_exp_in, 1)
            ts(HBA, colrange("rg_ba"), 0.5, None, ALU.mult)
            link(ts(HBX, colrange("rg_bx"), 0.5, None, ALU.mult))
            dve.wait_ge(c_tanh, 1)
            link(stt(out=cs[:, :], in0=cth[:, :], scalar=1.0, in1=colrange("c"), op0=ALU.add, op1=ALU.mult))
            link(ts(cs[:, :], cs[:, :], 0.5, None, ALU.mult))
            dve.wait_ge(lam_exp, 1)
            e = prm[:, 7, :]
            link(ts(d, e, 2.0, None, ALU.add))
            link(nc.vector.reciprocal(d, d))
            link(tt(s, e, d, ALU.mult))
            link(tt(s2, s, s, ALU.mult))
            link(ts(poly, s2, 1.0 / 15, None, ALU.mult))
            for odd in (13, 11, 9, 7, 5, 3):
                link(stt(out=poly, in0=poly, scalar=1.0 / odd, in1=s2, op0=ALU.add, op1=ALU.mult))
            link(stt(out=poly, in0=poly, scalar=1.0, in1=s, op0=ALU.add, op1=ALU.mult))
            link(ts(r2, r2, -2.0 * RG_C / 4, None, ALU.mult))
            link(stt(out=C4, in0=poly, scalar=-RG_C, in1=r2, op0=ALU.mult, op1=ALU.add))

            ch = area_f[:, 0:GT * (SEQ + 2)].rearrange("p (t s) -> p t s", t=GT)
            conv = area_f[:, 1024:1536].rearrange("p (t s) -> p t s", t=GT)
            link(nc.vector.memset(ch[:, :, 0:2], 0.0))
            for g in range(MXG):
                split_ahead(("sc", "C", g))
                await_evacuated(dve, "sc", "C", g)
                await_product(dve, "sc", "h", g)
                tt(ch[:, :, 2:], bank_of("sc", "h", g)[:, :].rearrange("p (t s) -> p t s", t=GT),
                   kT_f[:, (g % 2) * 512:(g % 2 + 1) * 512].rearrange("p (t s) -> p t s", t=GT), ALU.mult)\
                    .then_inc(evacuates("sc", "h", g), 1)
                split_ahead(("sc", "h", g))
                await_evacuated(dve, "sc", "h", g)
                for t in range(GT):
                    last = ts(conv[:, t, :], ch[:, t, 2:2 + SEQ], col("sc_w", 2 * KT + GT * g + t), None, ALU.mult)
                link(last)
                for k in (1, 0):
                    for t in range(GT):
                        last = stt(out=conv[:, t, :], in0=ch[:, t, k:k + SEQ], scalar=col("sc_w", k * KT + GT * g + t),
                                   in1=conv[:, t, :], op0=ALU.mult, op1=ALU.add)
                    link(last)
                split_ahead(("sc", "B", g))
                if g == MXG - 1:
                    read_mod(0)
                await_product(dve, "sc", "B", g)
                tt(buf_b[:, g % 2, :], bank_of("sc", "B", g)[:, :], area_f[:, 1024:1536], ALU.mult).then_inc(evacuates("sc", "B", g), 1)
                hidden_low_of("sc", g)
            layer_norms("ln0", "sc", 2, SCMODS - 1)
            feed_forward("ff0", SCMODS)
            layer_norms("ln1", "ff0", 2, SCMODS + FFG - 2)

            dve.wait_ge(consts_in_done, 16)
            cqn = flat(buf_a)[:, 0:TB * Q_LORA].rearrange("p (b n) -> p b n", b=TB)
            ckvn = buf_b[:, 0, :].rearrange("p (b n) -> p b n", b=TB)
            for i, (normed, half, width) in enumerate(((ckvn, 1, KV_LORA), (cqn, 0, Q_LORA))):
                split_ahead(("mla", "dkv", 0), 2 + 2 * i)
                n = slice(TB * i, TB * (i + 1))
                for b in range(TB):
                    dve.wait_ge(latent, TB * i + b + 1)
                    last = nc.vector.bn_stats(stats[:, TB * i + b, 0:6], Y[b][half][:, 0:width])
                link(last)
                for b in range(TB):
                    last = nc.vector.bn_aggr(mv[:, TB * i + b, :], stats[:, TB * i + b, 0:6])
                link(last)
                link(tt(msq[:, n], mv[:, n, 0], mv[:, n, 0], ALU.mult))
                tt(msq[:, n], msq[:, n], mv[:, n, 1], ALU.add).then_inc(S["var_ready"], 1)
                await_rstd("latent", i)
                for b in range(TB):
                    last = ts(normed[:, b, :], Y[b][half][:, 0:width], rstd[:, TB * i + b:TB * i + b + 1], None, ALU.mult)
                last.then_inc(lora_ready, 1)

            def rope(n, *key):
                await_product(dve, *key)
                src = bank_of(*key)
                scale = float(NOPE + ROPE) ** -0.5 if n < 4 else 1.0
                stt(out=area[:, 5, :], in0=src[:, 0:SEQ], scalar=scale, in1=cosT, op0=ALU.mult, op1=ALU.mult)
                stt(out=area[:, 6, :], in0=src[:, SEQ:], scalar=scale, in1=sinT, op0=ALU.mult, op1=ALU.mult).then_inc(evacuates(*key), 1)
                await_evacuated(dve, *key)
                tt(area[:, n, :], area[:, 5, :], area[:, 6, :], ALU.add).then_inc(rope_ready, 1)

            rope(4, "mla", "kpe")
            await_product(dve, "mla", "tkv")
            for kt in range(CT):
                last = ts(stage[:, 0, kt * SEQ:(kt + 1) * SEQ], bank_of("mla", "tkv")[:, kt * SEQ:(kt + 1) * SEQ], col("g_kv", kt), None, ALU.mult)
            last.then_inc(evacuates("mla", "tkv"), 1)
            dve.wait_ge(lora_high, 1)
            tt(hT_l[:, QT:QT + CT, :], stage[:, 0, :].rearrange("p (t s) -> p t s", t=CT),
               f32(hT_h[:, QT:QT + CT, :]), ALU.subtract).then_inc(lora_low, 1)
            dve.wait_ge(lora_low, 1)
            split_ahead(("mla", "kpe", 0))
            for b in range(TB):
                await_product(dve, "mla", "tq", b)
                for kt in range(QT):
                    last = ts(stage[:, b, kt * P:(kt + 1) * P], bank_of("mla", "tq", b)[:, kt * P:(kt + 1) * P], col("g_q", kt), None, ALU.mult)
                last.then_inc(evacuates("mla", "tq", b), 1)
            for b in range(TB):
                dve.wait_ge(lora_high, b + 2)
                tt(hT_l[:, 0:QT, tok(b)], stage[:, b, 0:QT * P].rearrange("p (t s) -> p t s", t=QT),
                   f32(hT_h[:, 0:QT, tok(b)]), ALU.subtract).then_inc(lora_low, 1)
            for g in range(MXG + 1):
                heads = (GT * g - 2, GT * g - 1)
                if g:
                    softmax("mla", heads)
                if g < MXG:
                    dve.wait_ge(rope_ready, g + 1)
                    rope(g, "mla", "qp", g)
                    split_ahead(("mla", "q", g))
                if g:
                    outputs_low("mla", heads)
            layer_norms("ln2", "mla", 2)
            feed_forward("ff1", SCMODS + FFG - 1)

            layer_norms("ln3", "ff1", 2, NMOD - 1, lows=False)
            for b in range(TB):
                split_transposed("rs1", b, *modulation["rs1"])

            uT = flat(buf_a)[:, 0:GT * (SEQ + 3)].rearrange("p (t s) -> p t s", t=GT)
            nc.vector.memset(uT[:, :, 0:3], 0.0).then_inc(conv_ready, 1)
            split_ahead(("rg", "u", 0), 2)
            hs = rows[:, 1, 512:1024]
            for g in range(MXG + 1):
                if g < MXG:
                    uc = kT[:, 2 * (g % 2):2 * (g % 2) + 2, :]
                    await_evacuated(dve, "rg", "u", g)
                    for t in range(GT):
                        kt = GT * g + t
                        last = ts(uc[:, t, :], uT[:, t, 3:3 + SEQ], col("rg_w", 3 * KT + kt), col("rg_cb", kt), ALU.mult, ALU.add)
                    link(last)
                    for k in (2, 1, 0):
                        for t in range(GT):
                            last = stt(out=uc[:, t, :], in0=uT[:, t, k:k + SEQ], scalar=col("rg_w", k * KT + GT * g + t),
                                       in1=uc[:, t, :], op0=ALU.mult, op1=ALU.add)
                        if k:
                            link(last)
                    last.then_inc(conv_ready, 1)
                    dve.wait_ge(uc_high, g + 1)
                    tt(hT_l[:, 4:6, :], uc, f32(hT_h[:, 4:6, :]), ALU.subtract).then_inc(uc_low, 1)
                    split_ahead(("rg", "u", g), RG_AHEAD)
                if g:
                    i = g - 1
                    uc = kT_f[:, (i % 2) * 512:(i % 2 + 1) * 512]
                    sg = kT_f[:, 1024 + (i % 2) * 512:1024 + (i % 2 + 1) * 512]
                    th_x, th_l, ratio = area_f[:, 512:1024], area_f[:, 1024:1536], stage[:, 1, :]
                    if g == MXG:
                        split_ahead(("rg", "ax", i))
                    dve.wait_ge(decay_ready, i + 1)
                    dve.wait_ge(square_ready, i + 1)
                    stt(out=ratio, in0=area_f[:, 1536:2048], scalar=1.0, in1=th_l, op0=ALU.add, op1=ALU.mult).then_inc(ratio_ready, 1)
                    await_evacuated(dve, "rg", "x", i)
                    stt(out=th_x, in0=th_x, scalar=1.0, in1=uc, op0=ALU.add, op1=ALU.mult).then_inc(gated_ready, 1)
                    dve.wait_ge(gated_ready, i + 1)
                    dve.wait_ge(root_ready, i + 1)
                    link(tt(th_x, th_x, th_l, ALU.mult))
                    for t in range(GT):
                        last = nc.vector.tensor_tensor_scan(hs[:, t * SEQ:(t + 1) * SEQ], stage[:, 0, t * SEQ:(t + 1) * SEQ],
                                                            th_x[:, t * SEQ:(t + 1) * SEQ], 0.0, ALU.mult, ALU.add)
                    last.then_inc(scan_ready, 1)
                    dve.wait_ge(gate_tanh, i + 1)
                    stt(out=sg, in0=rows[:, 1, 0:512], scalar=1.0, in1=bank_of("rg", "g", i)[:, :], op0=ALU.add, op1=ALU.mult)\
                        .then_inc(evacuates("rg", "g", i), 1)
                    await_evacuated(dve, "rg", "g", i)
                    dve.wait_ge(scan_ready, i + 1)
                    stt(out=buf_b[:, i % 2, :], in0=hs, scalar=0.5, in1=sg, op0=ALU.mult, op1=ALU.mult).then_inc(rg_hidden, 1)
                    hidden_low_of("rg", i)
                    split_ahead(("rg", "g", i), RG_AHEAD if g < MXG else AHEAD)
            gated_residual("rg", 0, 0)
            gated_residual("rg", 0, 1)
            split_ahead(("rg", "down", MXG - 1), 2)
            split_transposed("rs2kv", 0, *modulation["rs2kv"])
            split_ahead(("rg", "down", MXG - 1), 4)
            split_transposed("rs2kv", 1, *modulation["rs2kv"])

            for kind in "vk":
                for g in range(MXG):
                    split_ahead(("mo", kind, g))
            for b in range(TB):
                split_transposed("rs2", b, *modulation["rs2"])
            for g in range(MXG + 1):
                heads = (GT * g - 2, GT * g - 1)
                if g:
                    softmax("mo", heads)
                if g < MXG:
                    split_ahead(("mo", "q", g))
                    split_ahead(("mo", "g", g))
                    dve.wait_ge(gate_tanh, MXG + g + 1)
                    t0 = 2 * GT + GT * (g % 2)
                    stt(out=q_all[:, t0:t0 + GT, :], in0=stage[:, :, SEQ:], scalar=1.0,
                        in1=bank_of("mo", "g", g)[:, :].rearrange("p (t s) -> p t s", t=2),
                        op0=ALU.add, op1=ALU.mult).then_inc(evacuates("mo", "g", g), 1)
                if g:
                    outputs_low("mo", heads)
            split_ahead(("mo", "down", 0))
            for b in range(TB):
                gated_residual("mo", 1, b)
                dve.wait_ge(shift_in, 16 * 5)
                await_rstd("rs3", b)
                stt(out=x[:, b, :], in0=x[:, b, :], scalar=rstd[:, b:b + 1], in1=rows[:, 1, :], op0=ALU.mult, op1=ALU.mult)\
                    .then_inc(out_ready, 1)
            assert done[0] == len(STREAM)


def tiles(w, kts, width=P):
    k, n = w.shape
    return w.reshape(kts, P, n // width, width).transpose(1, 2, 0, 3).reshape(P, -1)


def k_major(w, kts):
    return w.reshape(kts, P, w.shape[1]).transpose(1, 0, 2).reshape(P, -1)


def piece_of(i, phase, kind, g):
    sl = slice(g * GT * P, (g + 1) * GT * P)
    if kind == "down":
        w = {"sc": i["sc_w_out"][0], "ff0": i["ff_w2"][0], "mla": i["mla_w_o"][0], "ff1": i["ff_w2"][1],
             "rg": i["rg_w_out_2"][0], "mo": i["att_w_out_2"][0]}[phase]
        return k_major(w[sl, :], GT)
    if phase == "sc":
        return tiles(i["sc_w_in"][0][:, "BCh".index(kind) * D:][:, sl], KT)
    if kind == "up":
        return tiles(i["ff_w1"][int(phase[2])][:, sl], KT)
    if phase == "mla":
        if kind == "dq":
            return k_major(i["mla_w_dq"][0][g * 4 * P:(g + 1) * 4 * P, :], KT // 2)
        dkv = i["mla_w_dkv"][0]
        if kind == "dkv":
            return k_major(dkv[:, 0:KV_LORA], KT)
        if kind == "kpe":
            a, b = dkv[:, KV_LORA:KV_LORA + ROPE // 2], dkv[:, KV_LORA + ROPE // 2:]
            return tiles(np.concatenate([a, b, a, b, b, a, b, a], axis=1), KT)
        if kind == "uk":
            return tiles(i["mla_w_uk"][0].reshape(KV_LORA, HEADS * P), CT)
        if kind == "uv":
            return k_major(i["mla_w_uv"][0].reshape(KV_LORA, HEADS * P), CT)
        uq = i["mla_w_uq"][0].reshape(Q_LORA, HEADS, NOPE + ROPE)
        heads = (GT * g, GT * g + 1)
        (a, b), (c, d) = [(uq[:, h, NOPE:NOPE + ROPE // 2], uq[:, h, NOPE + ROPE // 2:]) for h in heads]
        return tiles(np.concatenate([uq[:, h, 0:NOPE] for h in heads] + [a, b, c, d, b, a, d, c], axis=1), QT)
    if kind == "ax":
        return np.concatenate([tiles(i["rg_w_a_2"][0][g], GT), tiles(i["rg_w_x_2"][0][g], GT)], axis=1)
    w = {"rg": i["rg_w_in_2"][0], "mo": i["att_w_in_2"][0] if kind in "qg" else i["w_kv_2"]}[phase]
    w = w[:, ("ug" if phase == "rg" else "qg" if kind in "qg" else "kv").index(kind) * D:][:, sl]
    return k_major(w, KT) if kind == "v" else tiles(w, KT)


def pack_weights(i):
    mod = np.concatenate([i["mod_w_2"][0], i["mod_w_2"][1], i["kv_mod_w_2"]], axis=1)
    parts = []
    for kind, n in STREAM:
        if kind == "mod":
            a = k_major(mod[:, n * 2 * P:(n + 1) * 2 * P], KT)
        else:
            a = piece_of(i, *PIECES[n][0])
            assert a.shape == (P, COLS[n]), (PIECES[n], a.shape)
        parts.append(a.reshape(-1))
    return np.concatenate(parts)


def pack_cols(i):
    def c(v):
        return v.reshape(-1, P).T

    of = {"c": c(i["c_2"]), "mod_b": np.concatenate([c(i["mod_b_2"][0]), c(i["mod_b_2"][1]), c(i["kv_mod_b_2"])], axis=1),
          "norm_g0": c(i["norm_g_2"][0]), "norm_g1": c(i["norm_g_2"][1]), "kv_g": c(i["kv_norm_g_2"]),
          "ln0_g": c(i["ln_mix_g"][0]), "ln0_b": c(i["ln_mix_b"][0]), "ln1_g": c(i["ln_ff_g"][0]), "ln1_b": c(i["ln_ff_b"][0]),
          "ln2_g": c(i["ln_mix_g"][1]), "ln2_b": c(i["ln_mix_b"][1]),
          "sc_w": c(i["sc_conv_w"][0]), "rg_w": c(i["rg_conv_w_2"][0]), "rg_cb": c(i["rg_conv_b_2"]),
          "rg_ba": c(i["rg_b_a_2"]), "rg_bx": c(i["rg_b_x_2"]), "lam": c(i["rg_lambda_2"]),
          "g_q": c(i["mla_g_q"]), "g_kv": c(i["mla_g_kv"])}
    return np.ascontiguousarray(np.concatenate([of[name] for name in COL_WIDTHS], axis=1))


def constants():
    r = np.arange(P)
    tri = np.where(r[None, :] > r[:, None], np.float32(NEG_INF), np.float32(0))
    freq = np.float32(10000.0) ** (-np.arange(0, ROPE, 2, dtype=np.float32) / np.float32(ROPE))
    angle = (np.arange(SEQ, dtype=np.float32)[:, None] * freq[None, :]).T
    cos, sin = np.cos(angle)[r % (ROPE // 2)], np.sin(angle)[r % (ROPE // 2)]
    sin = np.where((r % ROPE < ROPE // 2)[:, None], -sin, sin)
    return np.concatenate([np.eye(P), tri, cos, sin], axis=1).astype(np.float32)


def kernel(**inputs):
    import concourse.bacc as bacc
    from concourse.bass_utils import run_bass_kernel_spmd

    i = {name: np.asarray(a) for name, a in inputs.items()}
    rows = np.stack([i["ln_mix_g"][0], i["ln_mix_b"][0], i["ln_ff_g"][0], i["ln_ff_b"][0],
                     i["ln_mix_g"][1], i["ln_mix_b"][1], i["ln_ff_g"][1], i["ln_ff_b"][1], i["final_norm_g_2"]])
    arrays = {"weights": pack_weights(i), "x_in": np.ascontiguousarray(i["x"][0]), "cols_in": pack_cols(i),
              "consts_in": constants(), "rows_in": rows}
    nc = bacc.Bacc("TRN2", target_bir_lowering=False, num_devices=1)
    args = [nc.dram_tensor(name, a.shape, F32, kind="ExternalInput").ap() for name, a in arrays.items()]
    out = nc.dram_tensor("out", (SEQ, D), F32, kind="ExternalOutput").ap()
    build(nc, *args, out)
    r = run_bass_kernel_spmd(nc, [arrays], core_ids=[0])
    return r.results[0]["out"].reshape(1, SEQ, D)
```
